# Optimizing a Trainium2 kernel written in Bass

```python
import jax
import jax.numpy as jnp
from jax import lax
import numpy as np

D_MODEL = 1024
BATCH = 1
SEQ = 512
DEPTH = 2

GRID_W = 64
CTX_LEN = 256
HEAD_DIM = 64
FOURIER_GROUPS = 4
FOURIER_GROUP_DIM = 64
FOURIER_WIDTH = FOURIER_GROUPS * FOURIER_GROUP_DIM
RET_HEADS = 4
RET_DK = 64
RET_DV = 64
RET_QK_WIDTH = RET_HEADS * RET_DK
RET_WIDTH = RET_HEADS * RET_DV
RET_CHUNK = 128
ATT_HEADS = 8
ATT_KV_HEADS = 2
ATT_GROUP = ATT_HEADS // ATT_KV_HEADS
ATT_WIDTH = ATT_HEADS * HEAD_DIM
ATT_KV_WIDTH = ATT_KV_HEADS * HEAD_DIM
WINDOW = 128
ATT_BLOCK = 128
KEY_SPAN = ATT_BLOCK + 2 * WINDOW
D_MIX = FOURIER_WIDTH + RET_WIDTH + ATT_WIDTH
D_FF = 2816
N_MOD = 9
ROPE_BASE = 10000.0
ROPE_AXIS_PAIRS = HEAD_DIM // 4
NORM_EPS = 1e-6
NEG_INF = -1e30
IN_SIZES = (FOURIER_WIDTH, RET_QK_WIDTH, RET_QK_WIDTH, RET_WIDTH, RET_WIDTH, ATT_WIDTH, ATT_KV_WIDTH, ATT_KV_WIDTH)
IN_OFFSETS = tuple(int(o) for o in np.cumsum(IN_SIZES)[:-1])
D_IN = int(sum(IN_SIZES))

kernel_name = 'hybrid_fourier_retention_swa_macaron_dit'

def rms_norm(x, w):
    xf = x.astype(jnp.float32)
    y = xf * lax.rsqrt(jnp.mean(xf * xf, axis=-1, keepdims=True) + NORM_EPS) * w.astype(jnp.float32)
    return y.astype(x.dtype)

def modulate(h, shift, scale):
    return h * (1.0 + scale) + shift

def swiglu(h, w_in, w_out):
    gate, up = jnp.split(h @ w_in, 2, axis=-1)
    return (jax.nn.silu(gate) * up) @ w_out

def to_heads(t, n_heads):
    return t.reshape(t.shape[0], t.shape[1], n_heads, t.shape[2] // n_heads)

def axial_rope_angles(length):
    rows = length // GRID_W
    row = jnp.repeat(jnp.arange(rows, dtype=jnp.float32), GRID_W)
    col = jnp.tile(jnp.arange(GRID_W, dtype=jnp.float32), rows)
    inv_freq = ROPE_BASE ** (-jnp.arange(ROPE_AXIS_PAIRS, dtype=jnp.float32) / ROPE_AXIS_PAIRS)
    ang = jnp.stack([row[:, None] * inv_freq, col[:, None] * inv_freq], axis=1)
    return jnp.cos(ang), jnp.sin(ang)

def apply_axial_rope(x, cos, sin):
    b, l, h, d = x.shape
    xr = x.astype(jnp.float32).reshape(b, l, h, 2, 2, ROPE_AXIS_PAIRS)
    x1, x2 = xr[..., 0, :], xr[..., 1, :]
    cs, sn = cos[:, None], sin[:, None]
    out = jnp.stack([x1 * cs - x2 * sn, x2 * cs + x1 * sn], axis=-2)
    return out.reshape(b, l, h, d).astype(x.dtype)

def fourier_mix(u):
    b, l, _ = u.shape
    g = u.astype(jnp.float32).reshape(b, l, FOURIER_GROUPS, FOURIER_GROUP_DIM)
    y = jnp.fft.fft2(g, axes=(1, 3), norm='ortho').real
    return y.reshape(b, l, FOURIER_WIDTH).astype(u.dtype)

def retention_scan(q, k, v, log_gamma, state0):
    b, l, h, _ = q.shape
    dv = v.shape[-1]
    n = l // RET_CHUNK
    cl = RET_CHUNK

    def chunks(t):
        return t.reshape(b, n, cl, h, t.shape[-1]).transpose(1, 0, 3, 2, 4)

    qc, kc, vc = chunks(q), chunks(k), chunks(v)
    pos = jnp.arange(cl, dtype=jnp.float32)
    diff = pos[:, None] - pos[None, :]
    causal = diff >= 0
    intra_decay = jnp.where(causal[None], jnp.exp(jnp.where(causal, diff, 0.0)[None] * log_gamma[:, None, None]), 0.0)
    q_decay = jnp.exp((pos + 1.0)[None] * log_gamma[:, None])
    k_decay = jnp.exp((cl - 1.0 - pos)[None] * log_gamma[:, None])
    chunk_decay = jnp.exp(cl * log_gamma)
    scores = jnp.einsum('nbhik,nbhjk->nbhij', qc, kc) * intra_decay
    intra = jnp.einsum('nbhij,nbhjv->nbhiv', scores, vc)
    kv = jnp.einsum('nbhjk,hj,nbhjv->nbhkv', kc, k_decay, vc)

    def step(state, kv_chunk):
        return state * chunk_decay[None, :, None, None] + kv_chunk, state

    state_final, state_in = lax.scan(step, state0, kv)
    cross = jnp.einsum('nbhik,nbhkv->nbhiv', qc, state_in) * q_decay[None, None, :, :, None]
    out = (intra + cross).transpose(1, 0, 3, 2, 4).reshape(b, l, h, dv)
    return out, state_final

def bidirectional_retention(q_lat, k_lat, v_lat, q_ctx, k_ctx, v_ctx, log_gamma):
    f32 = jnp.float32
    scale = RET_DK ** -0.5
    q_lat, v_lat, q_ctx, v_ctx = q_lat.astype(f32), v_lat.astype(f32), q_ctx.astype(f32), v_ctx.astype(f32)
    k_lat = k_lat.astype(f32) * scale
    k_ctx = k_ctx.astype(f32) * scale
    state0 = jnp.zeros((q_lat.shape[0], RET_HEADS, RET_DK, RET_DV), f32)
    outs_lat = []
    outs_ctx = []
    for direction in range(2):
        if direction == 0:
            rev = lambda t: t
        else:
            rev = lambda t: jnp.flip(t, axis=1)
        o_c, s_c = retention_scan(rev(q_ctx), rev(k_ctx), rev(v_ctx), log_gamma[direction], state0)
        o_l, _ = retention_scan(rev(q_lat), rev(k_lat), rev(v_lat), log_gamma[direction], s_c)
        outs_ctx.append(rev(o_c))
        outs_lat.append(rev(o_l))
    return outs_lat[0] + outs_lat[1], outs_ctx[0] + outs_ctx[1]

def retention_output(o, gate, gn_w):
    b, l = o.shape[0], o.shape[1]
    mu = jnp.mean(o, axis=-1, keepdims=True)
    var = jnp.mean(jnp.square(o - mu), axis=-1, keepdims=True)
    on = ((o - mu) * lax.rsqrt(var + NORM_EPS)).reshape(b, l, RET_WIDTH) * gn_w.astype(jnp.float32)
    return (jax.nn.silu(gate.astype(jnp.float32)) * on).astype(gate.dtype)

def windowed_attention_latent(q, k, v, k_ctx, v_ctx, sink):
    b, s = q.shape[0], q.shape[1]
    nb = s // ATT_BLOCK
    f32 = jnp.float32
    qb = q.astype(f32).reshape(b, nb, ATT_BLOCK, ATT_KV_HEADS, ATT_GROUP, HEAD_DIM) * (HEAD_DIM ** -0.5)
    pad = ((0, 0), (WINDOW, WINDOW), (0, 0), (0, 0))
    kp = jnp.pad(k.astype(f32), pad)
    vp = jnp.pad(v.astype(f32), pad)
    block_start = jnp.arange(nb) * ATT_BLOCK
    key_idx = block_start[:, None] + jnp.arange(KEY_SPAN)[None, :]
    kw = kp[:, key_idx]
    vw = vp[:, key_idx]
    key_pos = key_idx - WINDOW
    q_pos = block_start[:, None] + jnp.arange(ATT_BLOCK)[None, :]
    rel = key_pos[:, None, :] - q_pos[:, :, None]
    valid = (jnp.abs(rel) <= WINDOW) & (key_pos[:, None, :] >= 0) & (key_pos[:, None, :] < s)
    s_loc = jnp.einsum('bnqhgd,bnkhd->bnhgqk', qb, kw)
    s_loc = jnp.where(valid[None, :, None, None], s_loc, NEG_INF)
    s_ctx = jnp.einsum('bnqhgd,bchd->bnhgqc', qb, k_ctx.astype(f32))
    sink_l = sink.astype(f32).reshape(1, 1, ATT_KV_HEADS, ATT_GROUP, 1, 1)
    m = jnp.maximum(jnp.maximum(s_loc.max(-1, keepdims=True), s_ctx.max(-1, keepdims=True)), sink_l)
    p_loc = jnp.exp(s_loc - m)
    p_ctx = jnp.exp(s_ctx - m)
    denom = p_loc.sum(-1, keepdims=True) + p_ctx.sum(-1, keepdims=True) + jnp.exp(sink_l - m)
    o = jnp.einsum('bnhgqk,bnkhd->bnqhgd', p_loc / denom, vw) + jnp.einsum('bnhgqc,bchd->bnqhgd', p_ctx / denom, v_ctx.astype(f32))
    return o.reshape(b, s, ATT_WIDTH).astype(q.dtype)

def context_attention(q, k, v, sink):
    b, l = q.shape[0], q.shape[1]
    f32 = jnp.float32
    qg = q.astype(f32).reshape(b, l, ATT_KV_HEADS, ATT_GROUP, HEAD_DIM) * (HEAD_DIM ** -0.5)
    sc = jnp.einsum('blhgd,bmhd->bhglm', qg, k.astype(f32))
    sink_l = sink.astype(f32).reshape(1, ATT_KV_HEADS, ATT_GROUP, 1, 1)
    m = jnp.maximum(sc.max(-1, keepdims=True), sink_l)
    p = jnp.exp(sc - m)
    denom = p.sum(-1, keepdims=True) + jnp.exp(sink_l - m)
    o = jnp.einsum('bhglm,bmhd->blhgd', p / denom, v.astype(f32))
    return o.reshape(b, l, ATT_WIDTH).astype(q.dtype)

def token_mix(h_lat, h_ctx, w_in, w_o, log_gamma, gn_w, sink, rope_cos, rope_sin, need_ctx_out):
    f_l, rq_l, rk_l, rv_l, rg_l, aq_l, ak_l, av_l = jnp.split(h_lat @ w_in, IN_OFFSETS, axis=-1)
    f_c, rq_c, rk_c, rv_c, rg_c, aq_c, ak_c, av_c = jnp.split(h_ctx @ w_in, IN_OFFSETS, axis=-1)
    rq_l = apply_axial_rope(to_heads(rq_l, RET_HEADS), rope_cos, rope_sin)
    rk_l = apply_axial_rope(to_heads(rk_l, RET_HEADS), rope_cos, rope_sin)
    ret_l, ret_c = bidirectional_retention(rq_l, rk_l, to_heads(rv_l, RET_HEADS), to_heads(rq_c, RET_HEADS), to_heads(rk_c, RET_HEADS), to_heads(rv_c, RET_HEADS), log_gamma)
    y_ret = retention_output(ret_l, rg_l, gn_w)
    aq_l = apply_axial_rope(to_heads(aq_l, ATT_HEADS), rope_cos, rope_sin)
    ak_l = apply_axial_rope(to_heads(ak_l, ATT_KV_HEADS), rope_cos, rope_sin)
    ak_c = to_heads(ak_c, ATT_KV_HEADS)
    av_c = to_heads(av_c, ATT_KV_HEADS)
    y_att = windowed_attention_latent(aq_l, ak_l, to_heads(av_l, ATT_KV_HEADS), ak_c, av_c, sink)
    y_f = fourier_mix(f_l)
    out_lat = jnp.concatenate([y_f, y_ret, y_att], axis=-1) @ w_o
    if not need_ctx_out:
        return out_lat, None
    y_c = jnp.concatenate([fourier_mix(f_c), retention_output(ret_c, rg_c, gn_w), context_attention(to_heads(aq_c, ATT_HEADS), ak_c, av_c, sink)], axis=-1)
    return out_lat, y_c @ w_o

def setup_inputs(seed: int = 0) -> dict:
    key = jax.random.key(seed)
    ks = jax.random.split(key, 16)
    nrm = jax.random.normal
    f32 = jnp.float32
    x = nrm(ks[0], (BATCH, SEQ, D_MODEL), f32)
    c = nrm(ks[1], (BATCH, D_MODEL), f32)
    ctx = nrm(ks[2], (BATCH, CTX_LEN, D_MODEL), f32)
    c_ctx = nrm(ks[3], (D_MODEL,), f32)
    norm_w = 1.0 + 0.05 * nrm(ks[4], (DEPTH, 3, D_MODEL), f32)
    w_ada = nrm(ks[5], (DEPTH, D_MODEL, N_MOD * D_MODEL), f32) * (0.5 * D_MODEL ** -0.5)
    b_ada = 0.02 * nrm(ks[6], (DEPTH, N_MOD * D_MODEL), f32)
    ffn_w_in = nrm(ks[7], (DEPTH, 2, D_MODEL, 2 * D_FF), f32) * (D_MODEL ** -0.5)
    ffn_w_out = nrm(ks[8], (DEPTH, 2, D_FF, D_MODEL), f32) * (D_FF ** -0.5)
    w_in = nrm(ks[9], (DEPTH, D_MODEL, D_IN), f32) * (D_MODEL ** -0.5)
    w_o = nrm(ks[10], (DEPTH, D_MIX, D_MODEL), f32) * (D_MIX ** -0.5)
    base_logit = jnp.asarray(np.log(2.0 ** (5.0 + np.arange(RET_HEADS)) - 1.0).astype(np.float32))
    ret_decay = base_logit[None, None, :] + 0.1 * nrm(ks[11], (DEPTH, 2, RET_HEADS), f32)
    ret_gn_w = 1.0 + 0.05 * nrm(ks[12], (DEPTH, RET_WIDTH), f32)
    attn_sink = 0.5 * nrm(ks[13], (DEPTH, ATT_HEADS), f32)
    final_norm_w = 1.0 + 0.05 * nrm(ks[14], (D_MODEL,), f32)
    return {'x': x, 'c': c, 'ctx': ctx, 'c_ctx': c_ctx, 'norm_w': norm_w, 'w_ada': w_ada, 'b_ada': b_ada,
            'ffn_w_in': ffn_w_in, 'ffn_w_out': ffn_w_out, 'w_in': w_in, 'w_o': w_o, 'ret_decay': ret_decay,
            'ret_gn_w': ret_gn_w, 'attn_sink': attn_sink, 'final_norm_w': final_norm_w}

def reference(x, c, ctx, c_ctx, norm_w, w_ada, b_ada, ffn_w_in, ffn_w_out, w_in, w_o, ret_decay, ret_gn_w, attn_sink, final_norm_w):
    rope_cos, rope_sin = axial_rope_angles(x.shape[1])
    cond_lat = jax.nn.silu(c)
    cond_ctx = jax.nn.silu(c_ctx)
    h = x
    hc = ctx
    for layer in range(DEPTH):
        need_ctx_out = layer < DEPTH - 1
        mod = (cond_lat @ w_ada[layer] + b_ada[layer]).reshape(x.shape[0], N_MOD, 1, D_MODEL)
        mod_c = (cond_ctx @ w_ada[layer] + b_ada[layer]).reshape(N_MOD, 1, D_MODEL)
        lm = [mod[:, i] for i in range(N_MOD)]
        cm = [mod_c[i] for i in range(N_MOD)]
        h = h + 0.5 * lm[2] * swiglu(modulate(rms_norm(h, norm_w[layer, 0]), lm[0], lm[1]), ffn_w_in[layer, 0], ffn_w_out[layer, 0])
        hc = hc + 0.5 * cm[2] * swiglu(modulate(rms_norm(hc, norm_w[layer, 0]), cm[0], cm[1]), ffn_w_in[layer, 0], ffn_w_out[layer, 0])
        y, yc = token_mix(modulate(rms_norm(h, norm_w[layer, 1]), lm[3], lm[4]),
                          modulate(rms_norm(hc, norm_w[layer, 1]), cm[3], cm[4]),
                          w_in[layer], w_o[layer], jax.nn.log_sigmoid(ret_decay[layer].astype(jnp.float32)),
                          ret_gn_w[layer], attn_sink[layer], rope_cos, rope_sin, need_ctx_out)
        h = h + lm[5] * y
        h = h + 0.5 * lm[8] * swiglu(modulate(rms_norm(h, norm_w[layer, 2]), lm[6], lm[7]), ffn_w_in[layer, 1], ffn_w_out[layer, 1])
        if need_ctx_out:
            hc = hc + cm[5] * yc
            hc = hc + 0.5 * cm[8] * swiglu(modulate(rms_norm(hc, norm_w[layer, 2]), cm[6], cm[7]), ffn_w_in[layer, 1], ffn_w_out[layer, 1])
    return rms_norm(h, final_norm_w)


_drawn_inputs = setup_inputs


def setup_inputs(seed=0):
    import zlib

    import numpy as np

    out = dict(_drawn_inputs(seed))
    spreads = {}
    factors = {'ret_gn_w': 8.0, 'attn_sink': 44.893}
    for name, (base, spread) in spreads.items():
        noise = np.random.default_rng([zlib.crc32(name.encode()), seed]).standard_normal(out[name].shape)
        drawn = base * np.exp(spread * noise) if base else spread * noise
        out[name] = jnp.asarray(drawn.astype(out[name].dtype))
    for name, factor in factors.items():
        out[name] = (out[name] * factor).astype(out[name].dtype)
    return out
```

```python
import numpy as np

import concourse.bass as bass
from concourse import mybir
from contextlib import ExitStack

P = 128
D = 1024
KD = D // P
SEQ = 512
CTX = 256
TOK = SEQ + CTX
DEPTH = 2
DFF = 2816
HALF = DFF // P // 2
NMOD = 9
MT = NMOD * KD
HD = 64
RH = 4
AH = 8
EPS = 1e-6
NEG = -1e30
U_D = 896

WIN_TILES = 16
F_T, RQ_T, RK_T, RV_T, RG_T, AQ_T, AK_T, AV_T = 0, 2, 4, 6, 8, 10, 14, 15
ROPE_TILES = [2, 3, 4, 5, 10, 11, 12, 13, 14]
AQ_COL = 1280
KV_HEADS = 2
GROUP = AH // KV_HEADS

ADA_GROUPS = [(0, 16), (16, 38), (38, 64), (64, 88), (88, 110), (110, 144)]


def constants():
    a = np.arange(SEQ, dtype=np.float64)
    ang = 2 * np.pi * ((a[:, None] * a[None]) % SEQ) / SEQ
    dft = np.stack([np.cos(ang), np.sin(ang)])
    g = np.arange(HD, dtype=np.float64)
    ang = 2 * np.pi * ((g[:, None] * g[None]) % HD) / HD
    z = np.zeros((HD, HD))
    c64, s64 = np.cos(ang), -np.sin(ang)
    ident = np.eye(P)
    block = np.kron(np.eye(2), np.full((HD, HD), 1.0 / HD))
    q, k = np.arange(P)[:, None], np.arange(P)[None]
    small = np.concatenate([
        ident, block, ident - block,
        np.block([[c64, z], [z, c64]]), np.block([[s64, z], [z, s64]]),
        np.where(k >= q, 0.0, NEG), np.where(k <= q, 0.0, NEG)], axis=1)
    dist = (np.arange(U_D)[None] - 384.0) - np.arange(P)[:, None]
    pairs = HD // 4
    inv = np.float32(10000.0) ** (-np.arange(pairs, dtype=np.float32) / np.float32(pairs))
    d = np.arange(P) % HD
    t = np.arange(SEQ)
    pos = np.where((d // 32)[:, None] == 0, t[None] // HD, t[None] % HD).astype(np.float32)
    angle = (pos * inv[d % pairs][:, None]).astype(np.float32).astype(np.float64)
    sign = np.where((d % 32) < pairs, -1.0, 1.0)[:, None]
    rope = np.stack([np.cos(angle), sign * np.sin(angle)])
    return {n: np.ascontiguousarray(v.astype(np.float32)) for n, v in
            dict(dft=dft, small=small, dist=dist, rope=rope).items()}


def transformer(nc, x, c, ctx_in, c_ctx, norm_w, w_ada, b_ada, ffn_w_in, ffn_w_out, w_in, w_o,
                ret_decay, ret_gn_w, attn_sink, final_norm_w, dft, small, dist, rope, out):
    f32, f32r = mybir.dt.float32, mybir.dt.float32r
    ALU = mybir.AluOpType
    ACT = mybir.ActivationFunctionType
    AX = mybir.AxisListType
    ds = bass.ds

    ctx = ExitStack()
    with ctx:
        def sem(name):
            return ctx.enter_context(nc.semaphore(name))

        sizes = dict(h=KD * TOK * 4, xhi=KD * TOK * 4, xlo=KD * TOK * 4, ahi=HALF * TOK * 4,
                     alo=HALF * TOK * 4, raw=2 * HALF * P * 4, whi=2 * HALF * P * 4,
                     wlo=2 * HALF * P * 4, ada=2 * KD * P * 4, m=5 * TOK * 4)
        total = sum(sizes.values())
        slab = ctx.enter_context(nc.sbuf_tensor("slab", [P, total // 4], f32))
        start = {}
        at = nc.sbuf_base - total
        for name, size in sizes.items():
            start[name] = at
            at += size
        a0, x0, m0 = start["ahi"], start["xhi"], start["m"]

        def place(name, shape, dt, offset):
            return nc.alloc_sbuf_tensor_at(name, shape, dt, offset=offset)

        def sb(name, shape, dt=f32):
            return ctx.enter_context(nc.sbuf_tensor(name, shape, dt))

        h = place("h", [P, KD, TOK], f32, start["h"])
        xhi = place("xhi", [P, KD, TOK], f32r, start["xhi"])
        xlo = place("xlo", [P, KD, TOK], f32r, start["xlo"])
        ahi = place("ahi", [P, HALF, TOK], f32r, start["ahi"])
        alo = place("alo", [P, HALF, TOK], f32r, start["alo"])
        raw = place("raw", [P, 2, HALF, P], f32, start["raw"])
        whi = place("whi", [P, 2, HALF, P], f32r, start["whi"])
        wlo = place("wlo", [P, 2, HALF, P], f32r, start["wlo"])
        ada = place("ada", [P, 2, KD, P], f32, start["ada"])
        rstd = place("rstd", [P, TOK], f32, m0)
        tnorm = place("tnorm", [P, 2, TOK], f32, m0 + TOK * 4)
        xfull = place("xfull", [P, 2, TOK], f32, m0 + 3 * TOK * 4)
        gate = place("gate", [P, TOK], f32, m0 + TOK * 4)
        xtok = place("xtok", [P, TOK // P, D], f32, a0)
        rows = place("rows", [P, 3, P], f32, m0)
        t0 = a0 + WIN_TILES * TOK * 4
        z = place("z", [P, WIN_TILES, TOK], f32, a0)
        dft_sb = place("dft_sb", [P, 2, SEQ // P, SEQ], f32, t0)
        rope_sb = place("rope_sb", [P, 2, SEQ], f32, m0)
        swapped = place("swapped", [P, SEQ], f32, m0 + 2 * SEQ * 4)
        pq = place("pq", [P, TOK // P, 4 * P], f32, m0)
        strips = place("strips", [P, 2, U_D + 640], f32, t0)
        strip_b = place("strip_b", [P, 640], f32, t0 + 2 * (U_D + 640) * 4)
        vret = place("vret", [P, TOK // P, 2 * P], f32, m0)
        sdec = place("sdec", [P, 2, TOK], f32, m0 + 2 * TOK * 4)
        osq = place("osq", [P, 2, TOK], f32, x0 + 4 * TOK * 4)
        vatt = place("vatt", [P, TOK // P, P], f32, t0)
        prob = place("prob", [P, 2, 640], f32, t0 + 3072)
        probT = place("probT", [P, 2, 640], f32, t0 + 3072 + 5120)
        otok = place("otok", [P, 2, P], f32, t0 + 3072 + 10240)
        wfin = place("wfin", [P, D], f32, x0)
        osb = place("osb", [P, 2, D], f32, x0 + D * 4)
        junk = place("junk", [P, D], f32, x0 + 3 * D * 4)

        consts = sb("consts", [P, 7 * P])
        ident = consts[:, 0:P]
        block = consts[:, P:2 * P]
        center = consts[:, 2 * P:3 * P]
        cs64 = consts[:, 3 * P:5 * P]
        masks = [consts[:, 5 * P:6 * P], consts[:, 6 * P:7 * P]]
        ones = sb("ones", [P, P])
        dist_sb = sb("dist_sb", [P, U_D])
        eps = sb("eps", [P, 1])
        bias = sb("bias", [P, DEPTH * MT])
        vecs = sb("vecs", [P, 76])
        cond = sb("cond", [P, KD, 2])
        mod = sb("mod", [P, DEPTH * MT, 2])
        acol = sb("acol", [P, KD, 2])
        gcol = sb("gcol", [P, KD, 2])
        sink = sb("sink", [P, DEPTH * AH])
        lg = sb("lg", [P, DEPTH * 2 * RH])
        lgt = sb("lgt", [P, 3, DEPTH * 2 * RH])
        nlg = sb("nlg", [P, DEPTH * 2 * RH])
        lgb = sb("lgb", [P, 2, DEPTH * 2 * RH])
        mx = sb("mx", [P, 2])
        negm = sb("negm", [P, 2])
        esink = sb("esink", [P, 2])
        den = sb("den", [P, 2])
        rden = sb("rden", [P, 2])
        fstat = sb("fstat", [P, 2])

        pg = [ctx.enter_context(nc.psum_tensor(f"pg{i}", [P, 1024], f32)) for i in range(2)]
        pn = ctx.enter_context(nc.psum_tensor("pn", [P, 1024], f32))
        p67 = ctx.enter_context(nc.psum_tensor("p67", [P, 1024], f32))
        pa = [p67[:, 0:512], p67[:, 512:1024]]

        s_raw = [sem(f"raw_loaded{s}") for s in range(2)]
        s_whi = [sem(f"whi_ready{s}") for s in range(2)]
        s_w = [sem(f"weights_ready{s}") for s in range(2)]
        s_unit = [sem(f"unit_done{s}") for s in range(2)]
        s_free = [sem(f"psum_read{s}") for s in range(2)]
        s_ada = [sem(f"ada_loaded{s}") for s in range(2)]
        s_ada_used = sem("ada_used")
        s_mod = sem("mod_ready")
        s_rows = sem("rows_loaded")
        s_const = sem("consts_loaded")
        s_vec = sem("vectors_loaded")
        s_x = sem("x_loaded")
        s_ones = sem("ones_ready")
        s_rowsT = sem("rows_transposed")
        s_cols = sem("columns_ready")
        s_cond = sem("cond_ready")
        s_xT = sem("x_transposed")
        s_xTr = [sem(f"x_transposed_read{b}") for b in range(2)]
        s_lg = sem("decay_exp")
        s_lgd = sem("decay_ready")
        NS = 3 * DEPTH
        s_sq = [sem(f"squares{m}") for m in range(NS)]
        s_squ = [sem(f"squares_used{m}") for m in range(NS)]
        s_r = [sem(f"rstd_ready{m}") for m in range(NS)]
        s_t = [sem(f"t_ready{m}") for m in range(NS)]
        s_xf = [sem(f"xfull_ready{m}") for m in range(NS)]
        s_xn = [sem(f"xn_ready{m}") for m in range(NS)]
        s_coef = [sem(f"coef_ready{m}") for m in range(NS)]
        s_ahi = {(m, hf): sem(f"a_hi{m}_{hf}") for m in (0, 2, 3, 5) for hf in range(2)}
        s_a = {(m, hf): sem(f"a_ready{m}_{hf}") for m in (0, 2, 3, 5) for hf in range(2)}
        s_zr = [sem(f"z_roped{l}") for l in range(DEPTH)]
        s_rope = [sem(f"rope_loaded{l}") for l in range(DEPTH)]
        s_dft = [sem(f"dft_loaded{l}") for l in range(DEPTH)]
        s_f1 = [sem(f"f1_done{l}") for l in range(DEPTH)]
        s_pq = [sem(f"pq_ready{l}") for l in range(DEPTH)]
        s_f2 = [sem(f"f2_done{l}") for l in range(DEPTH)]
        s_yhi = [sem(f"y_hi{l}") for l in range(DEPTH)]
        s_y = [sem(f"y_ready{l}") for l in range(DEPTH)]
        s_vt = [sem(f"vret_done{l}") for l in range(DEPTH)]
        s_v = [sem(f"vret_ready{l}") for l in range(DEPTH)]
        s_st = [sem(f"strip_args{l}") for l in range(DEPTH)]
        s_se = [sem(f"strip_exp{l}") for l in range(DEPTH)]
        s_sr = [sem(f"strip_ready{l}") for l in range(DEPTH)]
        s_s = [sem(f"ret_scores{l}") for l in range(DEPTH)]
        s_sd = [sem(f"ret_decayed{l}") for l in range(DEPTH)]
        s_pv = [sem(f"ret_pv{l}") for l in range(DEPTH)]
        s_osq = [sem(f"ret_squares{l}") for l in range(DEPTH)]
        s_var = [sem(f"ret_var{l}") for l in range(DEPTH)]
        s_rr = [sem(f"ret_rstd{l}") for l in range(DEPTH)]
        s_va = [sem(f"vatt_done{l}") for l in range(DEPTH)]
        s_var2 = [sem(f"vatt_ready{l}") for l in range(DEPTH)]
        s_as = [sem(f"att_scores{l}") for l in range(DEPTH)]
        s_nm = [sem(f"att_negmax{l}") for l in range(DEPTH)]
        s_den = [sem(f"att_den_read{l}") for l in range(DEPTH)]
        s_p = [sem(f"att_probs{l}") for l in range(DEPTH)]
        s_pt = [sem(f"att_probsT{l}") for l in range(DEPTH)]
        s_ptl = [sem(f"att_pt_local{l}") for l in range(DEPTH)]
        s_ptc = [sem(f"att_pt_ctx{l}") for l in range(DEPTH)]
        s_av = [sem(f"att_av{l}") for l in range(DEPTH)]
        s_o = [sem(f"att_out{l}") for l in range(DEPTH)]
        s_oT = [sem(f"att_outT{l}") for l in range(DEPTH)]
        s_dv = sem("dve_chain")
        s_ac = sem("act_chain")
        s_wf = sem("wfin_loaded")
        s_fT = sem("final_transposed")
        s_fs = sem("final_stat")
        s_fo = sem("final_rows")
        s_out = [sem(f"out_stored{i}") for i in range(2)]

        phases = []
        for l in range(DEPTH):
            for kind, m in (("ffn", 3 * l), ("mix", 3 * l + 1), ("ffn", 3 * l + 2)):
                if kind == "ffn":
                    for hf in range(2):
                        phases.append(("in", l, m, hf, 2 * HALF, KD))
                        phases.append(("out", l, m, hf, KD, HALF))
                else:
                    phases.append(("win", l, m, 0, WIN_TILES, KD))
                    phases.append(("wo", l, m, 0, KD, KD))

        def dmas(kind, j):
            return 3 if kind == "wo" else 2 if kind == "win" and AQ_T <= 2 * j < AK_T else 1

        first, pair, loads = [], 0, 0
        for ph in phases:
            first.append((pair, loads))
            pair += ph[4] // 2
            loads += sum(dmas(ph[0], j) for j in range(ph[4] // 2))

        def pair0(i):
            return first[i][0]

        def read_value(i, j):
            return j + (pair0(i) + 2)

        def raw_value(i, j):
            kind = phases[i][0]
            if kind == "win":
                return 16 * (first[i][1] + sum(dmas(kind, a) for a in range(j + 1)))
            return j * (16 * dmas(kind, 0)) + 16 * (first[i][1] + dmas(kind, 0))

        def tokens(i):
            kind, l, m = phases[i][:3]
            return SEQ if l == DEPTH - 1 and (kind == "wo" or m == NS - 1) else TOK

        def h_value(m, k):
            if m == 0:
                return 1
            i = max(i for i, ph in enumerate(phases) if ph[2] == m - 1)
            return read_value(i, k // 2)

        def norm_tokens(m):
            return SEQ if m == NS - 1 else TOK

        def win_tokens(l, n):
            return TOK if l < DEPTH - 1 or n in (4, 5, 6, 7, 14, 15) else SEQ

        def ada_group(l, m, hf):
            return {(0, 0, 0): 1, (0, 0, 1): 2, (0, 2, 0): 3, (1, 3, 0): 4, (1, 3, 1): 5}.get((l, m, hf))

        ret_blocks = TOK // P

        def att_units(l):
            blocks = range(TOK // P if l < DEPTH - 1 else SEQ // P)
            return [(n, t, s) for n in blocks for t in range(GROUP) for s in range(KV_HEADS)]

        def local_keys(n):
            if n >= SEQ // P:
                return 0, 0
            lo, hi = max(n - 1, 0), min(n + 1, SEQ // P - 1)
            return lo, hi - lo + 1

        def y_count(l):
            return 4 + len(att_units(l)) // 2

        blk = ctx.enter_context(nc.Block())

        @blk.sync
        def _(sp):
            for l in range(DEPTH):
                sp.dma_start(rows[0:MT, l, :], b_ada[l].rearrange("(r q) -> r q", q=P)).then_inc(s_rows, 16)
            sp.dma_start(rows[0:48, 2, :], norm_w.rearrange("l i (k q) -> (l i k) q", q=P)).then_inc(s_rows, 16)
            sp.dma_start(rows[48:56, 2, :], c.rearrange("b (k q) -> (b k) q", q=P)).then_inc(s_rows, 16)
            sp.dma_start(rows[56:64, 2, :], c_ctx.rearrange("(k q) -> k q", q=P)).then_inc(s_rows, 16)
            sp.dma_start(rows[64:68, 2, :], ret_gn_w.rearrange("l (k q) -> (l k) q", q=P)).then_inc(s_rows, 16)
            sp.dma_start(consts[:, :], small).then_inc(s_const, 16)
            for tt in range(TOK // P):
                src = x[0] if tt < SEQ // P else ctx_in[0]
                r = tt * P - (0 if tt < SEQ // P else SEQ)
                sp.dma_start(xtok[:, tt, :], src[r:r + P, :]).then_inc(s_x, 16)

            def load_ada(t, i=None, layer=None):
                layer = t // MT if layer is None else layer
                if i is not None:
                    sp.wait_ge(s_ada_used, i * 2 + (t - 1))
                elif t >= 2:
                    sp.wait_ge(s_ada_used, t - 1)
                c0 = (t - layer * MT) * P
                cols = slice(c0, c0 + P) if i is None else ds(i * (2 * P) + c0, P)
                sp.dma_start(ada[:, t % 2], w_ada[layer][:, cols].rearrange("(k p) n -> p k n", p=P)
                             ).then_inc(s_ada[t % 2], 16)

            def load_unit(i, s, j, src, wait):
                if wait is not None:
                    sp.wait_ge(s_w[s], wait)
                if phases[i][0] == "wo":
                    sp.dma_start(raw[:, s, 0:4], src[0]).then_inc(s_raw[s], 16)
                    for v in range(KV_HEADS):
                        sp.dma_start(raw[HD * v:HD * v + HD, s, 4:8], src[1 + v]).then_inc(s_raw[s], 16)
                else:
                    sp.dma_start(raw[:, s, 0:phases[i][5]], src).then_inc(s_raw[s], 16)

            def ffn_in_src(l, m, col):
                return ffn_w_in[l, m % 3 // 2][:, col].rearrange("(k p) n -> p k n", p=P)

            for i, (kind, l, m, hf, units, kt) in enumerate(phases):
                j0 = pair0(i)
                if kind == "in":
                    c0 = hf * HALF * P
                    g = ada_group(l, m, hf)
                    load_unit(i, 0, 0, ffn_in_src(l, m, slice(c0, c0 + P)), j0 if j0 else None)
                    load_unit(i, 1, 0, ffn_in_src(l, m, slice(DFF + c0, DFF + c0 + P)), j0 if j0 else None)
                    if i == 0:
                        sp.dma_start(dist_sb[:, :], dist).then_inc(s_vec, 16)
                        sp.dma_start(sink[:, :], attn_sink.rearrange("l n -> (l n)").partition_broadcast(P)
                                     ).then_inc(s_vec, 16)
                        sp.dma_start(lg[:, :], ret_decay.rearrange("l d n -> (l d n)").partition_broadcast(P)
                                     ).then_inc(s_vec, 16)
                        for t in range(*ADA_GROUPS[0]):
                            load_ada(t)
                    if g is not None:
                        b = ADA_GROUPS[g][0]
                        load_ada(b)
                        load_ada(b + 1)
                    cut = (MT - b) // 2 if g is not None and b < MT < b + 2 * HALF else HALF
                    for f0, f1, layer in [(1, cut, l)] + ([(cut, HALF, l + 1)] if cut < HALF else []):
                        with sp.Fori(f0, f1) as f:
                            load_unit(i, 0, f, ffn_in_src(l, m, ds(f * P + c0, P)), f + j0)
                            load_unit(i, 1, f, ffn_in_src(l, m, ds(f * P + (DFF + c0), P)), f + j0)
                            if g is not None:
                                load_ada(b, f, layer)
                                load_ada(b + 1, f, layer)
                    if g is not None:
                        for t in range(b + 2 * HALF, ADA_GROUPS[g][1]):
                            load_ada(t)
                elif kind == "out":
                    r0 = hf * HALF * P
                    with sp.Fori(0, units // 2) as j:
                        for s in range(2):
                            src = ffn_w_out[l, m % 3 // 2][r0:r0 + HALF * P, ds(j * (2 * P) + s * P, P)]
                            load_unit(i, s, j, src.rearrange("(k p) n -> p k n", p=P), j + j0)
                elif kind == "win":
                    for n in range(WIN_TILES):
                        if n == 2:
                            sp.wait_ge(s_xn[m], KD)
                            sp.dma_start(rope_sb[:, :, :], rope.rearrange("a p t -> p a t")).then_inc(s_rope[l], 16)
                        if n == 4:
                            sp.dma_start(dft_sb[:, :, :, :], dft.rearrange("a (t p) q -> p a t q", p=P)
                                         ).then_inc(s_dft[l], 16)
                        if AQ_T <= n < AK_T:
                            sp.wait_ge(s_w[n % 2], j0 + n // 2)
                            for v in range(KV_HEADS):
                                c0 = AQ_COL + (v * GROUP + n - AQ_T) * HD
                                src = w_in[l][:, c0:c0 + HD].rearrange("(k p) n -> p k n", p=P)
                                sp.dma_start(raw[:, n % 2, 0:KD, v * HD:(v + 1) * HD], src
                                             ).then_inc(s_raw[n % 2], 16)
                        else:
                            c0 = n * P
                            src = w_in[l][:, c0:c0 + P].rearrange("(k p) n -> p k n", p=P)
                            load_unit(i, n % 2, n // 2, src, j0 + n // 2)
                else:
                    with sp.Fori(0, units // 2) as j:
                        for s in range(2):
                            cols = ds(j * (2 * P) + s * P, P)
                            src = [w_o[l][0:512, cols].rearrange("(k p) n -> p k n", p=P)] + [
                                w_o[l][512 + 256 * v:768 + 256 * v, cols].rearrange("(t q) n -> q t n", q=HD)
                                for v in range(KV_HEADS)]
                            load_unit(i, s, j, src, j + j0)
            for s in range(2):
                sp.wait_ge(s_free[s], h_value(NS, KD - 2))
            sp.dma_start(wfin[:, :], final_norm_w.partition_broadcast(P)).then_inc(s_wf, 16)
            for tt in range(SEQ // P):
                sp.wait_ge(s_fo, tt + 1)
                sp.dma_start(out[0, tt * P:(tt + 1) * P, :], osb[:, tt % 2]).then_inc(s_out[tt % 2], 16)
            for b in range(2):
                sp.wait_ge(s_out[b], 16 * (SEQ // P // 2))

        @blk.gpsimd
        def _(pool):
            nc.gpsimd.memset(eps[:, :], EPS).then_inc(s_ones, 1)
            nc.gpsimd.memset(ones[:, :], 1.0).then_inc(s_ones, 1)

        @blk.tensor
        def _(pe):
            def split_product(s, kt, i, hi, lo, t, before):
                parts = [(0, SEQ)] + ([(SEQ, TOK)] if t == TOK else [])
                last = None
                for k in range(kt):
                    if before is not None:
                        before(k)
                    for n, (w, v) in enumerate(((whi, hi), (whi, lo), (wlo, hi))):
                        for p0, p1 in parts:
                            last = nc.tensor.matmul(pg[s][:, p0:p1], w[:, s, k], v[:, k, p0:p1],
                                                    start=(k == 0 and n == 0), stop=(k == kt - 1 and n == 2))
                last.then_inc(s_unit[s], 1)

            def unit(i, s, j, hi, lo, t, before=None):
                pe.wait_ge(s_w[s], j + (pair0(i) + 1))
                pe.wait_ge(s_free[s], read_value(i, j - 1))
                split_product(s, phases[i][5], i, hi, lo, t, before)

            def ada_tile(g, t, i=None):
                b = ADA_GROUPS[g][0]
                pe.wait_ge(s_ada[t % 2], 16 * (t // 2 + 1) if i is None else i * 16 + 16 * (t // 2 + 1))
                col = 2 * (t - b)
                dst = pa[g % 2][:, col:col + 2] if i is None else p67[:, ds(i * 4 + (512 * (g % 2) + col), 2)]
                for k in range(KD):
                    last = nc.tensor.matmul(dst, ada[:, t % 2, k], cond[:, k], start=(k == 0), stop=(k == KD - 1))
                last.then_inc(s_ada_used, 1)

            pe.wait_ge(s_rows, 16 * 6)
            pe.wait_ge(s_const, 16)
            for r, n in enumerate((MT, MT, 68)):
                last = nc.tensor.transpose(pn[:, r * P:r * P + n], rows[0:n, r, :], ident[0:n, 0:n])
            last.then_inc(s_rowsT, 1)
            for tt in range(TOK // P):
                pe.wait_ge(s_x, 16 * (TOK // P))
                if tt >= 2:
                    pe.wait_ge(s_xTr[tt % 2], tt // 2)
                for k in range(KD):
                    last = nc.tensor.transpose(pg[tt % 2][:, k * P:(k + 1) * P], xtok[:, tt, k * P:(k + 1) * P],
                                               ident)
                last.then_inc(s_xT, 1)
            pe.wait_ge(s_cond, 1)
            for t in range(*ADA_GROUPS[0]):
                ada_tile(0, t)
            pe.wait_ge(s_ones, 2)

            def norm(m):
                t = norm_tokens(m)
                for k in range(KD):
                    pe.wait_ge(s_sq[m], k + 1)
                    for p0, p1 in [(0, SEQ)] + ([(SEQ, TOK)] if t == TOK else []):
                        last = nc.tensor.matmul(pn[:, p0:p1], ones[:, :], xfull[:, k % 2, p0:p1],
                                                start=(k == 0), stop=(k == KD - 1))
                    last.then_inc(s_squ[m], 1)

            def mix(i, l):
                nt = TOK // P if l < DEPTH - 1 else SEQ // P
                tq = nt * P
                for s in range(2):
                    pe.wait_ge(s_free[s], read_value(i, WIN_TILES // 2 - 1))
                pe.wait_ge(s_zr[l], len(ROPE_TILES))
                for tt in range(nt):
                    if tt >= 2:
                        pe.wait_ge(s_pq[l], tt - 1)
                    for ft in range(2):
                        last = nc.tensor.matmul(pa[tt % 2][:, ft * 256:ft * 256 + 256],
                                                z[:, F_T + ft, tt * P:(tt + 1) * P], cs64, start=True, stop=True)
                    last.then_inc(s_f1[l], 1)
                pe.wait_ge(s_pq[l], nt)
                pe.wait_ge(s_dft[l], 16)
                for ft in range(2):
                    dst = (pn, pg[0])[ft]
                    for tt in range(nt):
                        for cs in range(2):
                            w = pq[:, tt, ft * 256 + cs * P:ft * 256 + cs * P + P]
                            if tt < SEQ // P:
                                last = nc.tensor.matmul(dst[:, 0:SEQ], w, dft_sb[:, cs, tt],
                                                        start=(tt == 0 and cs == 0), stop=(tt == 3 and cs == 1))
                            else:
                                last = nc.tensor.matmul(dst[:, SEQ:TOK], w, dft_sb[:, cs, tt - 4, 0:SEQ:2],
                                                        start=(tt == 4 and cs == 0), stop=(tt == 5 and cs == 1))
                    last.then_inc(s_f2[l], 1)
                for tt in range(ret_blocks):
                    if tt >= 2:
                        pe.wait_ge(s_v[l], tt - 1)
                    for v in range(2):
                        last = nc.tensor.matmul(pa[tt % 2][:, v * P:(v + 1) * P],
                                                z[:, RV_T + v, tt * P:(tt + 1) * P], center, start=True, stop=True)
                    last.then_inc(s_vt[l], 1)
                pe.wait_ge(s_v[l], ret_blocks)
                pe.wait_ge(s_y[l], 2)
                spare = [pg[1], pn]
                steps = [(hd, jt) for hd in range(RH) for jt in range(ret_blocks)]

                def scores(r):
                    hd, jt = steps[r]
                    p0 = HD * (hd % 2)
                    if r >= 2:
                        pe.wait_ge(s_sd[l], r - 1)
                    kT = z[p0:p0 + HD, RK_T + hd // 2, jt * P:(jt + 1) * P]
                    q = z[p0:p0 + HD, RQ_T + hd // 2]
                    last = nc.tensor.matmul(spare[r % 2][:, 0:SEQ], kT, q[:, 0:SEQ], start=True, stop=True)
                    if jt >= SEQ // P and tq == TOK:
                        last = nc.tensor.matmul(spare[r % 2][:, SEQ:TOK], kT, q[:, SEQ:TOK], start=True, stop=True)
                    last.then_inc(s_s[l], 1)

                def values(r):
                    hd, jt = steps[r]
                    p0 = HD * (hd % 2)
                    pe.wait_ge(s_sd[l], r + 1)
                    o = (pg[0], p67)[hd // 2]
                    w = vret[:, jt, hd * HD:(hd + 1) * HD]
                    last = nc.tensor.matmul(o[p0:p0 + HD, 0:SEQ], w, sdec[:, r % 2, 0:SEQ],
                                            start=(jt == 0), stop=(jt == ret_blocks - 1))
                    if jt >= SEQ // P and tq == TOK:
                        last = nc.tensor.matmul(o[p0:p0 + HD, SEQ:TOK], w, sdec[:, r % 2, SEQ:TOK],
                                                start=(jt == SEQ // P), stop=(jt == ret_blocks - 1))
                    last.then_inc(s_pv[l], 1)

                scores(0)
                for r in range(len(steps)):
                    if r + 1 < len(steps):
                        scores(r + 1)
                    values(r)
                for p in range(2):
                    pe.wait_ge(s_osq[l], p + 1)
                    for p0, p1 in [(0, SEQ)] + ([(SEQ, TOK)] if tq == TOK else []):
                        last = nc.tensor.matmul(spare[p][:, p0:p1], block, osq[:, p, p0:p1], start=True, stop=True)
                    last.then_inc(s_var[l], 1)
                pe.wait_ge(s_y[l], 4)
                for tt in range(TOK // P):
                    last = nc.tensor.transpose(p67[:, tt * P:(tt + 1) * P], z[:, AV_T, tt * P:(tt + 1) * P], ident)
                last.then_inc(s_va[l], 1)
                units = att_units(l)

                def att_scores(q):
                    n, t, s = units[q]
                    lo, nk = local_keys(n)
                    p0 = HD * s
                    if q >= 2:
                        pe.wait_ge(s_p[l], q - 1)
                    w = z[p0:p0 + HD, AQ_T + t, n * P:(n + 1) * P]
                    kT = z[p0:p0 + HD, AK_T]
                    if nk:
                        c0 = SEQ - nk * P
                        left, right = n > 0, n < SEQ // P - 1
                        nc.tensor.matmul(pg[q % 2][:, c0:SEQ], w, kT[:, lo * P:(lo + nk) * P], start=True, stop=False,
                                         skip_group_check=True)
                        if left:
                            nc.tensor.matmul(pg[q % 2][:, c0:c0 + P], ident, masks[0], start=False,
                                             stop=not right, skip_group_check=True)
                        if right:
                            nc.tensor.matmul(pg[q % 2][:, SEQ - P:SEQ], ident, masks[1], start=False, stop=True,
                                             skip_group_check=True)
                    nc.tensor.matmul(pg[q % 2][:, SEQ:TOK], w, kT[:, SEQ:TOK], start=True, stop=True
                                     ).then_inc(s_as[l], 1)

                def att_transpose(q):
                    n, t, s = units[q]
                    nk, nb = local_keys(n)[1], max(local_keys(n)[1], 1)
                    pe.wait_ge(s_p[l], q + 1)
                    if q >= 1:
                        pe.wait_ge(s_ptc[l], q)
                        pe.wait_ge(s_ptl[l], q)
                    for j in range(nk + 2):
                        dst = j * P if j < nb else 512 + (j - nb) * P
                        last = nc.tensor.transpose(pn[:, dst:dst + P], prob[:, q % 2, j * P:(j + 1) * P], ident)
                    last.then_inc(s_pt[l], 1)

                def att_values(q):
                    n, t, s = units[q]
                    lo, nk = local_keys(n)
                    pe.wait_ge(s_ptc[l], q + 1)
                    pe.wait_ge(s_ptl[l], q + 1)
                    if s == 0 and q >= 2:
                        pe.wait_ge(s_o[l], q // 2)
                    tiles = [lo + j for j in range(nk)] + [4, 5]
                    for j, kt in enumerate(tiles):
                        last = nc.tensor.matmul(pa[0][:, s * HD:(s + 1) * HD], probT[:, q % 2, j * P:(j + 1) * P],
                                                vatt[:, kt, s * HD:(s + 1) * HD],
                                                start=(j == 0), stop=(j == len(tiles) - 1))
                    last.then_inc(s_av[l], 1)

                def att_out(pr):
                    pe.wait_ge(s_o[l], pr + 1)
                    if pr:
                        pe.wait_ge(s_y[l], 4 + pr)
                    nc.tensor.transpose(pa[1][:, 0:P], otok[:, pr % 2], ident).then_inc(s_oT[l], 1)

                att_scores(0)
                pe.wait_ge(s_var2[l], 1)
                for q in range(len(units) + 3):
                    if q + 1 < len(units):
                        att_scores(q + 1)
                    if 1 <= q <= len(units):
                        att_values(q - 1)
                    if q >= 3 and q % 2:
                        att_out((q - 3) // 2)
                    if q < len(units):
                        att_transpose(q)

            for i, (kind, l, m, hf, units, kt) in enumerate(phases):
                t = tokens(i)
                if kind == "in":
                    if hf == 0:
                        norm(m)
                    g = ada_group(l, m, hf)
                    if g is not None and g >= 2:
                        pe.wait_ge(s_mod, g - 1)
                    with pe.Fori(0, HALF) as f:
                        unit(i, 0, f, xhi, xlo, t, lambda k: pe.wait_ge(s_xn[m], k + 1))
                        unit(i, 1, f, xhi, xlo, t)
                        if g is not None:
                            for b in range(2):
                                ada_tile(g, ADA_GROUPS[g][0] + b, f)
                    if g is not None:
                        for at in range(ADA_GROUPS[g][0] + 2 * HALF, ADA_GROUPS[g][1]):
                            ada_tile(g, at)
                elif kind == "out":
                    with pe.Fori(0, units // 2) as j:
                        unit(i, 0, j, ahi, alo, t, lambda k: pe.wait_ge(s_a[m, hf], k + 1))
                        unit(i, 1, j, ahi, alo, t)
                elif kind == "win":
                    norm(m)
                    runs, n = [], 0
                    while n < WIN_TILES:
                        e = n
                        while e < WIN_TILES and win_tokens(l, e) == win_tokens(l, n):
                            e += 2
                        runs.append((n // 2, e // 2, win_tokens(l, n)))
                        n = e
                    for b, e, tw in runs:
                        with pe.Fori(b, e) as j:
                            unit(i, 0, j, xhi, xlo, tw, lambda k: pe.wait_ge(s_xn[m], k + 1))
                            unit(i, 1, j, xhi, xlo, tw)
                    mix(i, l)
                else:
                    pe.wait_ge(s_y[l], y_count(l))
                    with pe.Fori(0, units // 2) as j:
                        unit(i, 0, j, xhi, xlo, t)
                        unit(i, 1, j, xhi, xlo, t)
            for s in range(2):
                pe.wait_ge(s_free[s], h_value(NS, KD - 2))
            for tt in range(SEQ // P):
                if tt >= 2:
                    pe.wait_ge(s_fo, tt - 1)
                for k in range(KD):
                    last = nc.tensor.transpose(pg[tt % 2][:, k * P:(k + 1) * P], h[:, k, tt * P:(tt + 1) * P], ident)
                last.then_inc(s_fT, 1)

        @blk.scalar
        def _(act):
            chain = [0]

            def link(ins):
                chain[0] += 1
                ins.then_inc(s_ac, 1)
                act.wait_ge(s_ac, chain[0])

            def split_hi(i, s, j, after=None):
                act.wait_ge(s_raw[s], raw_value(i, j))
                if i or not isinstance(j, int) or j:
                    act.wait_ge(s_unit[s], j + pair0(i))
                nk = phases[i][5]
                nc.scalar.copy(whi[:, s, 0:nk], raw[:, s, 0:nk]).then_inc(s_whi[s], 1)

            act.wait_ge(s_cols, 1)
            nc.scalar.activation(cond[:, :, :], vecs[:, 48:64].rearrange("p (v k) -> p k v", v=2), ACT.Silu
                                 ).then_inc(s_cond, 1)
            for tt in range(0, TOK // P, 2):
                act.wait_ge(s_xT, tt + 1)
                nc.scalar.copy(h[:, :, tt * P:(tt + 1) * P], pg[0][:, :].rearrange("p (k t) -> p k t", k=KD)
                               ).then_inc(s_xTr[0] if tt < 4 else s_free[0], 1)
            split_hi(0, 0, 0)
            split_hi(0, 1, 0)
            act.wait_ge(s_lgd, 1)
            link(nc.scalar.activation(lgt[:, 1], lgt[:, 0], ACT.Exp, scale=-1.0))
            nc.scalar.activation(lgt[:, 2], lgt[:, 1], ACT.Ln, bias=1.0).then_inc(s_lg, 1)

            def norm(m):
                t = norm_tokens(m)
                act.wait_ge(s_ones, 1)
                if m == 0:
                    act.wait_ge(s_free[1], 1)
                for k in range(KD):
                    act.wait_ge(s_free[k % 2], h_value(m, k))
                    if k >= 2:
                        act.wait_ge(s_squ[m], k - 1)
                    nc.scalar.activation(xfull[:, k % 2, 0:t], h[:, k, 0:t], ACT.Square).then_inc(s_sq[m], 1)
                act.wait_ge(s_squ[m], KD)
                link(nc.scalar.activation(rstd[:, 0:t], pn[:, 0:t], ACT.Ln, bias=eps[:, :], scale=1.0 / D))
                nc.scalar.activation(rstd[:, 0:t], rstd[:, 0:t], ACT.Exp, scale=-0.5).then_inc(s_r[m], 1)
                act.wait_ge(s_coef[m], 1)
                shift = m // 3 * MT + m % 3 * 3 * KD
                for k in range(KD):
                    act.wait_ge(s_t[m], k + 1)
                    if k >= 2:
                        act.wait_ge(s_xn[m], k - 1)
                    for v, (p0, p1) in enumerate([(0, SEQ)] + ([(SEQ, TOK)] if t == TOK else [])):
                        for dst in (xfull[:, k % 2, p0:p1], xhi[:, k, p0:p1]):
                            last = nc.scalar.activation(dst, tnorm[:, k % 2, p0:p1], ACT.Identity,
                                                        bias=mod[:, shift + k, v:v + 1], scale=acol[:, k, v:v + 1])
                    last.then_inc(s_xf[m], 1)

            def mix(i, l):
                nt = TOK // P if l < DEPTH - 1 else SEQ // P
                tq = nt * P
                for tt in range(nt):
                    act.wait_ge(s_f1[l], tt + 1)
                    length = SEQ if tt < SEQ // P else CTX
                    nc.scalar.mul(pq[:, tt], pa[tt % 2], float((length * HD) ** -0.5)).then_inc(s_pq[l], 1)
                for ft in range(2):
                    act.wait_ge(s_f2[l], ft + 1)
                    nc.scalar.copy(xhi[:, ft, 0:tq], (pn, pg[0])[ft][:, 0:tq]).then_inc(s_yhi[l], 1)

                def strip(hd):
                    b = l * 2 * RH + hd
                    s = hd % 2
                    act.wait_ge(s_st[l], hd + 1)
                    if hd >= 2:
                        act.wait_ge(s_sd[l], ret_blocks * (hd - 1))
                        act.wait_ge(s_sr[l], hd)
                    elif hd == 1:
                        act.wait_ge(s_sr[l], hd)
                    nc.scalar.activation(strips[:, s, 0:U_D], strips[:, s, 0:U_D], ACT.Exp)
                    nc.scalar.activation(strips[:, s, U_D:], dist_sb[:, 256:U_D], ACT.Exp,
                                         bias=lgb[:, 0, b:b + 1], scale=lg[:, b:b + 1])
                    nc.scalar.activation(strip_b[:, :], dist_sb[:, 256:U_D], ACT.Exp,
                                         bias=lgb[:, 1, b + RH:b + RH + 1], scale=nlg[:, b + RH:b + RH + 1]
                                         ).then_inc(s_se[l], 1)

                for hd in range(RH):
                    strip(hd)
                for p in range(2):
                    act.wait_ge(s_pv[l], 2 * ret_blocks * (p + 1))
                    nc.scalar.activation(osq[:, p, 0:tq], (pg[0], p67)[p][:, 0:tq], ACT.Square).then_inc(s_osq[l], 1)
                for p in range(2):
                    act.wait_ge(s_var[l], p + 1)
                    link(nc.scalar.activation(osq[:, p, 0:tq], (pg[1], pn)[p][:, 0:tq], ACT.Ln, bias=eps[:, :]))
                    nc.scalar.activation(osq[:, p, 0:tq], osq[:, p, 0:tq], ACT.Exp, scale=-0.5).then_inc(s_rr[l], 1)
                units = att_units(l)
                for q in range(len(units) + 4):
                    if q < len(units):
                        n, t, s = units[q]
                        hd = l * AH + t + GROUP * s
                        w = (local_keys(n)[1] + 2) * P
                        act.wait_ge(s_nm[l], q + 1)
                        if q >= 2:
                            act.wait_ge(s_pt[l], q - 1)
                            act.wait_ge(s_den[l], q - 1)
                        nc.scalar.activation(esink[:, q % 2:q % 2 + 1], sink[:, hd:hd + 1], ACT.Exp,
                                             bias=negm[:, q % 2:q % 2 + 1])
                        nc.scalar.activation(prob[:, q % 2, 0:w], pg[q % 2][:, TOK - w:TOK], ACT.Exp,
                                             bias=negm[:, q % 2:q % 2 + 1], accum_out=den[:, q % 2:q % 2 + 1]
                                             ).then_inc(s_p[l], 1)
                    if 1 <= q <= len(units):
                        nk = local_keys(units[q - 1][0])[1]
                        nb = max(nk, 1)
                        act.wait_ge(s_pt[l], q)
                        if q >= 3:
                            act.wait_ge(s_av[l], q - 2)
                        nc.scalar.copy(probT[:, (q - 1) % 2, nb * P:(nk + 2) * P], pn[:, 512:512 + (nk + 2 - nb) * P]
                                       ).then_inc(s_ptc[l], 1)
                    if q >= 4 and q % 2 == 0:
                        pr = (q - 4) // 2
                        n, t, _ = units[2 * pr]
                        act.wait_ge(s_oT[l], pr + 1)
                        nc.scalar.copy(xhi[:, 4 + t, n * P:(n + 1) * P], pa[1][:, 0:P]).then_inc(s_yhi[l], 1)

            for i, (kind, l, m, hf, units, kt) in enumerate(phases):
                t = tokens(i)
                j0 = pair0(i)
                more = i + 1 < len(phases)
                if kind in ("in", "win") and hf == 0:
                    norm(m)
                if kind == "in":
                    def step(f, nxt, jn):
                        act.wait_ge(s_unit[0], f + (j0 + 1))
                        if hf or not isinstance(f, int) or f:
                            if isinstance(f, int) and f == 0:
                                act.wait_ge(s_a[m, 0], HALF)
                            else:
                                act.wait_ge(s_a[m, hf], f)
                        nc.scalar.activation(gate[:, 0:t], pg[0][:, 0:t], ACT.Silu).then_inc(s_free[0], 1)
                        split_hi(nxt, 0, jn)
                        split_hi(nxt, 1, jn)

                    step(0, i, 1)
                    with act.Fori(1, HALF - 1) as f:
                        step(f, i, f + 1)
                    step(HALF - 1, i + 1, 0)
                elif kind in ("out", "wo"):
                    with act.Fori(0, units // 2 - 1) as j:
                        split_hi(i, 0, j + 1)
                        split_hi(i, 1, j + 1)
                    if more:
                        split_hi(i + 1, 0, 0)
                        split_hi(i + 1, 1, 0)
                else:
                    for n in range(WIN_TILES):
                        s, tw = n % 2, win_tokens(l, n)
                        act.wait_ge(s_unit[s], j0 + n // 2 + 1)
                        if RG_T <= n < AQ_T:
                            nc.scalar.activation(z[:, n, 0:tw], pg[s][:, 0:tw], ACT.Silu).then_inc(s_free[s], 1)
                        else:
                            scaled = RK_T <= n < RV_T or AQ_T <= n < AK_T
                            nc.scalar.mul(z[:, n, 0:tw], pg[s][:, 0:tw], HD ** -0.5 if scaled else 1.0
                                          ).then_inc(s_free[s], 1)
                        nxt, jn = (i, n // 2 + 1) if n + 2 < WIN_TILES else (i + 1, 0)
                        split_hi(nxt, s, jn)
                    mix(i, l)
            for tt in range(SEQ // P):
                act.wait_ge(s_fT, tt + 1)
                if tt >= 2:
                    act.wait_ge(s_fo, tt - 1)
                b = slice(tt % 2, tt % 2 + 1)
                link(nc.scalar.activation(junk[:, :], pg[tt % 2][:, :], ACT.Square, accum_out=fstat[:, b]))
                link(nc.scalar.activation(fstat[:, b], fstat[:, b], ACT.Ln, bias=eps[:, :], scale=1.0 / D))
                nc.scalar.activation(fstat[:, b], fstat[:, b], ACT.Exp, scale=-0.5).then_inc(s_fs, 1)

        @blk.vector
        def _(dve):
            chain = [0]

            def link(ins):
                chain[0] += 1
                ins.then_inc(s_dv, 1)
                dve.wait_ge(s_dv, chain[0])

            def split_lo(i, s, j):
                dve.wait_ge(s_whi[s], j + (pair0(i) + 1))
                nk = phases[i][5]
                nc.vector.tensor_sub(wlo[:, s, 0:nk], raw[:, s, 0:nk], whi[:, s, 0:nk].bitcast(f32)
                                     ).then_inc(s_w[s], 1)

            dve.wait_ge(s_rowsT, 1)
            nc.vector.tensor_copy(bias[:, 0:MT], pn[:, 0:MT])
            nc.vector.tensor_copy(bias[:, MT:2 * MT], pn[:, P:P + MT])
            nc.vector.tensor_copy(vecs[:, 0:68], pn[:, 2 * P:2 * P + 68]).then_inc(s_cols, 1)
            dve.wait_ge(s_cols, 1)
            for tt in range(1, TOK // P, 2):
                dve.wait_ge(s_xT, tt + 1)
                nc.vector.tensor_copy(h[:, :, tt * P:(tt + 1) * P], pg[1][:, :].rearrange("p (k t) -> p k t", k=KD)
                                      ).then_inc(s_xTr[1] if tt < 4 else s_free[1], 1)
            split_lo(0, 0, 0)
            split_lo(0, 1, 0)
            dve.wait_ge(s_vec, 16 * 3)
            link(nc.vector.tensor_scalar(lgt[:, 1], lg[:, :], -1.0, None, ALU.mult))
            nc.vector.tensor_tensor(lgt[:, 0], lg[:, :], lgt[:, 1], ALU.max).then_inc(s_lgd, 1)
            dve.wait_ge(s_lg, 1)
            dve.wait_ge(s_lgd, 1)
            link(nc.vector.tensor_scalar(lgt[:, 0], lgt[:, 1], 1.0, -1.0, ALU.add, ALU.add))
            link(nc.vector.tensor_scalar(nlg[:, :], lgt[:, 0], 0.0, None, ALU.is_equal))
            link(nc.vector.tensor_tensor(lgt[:, 0], lgt[:, 0], nlg[:, :], ALU.add))
            link(nc.vector.tensor_tensor(lgt[:, 2], lgt[:, 2], nlg[:, :], ALU.add))
            link(nc.vector.reciprocal(lgt[:, 0], lgt[:, 0]))
            link(nc.vector.tensor_tensor(lgt[:, 2], lgt[:, 2], lgt[:, 0], ALU.mult))
            link(nc.vector.tensor_tensor(lgt[:, 2], lgt[:, 2], lgt[:, 1], ALU.mult))
            link(nc.vector.scalar_tensor_tensor(lg[:, :], lg[:, :], 0.0, lgt[:, 2], ALU.min, ALU.subtract))
            link(nc.vector.tensor_scalar(nlg[:, :], lg[:, :], -1.0, None, ALU.mult))
            link(nc.vector.tensor_scalar(lgb[:, 0], lg[:, :], float(CTX), None, ALU.mult))
            link(nc.vector.tensor_scalar(lgb[:, 1], lg[:, :], float(SEQ), None, ALU.mult))

            def read_mod(g):
                a, b = ADA_GROUPS[g]
                dve.wait_ge(s_ada_used, b)
                nc.vector.tensor_tensor(mod[:, a:b], pa[g % 2][:, 0:2 * (b - a)].rearrange("p (t v) -> p t v", v=2),
                                        bias[:, a:b].unsqueeze(2).broadcast_to([P, b - a, 2]), ALU.add
                                        ).then_inc(s_mod, 1)
                dve.wait_ge(s_mod, g + 1)

            def coefficients(m):
                b = m // 3 * MT + (m % 3 * 3 + 1) * KD
                nc.vector.scalar_tensor_tensor(acol[:, :, :], mod[:, b:b + KD], 1.0,
                                               vecs[:, m * KD:(m + 1) * KD].unsqueeze(2).broadcast_to([P, KD, 2]),
                                               ALU.add, ALU.mult).then_inc(s_coef[m], 1)

            def gates(m):
                b = m // 3 * MT + (m % 3 * 3 + 2) * KD
                link(nc.vector.tensor_scalar(gcol[:, :, :], mod[:, b:b + KD], 1.0 if m % 3 == 1 else 0.5, None,
                                             ALU.mult))

            def norm(m):
                t = norm_tokens(m)
                dve.wait_ge(s_r[m], 1)

                def low(k):
                    dve.wait_ge(s_xf[m], k + 1)
                    nc.vector.tensor_sub(xlo[:, k, 0:t], xfull[:, k % 2, 0:t], xhi[:, k, 0:t].bitcast(f32)
                                         ).then_inc(s_xn[m], 1)

                for k in range(KD):
                    nc.vector.tensor_tensor(tnorm[:, k % 2, 0:t], h[:, k, 0:t], rstd[:, 0:t], ALU.mult
                                            ).then_inc(s_t[m], 1)
                    if k:
                        low(k - 1)
                low(KD - 1)

            def add_branch(i, s, j, n):
                dve.wait_ge(s_unit[s], j + (pair0(i) + 1))
                t = tokens(i)
                col = slice(n, n + 1) if isinstance(n, int) else ds(n, 1)
                for v, (p0, p1) in enumerate([(0, SEQ)] + ([(SEQ, TOK)] if t == TOK else [])):
                    hv = h[:, col, p0:p1].rearrange("p o t -> p (o t)")
                    last = nc.vector.scalar_tensor_tensor(hv, pg[s][:, p0:p1], gcol[:, col, v:v + 1].rearrange(
                        "p o v -> p (o v)"), hv, ALU.mult, ALU.add)
                last.then_inc(s_free[s], 1)

            def y_low(l, k, src, p0, p1, hi_count):
                dve.wait_ge(s_yhi[l], hi_count)
                nc.vector.tensor_sub(xlo[:, k, p0:p1], src, xhi[:, k, p0:p1].bitcast(f32)).then_inc(s_y[l], 1)

            def mix(i, l):
                nt = TOK // P if l < DEPTH - 1 else SEQ // P
                tq = nt * P
                for ft in range(2):
                    y_low(l, ft, (pn, pg[0])[ft][:, 0:tq], 0, tq, ft + 1)
                for tt in range(ret_blocks):
                    dve.wait_ge(s_vt[l], tt + 1)
                    nc.vector.tensor_copy(vret[:, tt], pa[tt % 2][:, 0:256]).then_inc(s_v[l], 1)

                def strip_args(hd):
                    b = l * 2 * RH + hd
                    s = hd % 2
                    link(nc.vector.tensor_scalar(strips[:, s, 0:U_D], dist_sb[:, :], nlg[:, b + RH:b + RH + 1], None,
                                                 ALU.mult))
                    nc.vector.scalar_tensor_tensor(strips[:, s, 0:U_D], dist_sb[:, :], lg[:, b:b + 1],
                                                   strips[:, s, 0:U_D], ALU.mult, ALU.min).then_inc(s_st[l], 1)

                def strip_sum(hd):
                    s = hd % 2
                    dve.wait_ge(s_se[l], hd + 1)
                    nc.vector.tensor_tensor(strips[:, s, 384:512], strips[:, s, 384:512], ident, ALU.add)
                    nc.vector.tensor_tensor(strips[:, s, U_D:], strips[:, s, U_D:], strip_b[:, :], ALU.add
                                            ).then_inc(s_sr[l], 1)
                    dve.wait_ge(s_sr[l], hd + 1)

                strip_args(0)
                strip_sum(0)
                strip_args(1)
                for hd in range(RH):
                    s = hd % 2
                    for jt in range(ret_blocks):
                        r = hd * ret_blocks + jt
                        src = (pg[1], pn)[r % 2]
                        dve.wait_ge(s_s[l], r + 1)
                        if r >= 2:
                            dve.wait_ge(s_pv[l], r - 1)
                        if jt < SEQ // P:
                            g = strips[:, s, 384 - jt * P:384 - jt * P + SEQ]
                        else:
                            c0 = U_D + P * (1 - (jt - 4))
                            g = strips[:, s, c0:c0 + SEQ]
                            if tq == TOK:
                                g0 = 384 - (jt - 4) * P
                                nc.vector.tensor_tensor(sdec[:, r % 2, SEQ:TOK], src[:, SEQ:TOK],
                                                        strips[:, s, g0:g0 + CTX], ALU.mult)
                        nc.vector.tensor_tensor(sdec[:, r % 2, 0:SEQ], src[:, 0:SEQ], g, ALU.mult
                                                ).then_inc(s_sd[l], 1)
                        if jt == 1 and hd + 1 < RH:
                            strip_sum(hd + 1)
                    if hd + 2 < RH:
                        dve.wait_ge(s_sd[l], ret_blocks * (hd + 1))
                        strip_args(hd + 2)
                for p in range(2):
                    dve.wait_ge(s_rr[l], p + 1)
                    o = osq[:, p, 0:tq]
                    link(nc.vector.tensor_tensor(o, (pg[0], p67)[p][:, 0:tq], o, ALU.mult))
                    link(nc.vector.scalar_tensor_tensor(o, o, vecs[:, 64 + 2 * l + p:65 + 2 * l + p],
                                                        z[:, RG_T + p, 0:tq], ALU.mult, ALU.mult))
                    link(nc.vector.tensor_copy(xhi[:, 2 + p, 0:tq], o))
                    nc.vector.tensor_sub(xlo[:, 2 + p, 0:tq], o, xhi[:, 2 + p, 0:tq].bitcast(f32)).then_inc(s_y[l], 1)
                dve.wait_ge(s_va[l], 1)
                nc.vector.tensor_copy(vatt[:, :, :], p67[:, 0:TOK].rearrange("p (t n) -> p t n", n=P)
                                      ).then_inc(s_var2[l], 1)
                units = att_units(l)
                for q in range(len(units) + 4):
                    if q < len(units):
                        n, t, s = units[q]
                        hd = l * AH + t + GROUP * s
                        w = (local_keys(n)[1] + 2) * P
                        b = slice(q % 2, q % 2 + 1)
                        dve.wait_ge(s_as[l], q + 1)
                        link(nc.vector.reduce_max(mx[:, b], pg[q % 2][:, TOK - w:TOK], AX.X))
                        nc.vector.tensor_scalar(negm[:, b], mx[:, b], sink[:, hd:hd + 1], -1.0, ALU.max, ALU.mult
                                                ).then_inc(s_nm[l], 1)
                    if 1 <= q <= len(units):
                        n = units[q - 1][0]
                        nb = max(local_keys(n)[1], 1)
                        b = slice((q - 1) % 2, (q - 1) % 2 + 1)
                        dve.wait_ge(s_pt[l], q)
                        if q >= 3:
                            dve.wait_ge(s_av[l], q - 2)
                        nc.vector.tensor_copy(probT[:, (q - 1) % 2, 0:nb * P], pn[:, 0:nb * P]).then_inc(s_ptl[l], 1)
                        nc.vector.tensor_tensor(rden[:, b], den[:, b], esink[:, b], ALU.add).then_inc(s_den[l], 1)
                        dve.wait_ge(s_den[l], q)
                        link(nc.vector.reciprocal(rden[:, b], rden[:, b]))
                        if q % 2 == 0:
                            pr = q // 2 - 1
                            dve.wait_ge(s_av[l], q)
                            for s in range(2):
                                last = nc.vector.tensor_scalar(otok[:, pr % 2, s * HD:(s + 1) * HD],
                                                               pa[0][:, s * HD:(s + 1) * HD], rden[:, s:s + 1], None,
                                                               ALU.mult)
                            last.then_inc(s_o[l], 1)
                    if q >= 4 and q % 2 == 0:
                        pr = (q - 4) // 2
                        n, t, _ = units[2 * pr]
                        y_low(l, 4 + t, pa[1][:, 0:P], n * P, (n + 1) * P, 3 + pr)

            read_mod(0)
            for i, (kind, l, m, hf, units, kt) in enumerate(phases):
                t = tokens(i)
                j0 = pair0(i)
                more = i + 1 < len(phases)
                if kind in ("in", "win") and hf == 0:
                    coefficients(m)
                    norm(m)
                if kind == "in":
                    def step(f, nxt, jn):
                        split_lo(nxt, 0, jn)
                        dve.wait_ge(s_unit[1], f + (j0 + 1))
                        dve.wait_ge(s_free[0], read_value(i, f))
                        col = slice(f, f + 1) if isinstance(f, int) else ds(f, 1)
                        hi = ahi[:, col, 0:t].rearrange("p o t -> p (o t)")
                        lo = alo[:, col, 0:t].rearrange("p o t -> p (o t)")
                        nc.vector.tensor_tensor(gate[:, 0:t], gate[:, 0:t], pg[1][:, 0:t], ALU.mult
                                                ).then_inc(s_free[1], 1)
                        dve.wait_ge(s_free[1], read_value(i, f))
                        nc.vector.tensor_copy(hi, gate[:, 0:t]).then_inc(s_ahi[m, hf], 1)
                        dve.wait_ge(s_ahi[m, hf], f + 1)
                        nc.vector.tensor_sub(lo, gate[:, 0:t], hi.bitcast(f32)).then_inc(s_a[m, hf], 1)
                        split_lo(nxt, 1, jn)

                    with dve.Fori(0, HALF - 1) as f:
                        step(f, i, f + 1)
                    step(HALF - 1, i + 1, 0)
                    g = ada_group(l, m, hf)
                    if g is not None:
                        read_mod(g)
                    if hf == 0:
                        gates(m)
                elif kind in ("out", "wo"):
                    if kind == "wo":
                        gates(m)
                    with dve.Fori(0, units // 2 - 1) as j:
                        for s in range(2):
                            add_branch(i, s, j, j * 2 + s)
                            split_lo(i, s, j + 1)
                    for s in range(2):
                        add_branch(i, s, units // 2 - 1, units - 2 + s)
                        if more:
                            split_lo(i + 1, s, 0)
                else:
                    for n in range(WIN_TILES):
                        s = n % 2
                        if n in ROPE_TILES:
                            dve.wait_ge(s_free[s], read_value(i, n // 2))
                            if n == ROPE_TILES[0]:
                                dve.wait_ge(s_rope[l], 16)
                            else:
                                dve.wait_ge(s_zr[l], ROPE_TILES.index(n))
                            zn = z[:, n, 0:SEQ]
                            link(nc.vector.stream_shuffle(swapped[:, :], zn, [(a + 16) % 32 for a in range(32)]))
                            link(nc.vector.tensor_tensor(zn, zn, rope_sb[:, 0], ALU.mult))
                            link(nc.vector.tensor_tensor(swapped[:, :], swapped[:, :], rope_sb[:, 1], ALU.mult))
                            nc.vector.tensor_tensor(zn, zn, swapped[:, :], ALU.add).then_inc(s_zr[l], 1)
                        nxt, jn = (i, n // 2 + 1) if n + 2 < WIN_TILES else (i + 1, 0)
                        split_lo(nxt, s, jn)
                    mix(i, l)
            dve.wait_ge(s_wf, 16)
            for tt in range(SEQ // P):
                dve.wait_ge(s_fs, tt + 1)
                if tt >= 2:
                    dve.wait_ge(s_out[tt % 2], 16)
                nc.vector.scalar_tensor_tensor(osb[:, tt % 2], pg[tt % 2][:, :], fstat[:, tt % 2:tt % 2 + 1],
                                               wfin[:, :], ALU.mult, ALU.mult).then_inc(s_fo, 1)


INPUTS = ['x', 'c', 'ctx', 'c_ctx', 'norm_w', 'w_ada', 'b_ada', 'ffn_w_in', 'ffn_w_out', 'w_in', 'w_o',
          'ret_decay', 'ret_gn_w', 'attn_sink', 'final_norm_w']


def kernel(**inputs):
    import concourse.bacc as bacc
    from concourse.bass_utils import run_bass_kernel_spmd

    nc = bacc.Bacc("TRN2", target_bir_lowering=False, num_devices=1)
    arrays, args = {}, []
    tables = constants()
    for name in INPUTS + list(tables):
        a = np.ascontiguousarray(inputs[name] if name in inputs else tables[name])
        arrays[f"in_{name}"] = a
        args.append(nc.dram_tensor(f"in_{name}", a.shape, mybir.dt.from_np(a.dtype), kind="ExternalInput").ap())
    shape = (1, SEQ, D)
    args.append(nc.dram_tensor("out_h", shape, mybir.dt.float32, kind="ExternalOutput").ap())
    transformer(nc, *args)
    return run_bass_kernel_spmd(nc, [arrays], core_ids=[0]).results[0]["out_h"]
```

```python
import numpy as np

import concourse.bass as bass
from concourse import mybir
from contextlib import ExitStack

P = 128
D = 1024
KD = D // P
SEQ = 512
CTX = 256
TOK = SEQ + CTX
DEPTH = 2
DFF = 2816
HALF = DFF // P // 2
NMOD = 9
MT = NMOD * KD
HD = 64
RH = 4
AH = 8
EPS = 1e-6
NEG = -1e30
U_D = 896

WIN_TILES = 16
F_T, RQ_T, RK_T, RV_T, RG_T, AQ_T, AK_T, AV_T = 0, 2, 4, 6, 8, 10, 14, 15
ROPE_TILES = [2, 3, 4, 5, 10, 11, 12, 13, 14]
AQ_COL = 1280
KV_HEADS = 2
GROUP = AH // KV_HEADS

ADA_FIRST = 16
ADA_PAIRS = {(0, 0, 0): (16, 11, 1), (0, 0, 1): (40, 11, 1), (0, 1, 0): (64, 11, 1),
             (1, 0, 0): (88, 11, 3), (1, 0, 1): (116, 11, 3)}


def constants():
    a = np.arange(SEQ, dtype=np.float64)
    ang = 2 * np.pi * ((a[:, None] * a[None]) % SEQ) / SEQ
    dft = np.stack([np.cos(ang), np.sin(ang)])
    g = np.arange(HD, dtype=np.float64)
    ang = 2 * np.pi * ((g[:, None] * g[None]) % HD) / HD
    z = np.zeros((HD, HD))
    c64, s64 = np.cos(ang), -np.sin(ang)
    ident = np.eye(P)
    block = np.kron(np.eye(2), np.full((HD, HD), 1.0 / HD))
    q, k = np.arange(P)[:, None], np.arange(P)[None]
    small = np.concatenate([
        ident, block, ident - block,
        np.block([[c64, z], [z, c64]]), np.block([[s64, z], [z, s64]]),
        np.where(k >= q, 0.0, NEG), np.where(k <= q, 0.0, NEG),
        np.tile(np.eye(32)[:, :2], (4, 1))], axis=1)
    dist = (np.arange(U_D)[None] - 384.0) - np.arange(P)[:, None]
    pairs = HD // 4
    inv = np.float32(10000.0) ** (-np.arange(pairs, dtype=np.float32) / np.float32(pairs))
    d = np.arange(P) % HD
    t = np.arange(SEQ)
    pos = np.where((d // 32)[:, None] == 0, t[None] // HD, t[None] % HD).astype(np.float32)
    angle = (pos * inv[d % pairs][:, None]).astype(np.float32).astype(np.float64)
    sign = np.where((d % 32) < pairs, -1.0, 1.0)[:, None]
    rope = np.stack([np.cos(angle), sign * np.sin(angle)])
    return {n: np.ascontiguousarray(v.astype(np.float32)) for n, v in
            dict(dft=dft, small=small, dist=dist, rope=rope).items()}


def transformer(nc, x, c, ctx_in, c_ctx, norm_w, w_ada, b_ada, ffn_w_in, ffn_w_out, w_in, w_o,
                ret_decay, ret_gn_w, attn_sink, final_norm_w, dft, small, dist, rope, out):
    f32, f32r = mybir.dt.float32, mybir.dt.float32r
    ALU = mybir.AluOpType
    ACT = mybir.ActivationFunctionType
    AX = mybir.AxisListType
    ds = bass.ds

    ctx = ExitStack()
    with ctx:
        def sem(name):
            return ctx.enter_context(nc.semaphore(name))

        sizes = dict(h=KD * TOK * 4, xhi=KD * TOK * 4, xlo=KD * TOK * 4, ahi=HALF * TOK * 4,
                     alo=HALF * TOK * 4, raw=2 * HALF * P * 4, whi=2 * HALF * P * 4,
                     wlo=2 * HALF * P * 4, ada=2 * KD * P * 4, m=5 * TOK * 4)
        total = sum(sizes.values())
        slab = ctx.enter_context(nc.sbuf_tensor("slab", [P, total // 4], f32))
        start = {}
        at = nc.sbuf_base - total
        for name, size in sizes.items():
            start[name] = at
            at += size
        a0, x0, m0 = start["ahi"], start["xhi"], start["m"]

        def place(name, shape, dt, offset):
            return nc.alloc_sbuf_tensor_at(name, shape, dt, offset=offset)

        def sb(name, shape, dt=f32):
            return ctx.enter_context(nc.sbuf_tensor(name, shape, dt))

        h = place("h", [P, KD, TOK], f32, start["h"])
        xhi = place("xhi", [P, KD, TOK], f32r, start["xhi"])
        xlo = place("xlo", [P, KD, TOK], f32r, start["xlo"])
        ahi = place("ahi", [P, HALF, TOK], f32r, start["ahi"])
        alo = place("alo", [P, HALF, TOK], f32r, start["alo"])
        raw = place("raw", [P, 2, HALF, P], f32, start["raw"])
        whi = place("whi", [P, 2, HALF, P], f32r, start["whi"])
        wlo = place("wlo", [P, 2, HALF, P], f32r, start["wlo"])
        ada = place("ada", [P, 2, KD // 2, 2 * P], f32, start["ada"])
        rstd = place("rstd", [P, TOK], f32, m0)
        tnorm = place("tnorm", [P, 2, TOK], f32, m0 + TOK * 4)
        xfull = place("xfull", [P, 2, TOK], f32, m0 + 3 * TOK * 4)
        gate = place("gate", [P, TOK], f32, m0 + TOK * 4)
        xtok = place("xtok", [P, TOK // P, D], f32, start["alo"])
        ada_first = place("ada_first", [P, KD, ADA_FIRST * P], f32, x0)
        part_first = place("part_first", [P, ADA_FIRST * P], f32, x0 + KD * ADA_FIRST * P * 4)
        rows = place("rows", [P, 3, P], f32, m0)
        t0 = a0 + WIN_TILES * TOK * 4
        z = place("z", [P, WIN_TILES, TOK], f32, a0)
        dft_sb = place("dft_sb", [P, 2, SEQ // P, SEQ], f32, t0)
        rope_sb = place("rope_sb", [P, 2, SEQ], f32, m0)
        swapped = place("swapped", [P, SEQ], f32, m0 + 2 * SEQ * 4)
        pq = place("pq", [P, TOK // P, 4 * P], f32, m0)
        strips = place("strips", [P, 2, U_D + 640], f32, t0)
        strip_b = place("strip_b", [P, 640], f32, t0 + 2 * (U_D + 640) * 4)
        vret = place("vret", [P, TOK // P, 2 * P], f32, m0)
        sdec = place("sdec", [P, 2, TOK], f32, m0 + 2 * TOK * 4)
        osq = place("osq", [P, 2, TOK], f32, x0 + 4 * TOK * 4)
        vatt = place("vatt", [P, TOK // P, P], f32, t0)
        prob = place("prob", [P, 2, 640], f32, t0 + 3072)
        probT = place("probT", [P, 2, 640], f32, t0 + 3072 + 5120)
        otok = place("otok", [P, 2, P], f32, t0 + 3072 + 10240)
        wfin = place("wfin", [P, D], f32, x0)
        osb = place("osb", [P, 2, D], f32, x0 + D * 4)
        junk = place("junk", [P, D], f32, x0 + 3 * D * 4)

        consts = sb("consts", [P, 7 * P + 2])
        fold = consts[:, 7 * P:7 * P + 2]
        part = sb("part", [P, 2 * P])
        ident = consts[:, 0:P]
        block = consts[:, P:2 * P]
        center = consts[:, 2 * P:3 * P]
        cs64 = consts[:, 3 * P:5 * P]
        masks = [consts[:, 5 * P:6 * P], consts[:, 6 * P:7 * P]]
        ones = sb("ones", [P, P])
        dist_sb = sb("dist_sb", [P, U_D])
        eps = sb("eps", [P, 1])
        bias = sb("bias", [P, DEPTH * MT])
        vecs = sb("vecs", [P, 76])
        cond = sb("cond", [P, KD, 32])
        mod = sb("mod", [P, DEPTH * MT, 2])
        acol = sb("acol", [P, KD, 2])
        gcol = sb("gcol", [P, KD, 2])
        sink = sb("sink", [P, DEPTH * AH])
        lg = sb("lg", [P, DEPTH * 2 * RH])
        lgt = sb("lgt", [P, 3, DEPTH * 2 * RH])
        nlg = sb("nlg", [P, DEPTH * 2 * RH])
        lgb = sb("lgb", [P, 2, DEPTH * 2 * RH])
        mx = sb("mx", [P, 2])
        negm = sb("negm", [P, 2])
        esink = sb("esink", [P, 2])
        den = sb("den", [P, 2])
        rden = sb("rden", [P, 2])
        fstat = sb("fstat", [P, 2])

        pg = [ctx.enter_context(nc.psum_tensor(f"pg{i}", [P, 1024], f32)) for i in range(2)]
        pn = ctx.enter_context(nc.psum_tensor("pn", [P, 1024], f32))
        p67 = ctx.enter_context(nc.psum_tensor("p67", [P, 1024], f32))
        pa = [p67[:, 0:512], p67[:, 512:1024]]

        s_raw = [sem(f"raw_loaded{s}") for s in range(2)]
        s_whi = [sem(f"whi_ready{s}") for s in range(2)]
        s_w = [sem(f"weights_ready{s}") for s in range(2)]
        s_unit = [sem(f"unit_done{s}") for s in range(2)]
        s_free = [sem(f"psum_read{s}") for s in range(2)]
        s_ada = [sem(f"ada_loaded{s}") for s in range(2)]
        s_ada0 = [sem(f"ada_first_loaded{q}") for q in range(4)]
        s_ada_first = sem("ada_first_done")
        s_part0 = [sem(f"part_first_copied{b}") for b in range(2)]
        s_fold0 = sem("ada_first_folded")
        s_part = sem("ada_part_copied")
        s_fold = sem("ada_folded")
        s_ada_used = sem("ada_used")
        s_mod = sem("mod_ready")
        s_rows = sem("rows_loaded")
        s_const = sem("consts_loaded")
        s_vec = sem("vectors_loaded")
        s_x = sem("x_loaded")
        s_ones = sem("ones_ready")
        s_rowsT = sem("rows_transposed")
        s_cols = sem("columns_ready")
        s_cond = sem("cond_ready")
        s_xT = sem("x_transposed")
        s_xTr = [sem(f"x_transposed_read{b}") for b in range(2)]
        s_lg = sem("decay_exp")
        s_lgd = sem("decay_ready")
        NS = 3 * DEPTH
        s_sq = sem("squares")
        s_acc = sem("squares_summed")
        s_ss = sem("sum_squares")
        s_r = sem("rstd_ready")
        s_t = sem("t_ready")
        s_xf = sem("xfull_ready")
        s_xn = sem("xn_ready")
        s_coef = sem("coef_ready")
        s_ahi = {(m, hf): sem(f"a_hi{m}_{hf}") for m in (0, 2, 3, 5) for hf in range(2)}
        s_a = {(m, hf): sem(f"a_ready{m}_{hf}") for m in (0, 2, 3, 5) for hf in range(2)}
        s_zr = [sem(f"z_roped{l}") for l in range(DEPTH)]
        s_rope = [sem(f"rope_loaded{l}") for l in range(DEPTH)]
        s_dft = [sem(f"dft_loaded{l}") for l in range(DEPTH)]
        s_f1 = [sem(f"f1_done{l}") for l in range(DEPTH)]
        s_pq = [sem(f"pq_ready{l}") for l in range(DEPTH)]
        s_f2 = [sem(f"f2_done{l}") for l in range(DEPTH)]
        s_yhi = [sem(f"y_hi{l}") for l in range(DEPTH)]
        s_y = [sem(f"y_ready{l}") for l in range(DEPTH)]
        s_vt = [sem(f"vret_done{l}") for l in range(DEPTH)]
        s_v = [sem(f"vret_ready{l}") for l in range(DEPTH)]
        s_st = [sem(f"strip_args{l}") for l in range(DEPTH)]
        s_se = [sem(f"strip_exp{l}") for l in range(DEPTH)]
        s_sr = [sem(f"strip_ready{l}") for l in range(DEPTH)]
        s_s = [sem(f"ret_scores{l}") for l in range(DEPTH)]
        s_sd = [sem(f"ret_decayed{l}") for l in range(DEPTH)]
        s_pv = [sem(f"ret_pv{l}") for l in range(DEPTH)]
        s_osq = [sem(f"ret_squares{l}") for l in range(DEPTH)]
        s_var = [sem(f"ret_var{l}") for l in range(DEPTH)]
        s_rr = [sem(f"ret_rstd{l}") for l in range(DEPTH)]
        s_va = [sem(f"vatt_done{l}") for l in range(DEPTH)]
        s_var2 = [sem(f"vatt_ready{l}") for l in range(DEPTH)]
        s_as = [sem(f"att_scores{l}") for l in range(DEPTH)]
        s_nm = [sem(f"att_negmax{l}") for l in range(DEPTH)]
        s_den = [sem(f"att_den_read{l}") for l in range(DEPTH)]
        s_p = [sem(f"att_probs{l}") for l in range(DEPTH)]
        s_pt = [sem(f"att_probsT{l}") for l in range(DEPTH)]
        s_ptl = [sem(f"att_pt_local{l}") for l in range(DEPTH)]
        s_ptc = [sem(f"att_pt_ctx{l}") for l in range(DEPTH)]
        s_av = [sem(f"att_av{l}") for l in range(DEPTH)]
        s_o = [sem(f"att_out{l}") for l in range(DEPTH)]
        s_oT = [sem(f"att_outT{l}") for l in range(DEPTH)]
        s_dv = sem("dve_chain")
        s_ac = sem("act_chain")
        s_wf = sem("wfin_loaded")
        s_fT = sem("final_transposed")
        s_fs = sem("final_stat")
        s_fo = sem("final_rows")
        s_out = [sem(f"out_stored{i}") for i in range(2)]

        phases = []
        for l in range(DEPTH):
            for kind, m in (("ffn", 3 * l), ("mix", 3 * l + 1), ("ffn", 3 * l + 2)):
                if kind == "ffn":
                    for hf in range(2):
                        phases.append(("in", l, m, hf, 2 * HALF, KD))
                        phases.append(("out", l, m, hf, KD, HALF))
                else:
                    phases.append(("win", l, m, 0, WIN_TILES, KD))
                    phases.append(("wo", l, m, 0, KD, KD))

        def dmas(kind, j):
            return 3 if kind == "wo" else 2 if kind == "win" and AQ_T <= 2 * j < AK_T else 1

        first, pair, loads = [], 0, 0
        for ph in phases:
            first.append((pair, loads))
            pair += ph[4] // 2
            loads += sum(dmas(ph[0], j) for j in range(ph[4] // 2))

        def pair0(i):
            return first[i][0]

        def read_value(i, j):
            return j + (pair0(i) + 2)

        def raw_value(i, j):
            kind = phases[i][0]
            if kind == "win":
                return 16 * (first[i][1] + sum(dmas(kind, a) for a in range(j + 1)))
            return j * (16 * dmas(kind, 0)) + 16 * (first[i][1] + dmas(kind, 0))

        def tokens(i):
            kind, l, m = phases[i][:3]
            return SEQ if l == DEPTH - 1 and (kind == "wo" or m == NS - 1) else TOK

        def h_value(m, k):
            if m == 0:
                return 1
            i = max(i for i, ph in enumerate(phases) if ph[2] == m - 1)
            return read_value(i, k // 2)

        def next_norm(i):
            kind, l, m, hf = phases[i][:4]
            return m + 1 if (kind == "wo" or (kind == "out" and hf)) and m + 1 < NS else None

        def norm_tokens(m):
            return SEQ if m == NS - 1 else TOK

        def win_tokens(l, n):
            return TOK if l < DEPTH - 1 or n in (4, 5, 6, 7, 14, 15) else SEQ

        def ada_runs(i, n):
            kind, l, m, hf = phases[i][:4]
            b, first_pairs, second_pairs = ADA_PAIRS.get((l, m % 3 // 2, hf), (0, 0, 0))
            count = {"in": first_pairs, "out": second_pairs}.get(kind, 0)
            if kind == "out":
                b += 2 * first_pairs
            runs, at = [], 0
            while at < min(count, n):
                layer = (b + 2 * at) // MT
                end = min(count, n, ((layer + 1) * MT - b) // 2)
                runs.append((at, end, b, layer))
                at = end
            if at < n:
                runs.append((at, n, None, l))
            return runs

        ret_blocks = TOK // P

        def att_units(l):
            blocks = range(TOK // P if l < DEPTH - 1 else SEQ // P)
            return [(n, t, s) for n in blocks for t in range(GROUP) for s in range(KV_HEADS)]

        def local_keys(n):
            if n >= SEQ // P:
                return 0, 0
            lo, hi = max(n - 1, 0), min(n + 1, SEQ // P - 1)
            return lo, hi - lo + 1

        def y_count(l):
            return 4 + len(att_units(l)) // 2

        blk = ctx.enter_context(nc.Block())

        @blk.sync
        def _(sp):
            for l in range(DEPTH):
                sp.dma_start(rows[0:MT, l, :], b_ada[l].rearrange("(r q) -> r q", q=P)).then_inc(s_rows, 16)
            sp.dma_start(rows[0:48, 2, :], norm_w.rearrange("l i (k q) -> (l i k) q", q=P)).then_inc(s_rows, 16)
            sp.dma_start(rows[48:56, 2, :], c.rearrange("b (k q) -> (b k) q", q=P)).then_inc(s_rows, 16)
            sp.dma_start(rows[56:64, 2, :], c_ctx.rearrange("(k q) -> k q", q=P)).then_inc(s_rows, 16)
            sp.dma_start(rows[64:68, 2, :], ret_gn_w.rearrange("l (k q) -> (l k) q", q=P)).then_inc(s_rows, 16)
            sp.dma_start(consts[:, :], small).then_inc(s_const, 16)
            for tt in range(TOK // P):
                src = x[0] if tt < SEQ // P else ctx_in[0]
                r = tt * P - (0 if tt < SEQ // P else SEQ)
                sp.dma_start(xtok[:, tt, :], src[r:r + P, :]).then_inc(s_x, 16)

            def load_ada(t, i, layer):
                for b in range(2):
                    if not (isinstance(i, int) and t + 2 * i == ADA_FIRST):
                        sp.wait_ge(s_ada_used, i * 2 + (t + b - ADA_FIRST - 1))
                    c0 = (t - layer * MT) * P
                    sp.dma_start(ada[:, b], w_ada[layer][D // 2 * b:D // 2 * (b + 1), ds(i * (2 * P) + c0, 2 * P)
                                                         ].rearrange("(k p) n -> p k n", p=P)).then_inc(s_ada[b], 16)

            def load_unit(i, s, j, src, wait):
                if wait is not None:
                    sp.wait_ge(s_w[s], wait)
                if phases[i][0] == "wo":
                    sp.dma_start(raw[:, s, 0:4], src[0]).then_inc(s_raw[s], 16)
                    for v in range(KV_HEADS):
                        sp.dma_start(raw[HD * v:HD * v + HD, s, 4:8], src[1 + v]).then_inc(s_raw[s], 16)
                else:
                    sp.dma_start(raw[:, s, 0:phases[i][5]], src).then_inc(s_raw[s], 16)

            def ffn_in_src(l, m, col):
                return ffn_w_in[l, m % 3 // 2][:, col].rearrange("(k p) n -> p k n", p=P)

            for i, (kind, l, m, hf, units, kt) in enumerate(phases):
                j0 = pair0(i)
                if kind == "in":
                    c0 = hf * HALF * P

                    def load_step(f, b, layer):
                        load_unit(i, 0, f, ffn_in_src(l, m, ds(f * P + c0, P)), f + j0)
                        load_unit(i, 1, f, ffn_in_src(l, m, ds(f * P + (DFF + c0), P)),
                                  f + j0)
                        if b is not None:
                            load_ada(b, f, layer)
                elif kind == "out":
                    r0 = hf * HALF * P

                    def load_step(j, b, layer):
                        for s in range(2):
                            src = ffn_w_out[l, m % 3 // 2][r0:r0 + HALF * P, ds(j * (2 * P) + s * P, P)]
                            load_unit(i, s, j, src.rearrange("(k p) n -> p k n", p=P), j + j0)
                        if b is not None:
                            load_ada(b, j, layer)
                if kind in ("in", "out"):
                    for a, e, b, layer in ada_runs(i, units // 2):
                        if i == 0 and a == 0:
                            load_unit(i, 0, 0, ffn_in_src(l, m, slice(0, P)), None)
                            load_unit(i, 1, 0, ffn_in_src(l, m, slice(DFF, DFF + P)), None)
                            for q in range(4):
                                cols = slice(q * 4 * P, (q + 1) * 4 * P)
                                sp.dma_start(ada_first[:, :, cols], w_ada[0][:, cols].rearrange(
                                    "(k p) n -> p k n", p=P)).then_inc(s_ada0[q], 16)
                            sp.dma_start(dist_sb[:, :], dist).then_inc(s_vec, 16)
                            sp.dma_start(sink[:, :], attn_sink.rearrange("l n -> (l n)").partition_broadcast(P)
                                         ).then_inc(s_vec, 16)
                            sp.dma_start(lg[:, :], ret_decay.rearrange("l d n -> (l d n)").partition_broadcast(P)
                                         ).then_inc(s_vec, 16)
                            load_ada(b, 0, layer)
                            a = 1
                        with sp.Fori(a, e) as j:
                            load_step(j, b, layer)
                elif kind == "win":
                    for n in range(WIN_TILES):
                        if n == 2:
                            sp.wait_ge(s_xn, KD * m + KD)
                            sp.dma_start(rope_sb[:, :, :], rope.rearrange("a p t -> p a t")).then_inc(s_rope[l], 16)
                        if n == 4:
                            sp.dma_start(dft_sb[:, :, :, :], dft.rearrange("a (t p) q -> p a t q", p=P)
                                         ).then_inc(s_dft[l], 16)
                        if AQ_T <= n < AK_T:
                            sp.wait_ge(s_w[n % 2], j0 + n // 2)
                            for v in range(KV_HEADS):
                                c0 = AQ_COL + (v * GROUP + n - AQ_T) * HD
                                src = w_in[l][:, c0:c0 + HD].rearrange("(k p) n -> p k n", p=P)
                                sp.dma_start(raw[:, n % 2, 0:KD, v * HD:(v + 1) * HD], src
                                             ).then_inc(s_raw[n % 2], 16)
                        else:
                            c0 = n * P
                            src = w_in[l][:, c0:c0 + P].rearrange("(k p) n -> p k n", p=P)
                            load_unit(i, n % 2, n // 2, src, j0 + n // 2)
                else:
                    with sp.Fori(0, units // 2) as j:
                        for s in range(2):
                            cols = ds(j * (2 * P) + s * P, P)
                            src = [w_o[l][0:512, cols].rearrange("(k p) n -> p k n", p=P)] + [
                                w_o[l][512 + 256 * v:768 + 256 * v, cols].rearrange("(t q) n -> q t n", q=HD)
                                for v in range(KV_HEADS)]
                            load_unit(i, s, j, src, j + j0)
            for s in range(2):
                sp.wait_ge(s_free[s], h_value(NS, KD - 2))
            sp.dma_start(wfin[:, :], final_norm_w.partition_broadcast(P)).then_inc(s_wf, 16)
            for tt in range(SEQ // P):
                sp.wait_ge(s_fo, tt + 1)
                sp.dma_start(out[0, tt * P:(tt + 1) * P, :], osb[:, tt % 2]).then_inc(s_out[tt % 2], 16)
            for b in range(2):
                sp.wait_ge(s_out[b], 16 * (SEQ // P // 2))

        @blk.gpsimd
        def _(pool):
            nc.gpsimd.memset(cond[:, :, :], 0.0).then_inc(s_ones, 1)
            nc.gpsimd.memset(eps[:, :], EPS).then_inc(s_ones, 1)
            nc.gpsimd.memset(ones[:, :], 1.0).then_inc(s_ones, 1)

        @blk.tensor
        def _(pe):
            def split_product(s, kt, i, hi, lo, t, before):
                parts = [(0, SEQ)] + ([(SEQ, TOK)] if t == TOK else [])
                last = None
                for k in range(kt):
                    if before is not None:
                        before(k)
                    for n, (w, v) in enumerate(((whi, hi), (whi, lo), (wlo, hi))):
                        for p0, p1 in parts:
                            last = nc.tensor.matmul(pg[s][:, p0:p1], w[:, s, k], v[:, k, p0:p1],
                                                    start=(k == 0 and n == 0), stop=(k == kt - 1 and n == 2))
                last.then_inc(s_unit[s], 1)

            def unit(i, s, j, hi, lo, t, before=None):
                pe.wait_ge(s_w[s], j + (pair0(i) + 1))
                pe.wait_ge(s_free[s], read_value(i, j - 1))
                split_product(s, phases[i][5], i, hi, lo, t, before)

            def ada_product(t, i):
                for b in range(2):
                    pe.wait_ge(s_ada[b], i * 16 + (8 * (t - ADA_FIRST) + 16))
                    for j in range(4):
                        last = nc.tensor.matmul(pa[0][32 * j:32 * j + 32, 0:2 * P], cond[:, 4 * b + j], ada[:, b, j],
                                                start=(b == 0), stop=(b == 1))
                    last.then_inc(s_ada_used, 1)

            def ada_fold(t, i):
                pe.wait_ge(s_part, i + ((t - ADA_FIRST) // 2 + 1))
                pe.wait_ge(s_mod, i + t // 2)
                for b in range(2):
                    last = nc.tensor.matmul(pa[1][:, 2 * b:2 * b + 2], part[:, b * P:(b + 1) * P], fold,
                                            start=True, stop=True)
                last.then_inc(s_fold, 1)

            pe.wait_ge(s_rows, 16 * 6)
            pe.wait_ge(s_const, 16)
            for r, n in enumerate((MT, MT, 68)):
                last = nc.tensor.transpose(pn[:, r * P:r * P + n], rows[0:n, r, :], ident[0:n, 0:n])
            last.then_inc(s_rowsT, 1)
            for tt in range(TOK // P):
                pe.wait_ge(s_x, 16 * (TOK // P))
                if tt >= 2:
                    pe.wait_ge(s_xTr[tt % 2], tt // 2)
                for k in range(KD):
                    last = nc.tensor.transpose(pg[tt % 2][:, k * P:(k + 1) * P], xtok[:, tt, k * P:(k + 1) * P],
                                               ident)
                last.then_inc(s_xT, 1)
            pe.wait_ge(s_cond, 1)
            first_banks = [p67[:, 0:512], p67[:, 512:1024], pn[:, 0:512], pn[:, 512:1024]]
            for q in range(4):
                pe.wait_ge(s_ada0[q], 16)
                for k in range(KD):
                    j = k % 4
                    last = nc.tensor.matmul(first_banks[q][32 * j:32 * j + 32, :], cond[:, k],
                                            ada_first[:, k, q * 512:(q + 1) * 512], start=(k < 4), stop=(k >= 4))
                last.then_inc(s_ada_first, 1)
            for b in range(2):
                pe.wait_ge(s_part0[b], 2)
            for t in range(ADA_FIRST):
                last = nc.tensor.matmul(pa[1][:, 2 * t:2 * t + 2], part_first[:, t * P:(t + 1) * P], fold,
                                        start=True, stop=True)
            last.then_inc(s_fold0, 1)
            pe.wait_ge(s_ones, 3)

            def norm(m):
                t = norm_tokens(m)
                pe.wait_ge(s_acc, (KD + 2) * m + 2 + KD)
                for p0, p1 in [(0, SEQ)] + ([(SEQ, TOK)] if t == TOK else []):
                    last = nc.tensor.matmul(pn[:, p0:p1], ones[:, :], rstd[:, p0:p1], start=True, stop=True)
                last.then_inc(s_ss, 1)

            def mix(i, l):
                nt = TOK // P if l < DEPTH - 1 else SEQ // P
                tq = nt * P
                for s in range(2):
                    pe.wait_ge(s_free[s], read_value(i, WIN_TILES // 2 - 1))
                pe.wait_ge(s_zr[l], len(ROPE_TILES))
                for tt in range(nt):
                    if tt >= 2:
                        pe.wait_ge(s_pq[l], tt - 1)
                    for ft in range(2):
                        last = nc.tensor.matmul(pa[tt % 2][:, ft * 256:ft * 256 + 256],
                                                z[:, F_T + ft, tt * P:(tt + 1) * P], cs64, start=True, stop=True)
                    last.then_inc(s_f1[l], 1)
                pe.wait_ge(s_pq[l], nt)
                pe.wait_ge(s_dft[l], 16)
                for ft in range(2):
                    dst = (pn, pg[0])[ft]
                    for tt in range(nt):
                        for cs in range(2):
                            w = pq[:, tt, ft * 256 + cs * P:ft * 256 + cs * P + P]
                            if tt < SEQ // P:
                                last = nc.tensor.matmul(dst[:, 0:SEQ], w, dft_sb[:, cs, tt],
                                                        start=(tt == 0 and cs == 0), stop=(tt == 3 and cs == 1))
                            else:
                                last = nc.tensor.matmul(dst[:, SEQ:TOK], w, dft_sb[:, cs, tt - 4, 0:SEQ:2],
                                                        start=(tt == 4 and cs == 0), stop=(tt == 5 and cs == 1))
                    last.then_inc(s_f2[l], 1)
                for tt in range(ret_blocks):
                    if tt >= 2:
                        pe.wait_ge(s_v[l], tt - 1)
                    for v in range(2):
                        last = nc.tensor.matmul(pa[tt % 2][:, v * P:(v + 1) * P],
                                                z[:, RV_T + v, tt * P:(tt + 1) * P], center, start=True, stop=True)
                    last.then_inc(s_vt[l], 1)
                pe.wait_ge(s_v[l], ret_blocks)
                pe.wait_ge(s_y[l], 2)
                spare = [pg[1], pn]
                steps = [(hd, jt) for hd in range(RH) for jt in range(ret_blocks)]

                def scores(r):
                    hd, jt = steps[r]
                    p0 = HD * (hd % 2)
                    if r >= 2:
                        pe.wait_ge(s_sd[l], r - 1)
                    kT = z[p0:p0 + HD, RK_T + hd // 2, jt * P:(jt + 1) * P]
                    q = z[p0:p0 + HD, RQ_T + hd // 2]
                    last = nc.tensor.matmul(spare[r % 2][:, 0:SEQ], kT, q[:, 0:SEQ], start=True, stop=True)
                    if jt >= SEQ // P and tq == TOK:
                        last = nc.tensor.matmul(spare[r % 2][:, SEQ:TOK], kT, q[:, SEQ:TOK], start=True, stop=True)
                    last.then_inc(s_s[l], 1)

                def values(r):
                    hd, jt = steps[r]
                    p0 = HD * (hd % 2)
                    pe.wait_ge(s_sd[l], r + 1)
                    o = (pg[0], p67)[hd // 2]
                    w = vret[:, jt, hd * HD:(hd + 1) * HD]
                    last = nc.tensor.matmul(o[p0:p0 + HD, 0:SEQ], w, sdec[:, r % 2, 0:SEQ],
                                            start=(jt == 0), stop=(jt == ret_blocks - 1))
                    if jt >= SEQ // P and tq == TOK:
                        last = nc.tensor.matmul(o[p0:p0 + HD, SEQ:TOK], w, sdec[:, r % 2, SEQ:TOK],
                                                start=(jt == SEQ // P), stop=(jt == ret_blocks - 1))
                    last.then_inc(s_pv[l], 1)

                scores(0)
                for r in range(len(steps)):
                    if r + 1 < len(steps):
                        scores(r + 1)
                    values(r)
                for p in range(2):
                    pe.wait_ge(s_osq[l], p + 1)
                    for p0, p1 in [(0, SEQ)] + ([(SEQ, TOK)] if tq == TOK else []):
                        last = nc.tensor.matmul(spare[p][:, p0:p1], block, osq[:, p, p0:p1], start=True, stop=True)
                    last.then_inc(s_var[l], 1)
                pe.wait_ge(s_y[l], 4)
                for tt in range(TOK // P):
                    last = nc.tensor.transpose(p67[:, tt * P:(tt + 1) * P], z[:, AV_T, tt * P:(tt + 1) * P], ident)
                last.then_inc(s_va[l], 1)
                units = att_units(l)

                def att_scores(q):
                    n, t, s = units[q]
                    lo, nk = local_keys(n)
                    p0 = HD * s
                    if q >= 2:
                        pe.wait_ge(s_p[l], q - 1)
                    w = z[p0:p0 + HD, AQ_T + t, n * P:(n + 1) * P]
                    kT = z[p0:p0 + HD, AK_T]
                    if nk:
                        c0 = SEQ - nk * P
                        left, right = n > 0, n < SEQ // P - 1
                        nc.tensor.matmul(pg[q % 2][:, c0:SEQ], w, kT[:, lo * P:(lo + nk) * P], start=True, stop=False,
                                         skip_group_check=True)
                        if left:
                            nc.tensor.matmul(pg[q % 2][:, c0:c0 + P], ident, masks[0], start=False,
                                             stop=not right, skip_group_check=True)
                        if right:
                            nc.tensor.matmul(pg[q % 2][:, SEQ - P:SEQ], ident, masks[1], start=False, stop=True,
                                             skip_group_check=True)
                    nc.tensor.matmul(pg[q % 2][:, SEQ:TOK], w, kT[:, SEQ:TOK], start=True, stop=True
                                     ).then_inc(s_as[l], 1)

                def att_transpose(q):
                    n, t, s = units[q]
                    nk, nb = local_keys(n)[1], max(local_keys(n)[1], 1)
                    pe.wait_ge(s_p[l], q + 1)
                    if q >= 1:
                        pe.wait_ge(s_ptc[l], q)
                        pe.wait_ge(s_ptl[l], q)
                    for j in range(nk + 2):
                        dst = j * P if j < nb else 512 + (j - nb) * P
                        last = nc.tensor.transpose(pn[:, dst:dst + P], prob[:, q % 2, j * P:(j + 1) * P], ident)
                    last.then_inc(s_pt[l], 1)

                def att_values(q):
                    n, t, s = units[q]
                    lo, nk = local_keys(n)
                    pe.wait_ge(s_ptc[l], q + 1)
                    pe.wait_ge(s_ptl[l], q + 1)
                    if s == 0 and q >= 2:
                        pe.wait_ge(s_o[l], q // 2)
                    tiles = [lo + j for j in range(nk)] + [4, 5]
                    for j, kt in enumerate(tiles):
                        last = nc.tensor.matmul(pa[0][:, s * HD:(s + 1) * HD], probT[:, q % 2, j * P:(j + 1) * P],
                                                vatt[:, kt, s * HD:(s + 1) * HD],
                                                start=(j == 0), stop=(j == len(tiles) - 1))
                    last.then_inc(s_av[l], 1)

                def att_out(pr):
                    pe.wait_ge(s_o[l], pr + 1)
                    if pr:
                        pe.wait_ge(s_y[l], 4 + pr)
                    nc.tensor.transpose(pa[1][:, 0:P], otok[:, pr % 2], ident).then_inc(s_oT[l], 1)

                att_scores(0)
                pe.wait_ge(s_var2[l], 1)
                for q in range(len(units) + 3):
                    if q + 1 < len(units):
                        att_scores(q + 1)
                    if 1 <= q <= len(units):
                        att_values(q - 1)
                    if q >= 3 and q % 2:
                        att_out((q - 3) // 2)
                    if q < len(units):
                        att_transpose(q)

            for i, (kind, l, m, hf, units, kt) in enumerate(phases):
                t = tokens(i)
                if kind == "in":
                    if hf == 0:
                        norm(m)
                    for a, e, b, _ in ada_runs(i, units // 2):
                        with pe.Fori(a, e) as f:
                            unit(i, 0, f, xhi, xlo, t, lambda k: pe.wait_ge(s_xn, KD * m + k + 1))
                            if b is not None:
                                ada_product(b, f)
                            unit(i, 1, f, xhi, xlo, t)
                            if b is not None:
                                ada_fold(b, f)
                elif kind == "out":
                    for a, e, b, _ in ada_runs(i, units // 2):
                        with pe.Fori(a, e) as j:
                            unit(i, 0, j, ahi, alo, t, lambda k: pe.wait_ge(s_a[m, hf], k + 1))
                            if b is not None:
                                ada_product(b, j)
                            unit(i, 1, j, ahi, alo, t)
                            if b is not None:
                                ada_fold(b, j)
                elif kind == "win":
                    norm(m)
                    runs, n = [], 0
                    while n < WIN_TILES:
                        e = n
                        while e < WIN_TILES and win_tokens(l, e) == win_tokens(l, n):
                            e += 2
                        runs.append((n // 2, e // 2, win_tokens(l, n)))
                        n = e
                    for b, e, tw in runs:
                        with pe.Fori(b, e) as j:
                            unit(i, 0, j, xhi, xlo, tw, lambda k: pe.wait_ge(s_xn, KD * m + k + 1))
                            unit(i, 1, j, xhi, xlo, tw)
                    mix(i, l)
                else:
                    pe.wait_ge(s_y[l], y_count(l))
                    with pe.Fori(0, units // 2) as j:
                        unit(i, 0, j, xhi, xlo, t)
                        unit(i, 1, j, xhi, xlo, t)
            for s in range(2):
                pe.wait_ge(s_free[s], h_value(NS, KD - 2))
            for tt in range(SEQ // P):
                if tt >= 2:
                    pe.wait_ge(s_fo, tt - 1)
                for k in range(KD):
                    last = nc.tensor.transpose(pg[tt % 2][:, k * P:(k + 1) * P], h[:, k, tt * P:(tt + 1) * P], ident)
                last.then_inc(s_fT, 1)

        @blk.scalar
        def _(act):
            chain = [0]

            def link(ins):
                chain[0] += 1
                ins.then_inc(s_ac, 1)
                act.wait_ge(s_ac, chain[0])

            def split_hi(i, s, j, after=None):
                act.wait_ge(s_raw[s], raw_value(i, j))
                if i or not isinstance(j, int) or j:
                    act.wait_ge(s_unit[s], j + pair0(i))
                nk = phases[i][5]
                nc.scalar.copy(whi[:, s, 0:nk], raw[:, s, 0:nk]).then_inc(s_whi[s], 1)

            def square(m, k, s, value):
                t = norm_tokens(m)
                col = slice(k, k + 1) if isinstance(k, int) else ds(k, 1)
                act.wait_ge(s_free[s], value)
                act.wait_ge(s_acc, (KD + 2) * m + k + 1)
                nc.scalar.activation(xfull[:, s, 0:t], h[:, col, 0:t].rearrange("p o t -> p (o t)"), ACT.Square
                                     ).then_inc(s_sq, 1)

            def copy_part(t, i):
                act.wait_ge(s_ada_used, i * 2 + (t - ADA_FIRST + 2))
                nc.scalar.copy(part[:, :], pa[0][:, 0:2 * P]).then_inc(s_part, 1)

            act.wait_ge(s_cols, 1)
            act.wait_ge(s_ones, 3)
            nc.scalar.activation(cond[:, :, 0:2], vecs[:, 48:64].rearrange("p (v k) -> p k v", v=2), ACT.Silu
                                 ).then_inc(s_cond, 1)
            for tt in range(0, TOK // P, 2):
                act.wait_ge(s_xT, tt + 1)
                nc.scalar.copy(h[:, :, tt * P:(tt + 1) * P], pg[0][:, :].rearrange("p (k t) -> p k t", k=KD)
                               ).then_inc(s_xTr[0] if tt < 4 else s_free[0], 1)
            split_hi(0, 0, 0)
            split_hi(0, 1, 0)
            act.wait_ge(s_free[1], 1)
            for k in range(KD):
                square(0, k, k % 2, 1)
            for q in (0, 2):
                act.wait_ge(s_ada_first, q + 1)
                nc.scalar.copy(part_first[:, q * 512:(q + 1) * 512], (p67, pn)[q // 2][:, 0:512]
                               ).then_inc(s_part0[0], 1)
            act.wait_ge(s_lgd, 1)
            link(nc.scalar.activation(lgt[:, 1], lgt[:, 0], ACT.Exp, scale=-1.0))
            nc.scalar.activation(lgt[:, 2], lgt[:, 1], ACT.Ln, bias=1.0).then_inc(s_lg, 1)

            def norm(m):
                t = norm_tokens(m)
                act.wait_ge(s_ss, m + 1)
                link(nc.scalar.activation(rstd[:, 0:t], pn[:, 0:t], ACT.Ln, bias=eps[:, :], scale=1.0 / D))
                nc.scalar.activation(rstd[:, 0:t], rstd[:, 0:t], ACT.Exp, scale=-0.5).then_inc(s_r, 1)
                act.wait_ge(s_coef, m + 1)
                shift = m // 3 * MT + m % 3 * 3 * KD
                for k in range(KD):
                    act.wait_ge(s_t, KD * m + k + 1)
                    if k >= 2:
                        act.wait_ge(s_xn, KD * m + k - 1)
                    for v, (p0, p1) in enumerate([(0, SEQ)] + ([(SEQ, TOK)] if t == TOK else [])):
                        for dst in (xfull[:, k % 2, p0:p1], xhi[:, k, p0:p1]):
                            last = nc.scalar.activation(dst, tnorm[:, k % 2, p0:p1], ACT.Identity,
                                                        bias=mod[:, shift + k, v:v + 1], scale=acol[:, k, v:v + 1])
                    last.then_inc(s_xf, 1)

            def mix(i, l):
                nt = TOK // P if l < DEPTH - 1 else SEQ // P
                tq = nt * P
                for tt in range(nt):
                    act.wait_ge(s_f1[l], tt + 1)
                    length = SEQ if tt < SEQ // P else CTX
                    nc.scalar.mul(pq[:, tt], pa[tt % 2], float((length * HD) ** -0.5)).then_inc(s_pq[l], 1)
                for ft in range(2):
                    act.wait_ge(s_f2[l], ft + 1)
                    nc.scalar.copy(xhi[:, ft, 0:tq], (pn, pg[0])[ft][:, 0:tq]).then_inc(s_yhi[l], 1)

                def strip(hd):
                    b = l * 2 * RH + hd
                    s = hd % 2
                    act.wait_ge(s_st[l], hd + 1)
                    if hd >= 2:
                        act.wait_ge(s_sd[l], ret_blocks * (hd - 1))
                        act.wait_ge(s_sr[l], hd)
                    elif hd == 1:
                        act.wait_ge(s_sr[l], hd)
                    nc.scalar.activation(strips[:, s, 0:U_D], strips[:, s, 0:U_D], ACT.Exp)
                    nc.scalar.activation(strips[:, s, U_D:], dist_sb[:, 256:U_D], ACT.Exp,
                                         bias=lgb[:, 0, b:b + 1], scale=lg[:, b:b + 1])
                    nc.scalar.activation(strip_b[:, :], dist_sb[:, 256:U_D], ACT.Exp,
                                         bias=lgb[:, 1, b + RH:b + RH + 1], scale=nlg[:, b + RH:b + RH + 1]
                                         ).then_inc(s_se[l], 1)

                for hd in range(RH):
                    strip(hd)
                for p in range(2):
                    act.wait_ge(s_pv[l], 2 * ret_blocks * (p + 1))
                    nc.scalar.activation(osq[:, p, 0:tq], (pg[0], p67)[p][:, 0:tq], ACT.Square).then_inc(s_osq[l], 1)
                for p in range(2):
                    act.wait_ge(s_var[l], p + 1)
                    link(nc.scalar.activation(osq[:, p, 0:tq], (pg[1], pn)[p][:, 0:tq], ACT.Ln, bias=eps[:, :]))
                    nc.scalar.activation(osq[:, p, 0:tq], osq[:, p, 0:tq], ACT.Exp, scale=-0.5).then_inc(s_rr[l], 1)
                units = att_units(l)
                for q in range(len(units) + 4):
                    if q < len(units):
                        n, t, s = units[q]
                        hd = l * AH + t + GROUP * s
                        w = (local_keys(n)[1] + 2) * P
                        act.wait_ge(s_nm[l], q + 1)
                        if q >= 2:
                            act.wait_ge(s_pt[l], q - 1)
                            act.wait_ge(s_den[l], q - 1)
                        nc.scalar.activation(esink[:, q % 2:q % 2 + 1], sink[:, hd:hd + 1], ACT.Exp,
                                             bias=negm[:, q % 2:q % 2 + 1])
                        nc.scalar.activation(prob[:, q % 2, 0:w], pg[q % 2][:, TOK - w:TOK], ACT.Exp,
                                             bias=negm[:, q % 2:q % 2 + 1], accum_out=den[:, q % 2:q % 2 + 1]
                                             ).then_inc(s_p[l], 1)
                    if 1 <= q <= len(units):
                        nk = local_keys(units[q - 1][0])[1]
                        nb = max(nk, 1)
                        act.wait_ge(s_pt[l], q)
                        if q >= 3:
                            act.wait_ge(s_av[l], q - 2)
                        nc.scalar.copy(probT[:, (q - 1) % 2, nb * P:(nk + 2) * P], pn[:, 512:512 + (nk + 2 - nb) * P]
                                       ).then_inc(s_ptc[l], 1)
                    if q >= 4 and q % 2 == 0:
                        pr = (q - 4) // 2
                        n, t, _ = units[2 * pr]
                        act.wait_ge(s_oT[l], pr + 1)
                        nc.scalar.copy(xhi[:, 4 + t, n * P:(n + 1) * P], pa[1][:, 0:P]).then_inc(s_yhi[l], 1)

            for i, (kind, l, m, hf, units, kt) in enumerate(phases):
                t = tokens(i)
                j0 = pair0(i)
                more = i + 1 < len(phases)
                if kind in ("in", "win") and hf == 0:
                    norm(m)
                if kind == "in":
                    def step(f, nxt, jn, b):
                        act.wait_ge(s_unit[0], f + (j0 + 1))
                        if hf or not isinstance(f, int) or f:
                            if isinstance(f, int) and f == 0:
                                act.wait_ge(s_a[m, 0], HALF)
                            else:
                                act.wait_ge(s_a[m, hf], f)
                        nc.scalar.activation(gate[:, 0:t], pg[0][:, 0:t], ACT.Silu).then_inc(s_free[0], 1)
                        split_hi(nxt, 0, jn)
                        if b is not None:
                            copy_part(b, f)
                        split_hi(nxt, 1, jn)

                    for a, e, b, _ in ada_runs(i, HALF):
                        if a == 0:
                            step(0, i, 1, b)
                            a = 1
                        with act.Fori(a, e if e < HALF else HALF - 1) as f:
                            step(f, i, f + 1, b)
                    step(HALF - 1, i + 1, 0, b)
                elif kind in ("out", "wo"):
                    def step(j, nxt, jn, b):
                        for s in range(2):
                            if nxt < len(phases):
                                split_hi(nxt, s, jn)
                            if b is not None and s == 0:
                                copy_part(b, j)
                            if next_norm(i) is not None:
                                square(next_norm(i), j * 2 + s, s, read_value(i, j))

                    for a, e, b, _ in ada_runs(i, units // 2 - 1):
                        with act.Fori(a, e) as j:
                            step(j, i, j + 1, b)
                    step(units // 2 - 1, i + 1, 0, None)
                else:
                    for n in range(WIN_TILES):
                        s, tw = n % 2, win_tokens(l, n)
                        act.wait_ge(s_unit[s], j0 + n // 2 + 1)
                        if RG_T <= n < AQ_T:
                            nc.scalar.activation(z[:, n, 0:tw], pg[s][:, 0:tw], ACT.Silu).then_inc(s_free[s], 1)
                        else:
                            scaled = RK_T <= n < RV_T or AQ_T <= n < AK_T
                            nc.scalar.mul(z[:, n, 0:tw], pg[s][:, 0:tw], HD ** -0.5 if scaled else 1.0
                                          ).then_inc(s_free[s], 1)
                        nxt, jn = (i, n // 2 + 1) if n + 2 < WIN_TILES else (i + 1, 0)
                        split_hi(nxt, s, jn)
                    mix(i, l)
            for tt in range(SEQ // P):
                act.wait_ge(s_fT, tt + 1)
                if tt >= 2:
                    act.wait_ge(s_fo, tt - 1)
                b = slice(tt % 2, tt % 2 + 1)
                link(nc.scalar.activation(junk[:, :], pg[tt % 2][:, :], ACT.Square, accum_out=fstat[:, b]))
                link(nc.scalar.activation(fstat[:, b], fstat[:, b], ACT.Ln, bias=eps[:, :], scale=1.0 / D))
                nc.scalar.activation(fstat[:, b], fstat[:, b], ACT.Exp, scale=-0.5).then_inc(s_fs, 1)

        @blk.vector
        def _(dve):
            chain = [0]

            def link(ins):
                chain[0] += 1
                ins.then_inc(s_dv, 1)
                dve.wait_ge(s_dv, chain[0])

            def split_lo(i, s, j):
                dve.wait_ge(s_whi[s], j + (pair0(i) + 1))
                nk = phases[i][5]
                nc.vector.tensor_sub(wlo[:, s, 0:nk], raw[:, s, 0:nk], whi[:, s, 0:nk].bitcast(f32)
                                     ).then_inc(s_w[s], 1)

            def clear_squares(m):
                nc.vector.memset(rstd[:, 0:norm_tokens(m)], 0.0).then_inc(s_acc, 2)

            def sum_squares(m, k, s):
                t = norm_tokens(m)
                dve.wait_ge(s_sq, KD * m + k + 1)
                dve.wait_ge(s_acc, (KD + 2) * m + k + 2)
                nc.vector.tensor_tensor(rstd[:, 0:t], rstd[:, 0:t], xfull[:, s, 0:t], ALU.add).then_inc(s_acc, 1)

            dve.wait_ge(s_rowsT, 1)
            nc.vector.tensor_copy(bias[:, 0:MT], pn[:, 0:MT])
            nc.vector.tensor_copy(bias[:, MT:2 * MT], pn[:, P:P + MT])
            nc.vector.tensor_copy(vecs[:, 0:68], pn[:, 2 * P:2 * P + 68]).then_inc(s_cols, 1)
            dve.wait_ge(s_cols, 1)
            for tt in range(1, TOK // P, 2):
                dve.wait_ge(s_xT, tt + 1)
                nc.vector.tensor_copy(h[:, :, tt * P:(tt + 1) * P], pg[1][:, :].rearrange("p (k t) -> p k t", k=KD)
                                      ).then_inc(s_xTr[1] if tt < 4 else s_free[1], 1)
            split_lo(0, 0, 0)
            split_lo(0, 1, 0)
            clear_squares(0)
            for k in range(KD):
                sum_squares(0, k, k % 2)
            for q in (1, 3):
                dve.wait_ge(s_ada_first, q + 1)
                nc.vector.tensor_copy(part_first[:, q * 512:(q + 1) * 512], (p67, pn)[q // 2][:, 512:1024]
                                      ).then_inc(s_part0[1], 1)
            dve.wait_ge(s_vec, 16 * 3)
            link(nc.vector.tensor_scalar(lgt[:, 1], lg[:, :], -1.0, None, ALU.mult))
            nc.vector.tensor_tensor(lgt[:, 0], lg[:, :], lgt[:, 1], ALU.max).then_inc(s_lgd, 1)
            dve.wait_ge(s_lg, 1)
            dve.wait_ge(s_lgd, 1)
            link(nc.vector.tensor_scalar(lgt[:, 0], lgt[:, 1], 1.0, -1.0, ALU.add, ALU.add))
            link(nc.vector.tensor_scalar(nlg[:, :], lgt[:, 0], 0.0, None, ALU.is_equal))
            link(nc.vector.tensor_tensor(lgt[:, 0], lgt[:, 0], nlg[:, :], ALU.add))
            link(nc.vector.tensor_tensor(lgt[:, 2], lgt[:, 2], nlg[:, :], ALU.add))
            link(nc.vector.reciprocal(lgt[:, 0], lgt[:, 0]))
            link(nc.vector.tensor_tensor(lgt[:, 2], lgt[:, 2], lgt[:, 0], ALU.mult))
            link(nc.vector.tensor_tensor(lgt[:, 2], lgt[:, 2], lgt[:, 1], ALU.mult))
            link(nc.vector.scalar_tensor_tensor(lg[:, :], lg[:, :], 0.0, lgt[:, 2], ALU.min, ALU.subtract))
            link(nc.vector.tensor_scalar(nlg[:, :], lg[:, :], -1.0, None, ALU.mult))
            link(nc.vector.tensor_scalar(lgb[:, 0], lg[:, :], float(CTX), None, ALU.mult))
            link(nc.vector.tensor_scalar(lgb[:, 1], lg[:, :], float(SEQ), None, ALU.mult))

            def read_mod(t, i):
                dve.wait_ge(s_fold, i + ((t - ADA_FIRST) // 2 + 1))
                nc.vector.tensor_tensor(mod[:, ds(i * 2 + t, 2)], pa[1][:, 0:4].rearrange("p (t v) -> p t v", v=2),
                                        bias[:, ds(i * 2 + t, 2)].unsqueeze(2).broadcast_to([P, 2, 2]), ALU.add
                                        ).then_inc(s_mod, 1)

            def coefficients(m):
                b = m // 3 * MT + (m % 3 * 3 + 1) * KD
                dve.wait_ge(s_mod, (b + KD) // 2)
                nc.vector.scalar_tensor_tensor(acol[:, :, :], mod[:, b:b + KD], 1.0,
                                               vecs[:, m * KD:(m + 1) * KD].unsqueeze(2).broadcast_to([P, KD, 2]),
                                               ALU.add, ALU.mult).then_inc(s_coef, 1)

            def gates(m):
                b = m // 3 * MT + (m % 3 * 3 + 2) * KD
                dve.wait_ge(s_mod, (b + KD) // 2)
                link(nc.vector.tensor_scalar(gcol[:, :, :], mod[:, b:b + KD], 1.0 if m % 3 == 1 else 0.5, None,
                                             ALU.mult))

            def norm(m):
                t = norm_tokens(m)
                dve.wait_ge(s_r, m + 1)

                def low(k):
                    dve.wait_ge(s_xf, KD * m + k + 1)
                    nc.vector.tensor_sub(xlo[:, k, 0:t], xfull[:, k % 2, 0:t], xhi[:, k, 0:t].bitcast(f32)
                                         ).then_inc(s_xn, 1)

                for k in range(KD):
                    nc.vector.tensor_tensor(tnorm[:, k % 2, 0:t], h[:, k, 0:t], rstd[:, 0:t], ALU.mult
                                            ).then_inc(s_t, 1)
                    if k:
                        low(k - 1)
                low(KD - 1)

            def add_branch(i, s, j, n):
                dve.wait_ge(s_unit[s], j + (pair0(i) + 1))
                t = tokens(i)
                col = slice(n, n + 1) if isinstance(n, int) else ds(n, 1)
                for v, (p0, p1) in enumerate([(0, SEQ)] + ([(SEQ, TOK)] if t == TOK else [])):
                    hv = h[:, col, p0:p1].rearrange("p o t -> p (o t)")
                    last = nc.vector.scalar_tensor_tensor(hv, pg[s][:, p0:p1], gcol[:, col, v:v + 1].rearrange(
                        "p o v -> p (o v)"), hv, ALU.mult, ALU.add)
                last.then_inc(s_free[s], 1)

            def y_low(l, k, src, p0, p1, hi_count):
                dve.wait_ge(s_yhi[l], hi_count)
                nc.vector.tensor_sub(xlo[:, k, p0:p1], src, xhi[:, k, p0:p1].bitcast(f32)).then_inc(s_y[l], 1)

            def mix(i, l):
                nt = TOK // P if l < DEPTH - 1 else SEQ // P
                tq = nt * P
                for ft in range(2):
                    y_low(l, ft, (pn, pg[0])[ft][:, 0:tq], 0, tq, ft + 1)
                for tt in range(ret_blocks):
                    dve.wait_ge(s_vt[l], tt + 1)
                    nc.vector.tensor_copy(vret[:, tt], pa[tt % 2][:, 0:256]).then_inc(s_v[l], 1)

                def strip_args(hd):
                    b = l * 2 * RH + hd
                    s = hd % 2
                    link(nc.vector.tensor_scalar(strips[:, s, 0:U_D], dist_sb[:, :], nlg[:, b + RH:b + RH + 1], None,
                                                 ALU.mult))
                    nc.vector.scalar_tensor_tensor(strips[:, s, 0:U_D], dist_sb[:, :], lg[:, b:b + 1],
                                                   strips[:, s, 0:U_D], ALU.mult, ALU.min).then_inc(s_st[l], 1)

                def strip_sum(hd):
                    s = hd % 2
                    dve.wait_ge(s_se[l], hd + 1)
                    nc.vector.tensor_tensor(strips[:, s, 384:512], strips[:, s, 384:512], ident, ALU.add)
                    nc.vector.tensor_tensor(strips[:, s, U_D:], strips[:, s, U_D:], strip_b[:, :], ALU.add
                                            ).then_inc(s_sr[l], 1)
                    dve.wait_ge(s_sr[l], hd + 1)

                strip_args(0)
                strip_sum(0)
                strip_args(1)
                for hd in range(RH):
                    s = hd % 2
                    for jt in range(ret_blocks):
                        r = hd * ret_blocks + jt
                        src = (pg[1], pn)[r % 2]
                        dve.wait_ge(s_s[l], r + 1)
                        if r >= 2:
                            dve.wait_ge(s_pv[l], r - 1)
                        if jt < SEQ // P:
                            g = strips[:, s, 384 - jt * P:384 - jt * P + SEQ]
                        else:
                            c0 = U_D + P * (1 - (jt - 4))
                            g = strips[:, s, c0:c0 + SEQ]
                            if tq == TOK:
                                g0 = 384 - (jt - 4) * P
                                nc.vector.tensor_tensor(sdec[:, r % 2, SEQ:TOK], src[:, SEQ:TOK],
                                                        strips[:, s, g0:g0 + CTX], ALU.mult)
                        nc.vector.tensor_tensor(sdec[:, r % 2, 0:SEQ], src[:, 0:SEQ], g, ALU.mult
                                                ).then_inc(s_sd[l], 1)
                        if jt == 1 and hd + 1 < RH:
                            strip_sum(hd + 1)
                    if hd + 2 < RH:
                        dve.wait_ge(s_sd[l], ret_blocks * (hd + 1))
                        strip_args(hd + 2)
                for p in range(2):
                    dve.wait_ge(s_rr[l], p + 1)
                    o = osq[:, p, 0:tq]
                    link(nc.vector.tensor_tensor(o, (pg[0], p67)[p][:, 0:tq], o, ALU.mult))
                    link(nc.vector.scalar_tensor_tensor(o, o, vecs[:, 64 + 2 * l + p:65 + 2 * l + p],
                                                        z[:, RG_T + p, 0:tq], ALU.mult, ALU.mult))
                    link(nc.vector.tensor_copy(xhi[:, 2 + p, 0:tq], o))
                    nc.vector.tensor_sub(xlo[:, 2 + p, 0:tq], o, xhi[:, 2 + p, 0:tq].bitcast(f32)).then_inc(s_y[l], 1)
                dve.wait_ge(s_va[l], 1)
                nc.vector.tensor_copy(vatt[:, :, :], p67[:, 0:TOK].rearrange("p (t n) -> p t n", n=P)
                                      ).then_inc(s_var2[l], 1)
                units = att_units(l)
                for q in range(len(units) + 4):
                    if q < len(units):
                        n, t, s = units[q]
                        hd = l * AH + t + GROUP * s
                        w = (local_keys(n)[1] + 2) * P
                        b = slice(q % 2, q % 2 + 1)
                        dve.wait_ge(s_as[l], q + 1)
                        link(nc.vector.reduce_max(mx[:, b], pg[q % 2][:, TOK - w:TOK], AX.X))
                        nc.vector.tensor_scalar(negm[:, b], mx[:, b], sink[:, hd:hd + 1], -1.0, ALU.max, ALU.mult
                                                ).then_inc(s_nm[l], 1)
                    if 1 <= q <= len(units):
                        n = units[q - 1][0]
                        nb = max(local_keys(n)[1], 1)
                        b = slice((q - 1) % 2, (q - 1) % 2 + 1)
                        dve.wait_ge(s_pt[l], q)
                        if q >= 3:
                            dve.wait_ge(s_av[l], q - 2)
                        nc.vector.tensor_copy(probT[:, (q - 1) % 2, 0:nb * P], pn[:, 0:nb * P]).then_inc(s_ptl[l], 1)
                        nc.vector.tensor_tensor(rden[:, b], den[:, b], esink[:, b], ALU.add).then_inc(s_den[l], 1)
                        dve.wait_ge(s_den[l], q)
                        link(nc.vector.reciprocal(rden[:, b], rden[:, b]))
                        if q % 2 == 0:
                            pr = q // 2 - 1
                            dve.wait_ge(s_av[l], q)
                            for s in range(2):
                                last = nc.vector.tensor_scalar(otok[:, pr % 2, s * HD:(s + 1) * HD],
                                                               pa[0][:, s * HD:(s + 1) * HD], rden[:, s:s + 1], None,
                                                               ALU.mult)
                            last.then_inc(s_o[l], 1)
                    if q >= 4 and q % 2 == 0:
                        pr = (q - 4) // 2
                        n, t, _ = units[2 * pr]
                        y_low(l, 4 + t, pa[1][:, 0:P], n * P, (n + 1) * P, 3 + pr)

            dve.wait_ge(s_fold0, 1)
            nc.vector.tensor_tensor(mod[:, 0:ADA_FIRST], pa[1][:, 0:2 * ADA_FIRST].rearrange("p (t v) -> p t v", v=2),
                                    bias[:, 0:ADA_FIRST].unsqueeze(2).broadcast_to([P, ADA_FIRST, 2]), ALU.add
                                    ).then_inc(s_mod, ADA_FIRST // 2)
            for i, (kind, l, m, hf, units, kt) in enumerate(phases):
                t = tokens(i)
                j0 = pair0(i)
                more = i + 1 < len(phases)
                if kind in ("in", "win") and hf == 0:
                    coefficients(m)
                    norm(m)
                if kind == "in":
                    def step(f, nxt, jn):
                        split_lo(nxt, 0, jn)
                        dve.wait_ge(s_unit[1], f + (j0 + 1))
                        dve.wait_ge(s_free[0], read_value(i, f))
                        col = slice(f, f + 1) if isinstance(f, int) else ds(f, 1)
                        hi = ahi[:, col, 0:t].rearrange("p o t -> p (o t)")
                        lo = alo[:, col, 0:t].rearrange("p o t -> p (o t)")
                        nc.vector.tensor_tensor(gate[:, 0:t], gate[:, 0:t], pg[1][:, 0:t], ALU.mult
                                                ).then_inc(s_free[1], 1)
                        dve.wait_ge(s_free[1], read_value(i, f))
                        nc.vector.tensor_copy(hi, gate[:, 0:t]).then_inc(s_ahi[m, hf], 1)
                        dve.wait_ge(s_ahi[m, hf], f + 1)
                        nc.vector.tensor_sub(lo, gate[:, 0:t], hi.bitcast(f32)).then_inc(s_a[m, hf], 1)
                        split_lo(nxt, 1, jn)

                    runs = ada_runs(i, HALF)
                    for a, e, b, _ in runs:
                        with dve.Fori(a, e if e < HALF else HALF - 1) as f:
                            step(f, i, f + 1)
                            if b is not None:
                                read_mod(b, f)
                    step(HALF - 1, i + 1, 0)
                    if runs[-1][2] is not None:
                        read_mod(runs[-1][2], HALF - 1)
                    if hf == 0:
                        gates(m)
                elif kind in ("out", "wo"):
                    nn = next_norm(i)
                    if nn is not None:
                        clear_squares(nn)
                    if kind == "wo":
                        gates(m)
                    for a, e, b, _ in ada_runs(i, units // 2 - 1):
                        with dve.Fori(a, e) as j:
                            for s in range(2):
                                add_branch(i, s, j, j * 2 + s)
                                split_lo(i, s, j + 1)
                                if nn is not None:
                                    sum_squares(nn, j * 2 + s, s)
                            if b is not None:
                                read_mod(b, j)
                    for s in range(2):
                        n = units - 2 + s
                        add_branch(i, s, units // 2 - 1, n)
                        if nn is not None and s:
                            sum_squares(nn, n, s)
                        if more:
                            split_lo(i + 1, s, 0)
                        if nn is not None and not s:
                            sum_squares(nn, n, s)
                else:
                    for n in range(WIN_TILES):
                        s = n % 2
                        if n in ROPE_TILES:
                            dve.wait_ge(s_free[s], read_value(i, n // 2))
                            if n == ROPE_TILES[0]:
                                dve.wait_ge(s_rope[l], 16)
                            else:
                                dve.wait_ge(s_zr[l], ROPE_TILES.index(n))
                            zn = z[:, n, 0:SEQ]
                            link(nc.vector.stream_shuffle(swapped[:, :], zn, [(a + 16) % 32 for a in range(32)]))
                            link(nc.vector.tensor_tensor(zn, zn, rope_sb[:, 0], ALU.mult))
                            link(nc.vector.tensor_tensor(swapped[:, :], swapped[:, :], rope_sb[:, 1], ALU.mult))
                            nc.vector.tensor_tensor(zn, zn, swapped[:, :], ALU.add).then_inc(s_zr[l], 1)
                        nxt, jn = (i, n // 2 + 1) if n + 2 < WIN_TILES else (i + 1, 0)
                        split_lo(nxt, s, jn)
                    mix(i, l)
            dve.wait_ge(s_wf, 16)
            for tt in range(SEQ // P):
                dve.wait_ge(s_fs, tt + 1)
                if tt >= 2:
                    dve.wait_ge(s_out[tt % 2], 16)
                nc.vector.scalar_tensor_tensor(osb[:, tt % 2], pg[tt % 2][:, :], fstat[:, tt % 2:tt % 2 + 1],
                                               wfin[:, :], ALU.mult, ALU.mult).then_inc(s_fo, 1)


INPUTS = ['x', 'c', 'ctx', 'c_ctx', 'norm_w', 'w_ada', 'b_ada', 'ffn_w_in', 'ffn_w_out', 'w_in', 'w_o',
          'ret_decay', 'ret_gn_w', 'attn_sink', 'final_norm_w']


def kernel(**inputs):
    import concourse.bacc as bacc
    from concourse.bass_utils import run_bass_kernel_spmd

    nc = bacc.Bacc("TRN2", target_bir_lowering=False, num_devices=1)
    arrays, args = {}, []
    tables = constants()
    for name in INPUTS + list(tables):
        a = np.ascontiguousarray(inputs[name] if name in inputs else tables[name])
        arrays[f"in_{name}"] = a
        args.append(nc.dram_tensor(f"in_{name}", a.shape, mybir.dt.from_np(a.dtype), kind="ExternalInput").ap())
    shape = (1, SEQ, D)
    args.append(nc.dram_tensor("out_h", shape, mybir.dt.float32, kind="ExternalOutput").ap())
    transformer(nc, *args)
    return run_bass_kernel_spmd(nc, [arrays], core_ids=[0]).results[0]["out_h"]
```

```python
import numpy as np

import concourse.bass as bass
from concourse import mybir
from contextlib import ExitStack

P = 128
D = 1024
KD = D // P
SEQ = 512
CTX = 256
TOK = SEQ + CTX
DEPTH = 2
DFF = 2816
HALF = DFF // P // 2
NMOD = 9
MT = NMOD * KD
HD = 64
RH = 4
AH = 8
EPS = 1e-6
NEG = -1e30
U_D = 896

WIN_TILES = 16
F_T, RQ_T, RK_T, RV_T, RG_T, AQ_T, AK_T, AV_T = 0, 2, 4, 6, 8, 10, 14, 15
ROPE_TILES = [2, 3, 4, 5, 10, 11, 12, 13, 14]
AQ_COL = 1280
KV_HEADS = 2
GROUP = AH // KV_HEADS

ADA_FIRST = 16
ADA_PAIRS = {(0, 0, 0): (16, 11, 1), (0, 0, 1): (40, 11, 1), (0, 1, 0): (64, 11, 1),
             (1, 0, 0): (88, 11, 3), (1, 0, 1): (116, 11, 3)}


def constants():
    a = np.arange(SEQ, dtype=np.float64)
    ang = 2 * np.pi * ((a[:, None] * a[None]) % SEQ) / SEQ
    dft = np.stack([np.cos(ang), np.sin(ang)])
    g = np.arange(HD, dtype=np.float64)
    ang = 2 * np.pi * ((g[:, None] * g[None]) % HD) / HD
    z = np.zeros((HD, HD))
    c64, s64 = np.cos(ang), -np.sin(ang)
    ident = np.eye(P)
    block = np.kron(np.eye(2), np.full((HD, HD), 1.0 / HD))
    q, k = np.arange(P)[:, None], np.arange(P)[None]
    small = np.concatenate([
        ident, block, ident - block,
        np.block([[c64, z], [z, c64]]), np.block([[s64, z], [z, s64]]),
        np.tile(np.eye(32)[:, :2], (4, 1))], axis=1)
    window = np.concatenate([np.where(k >= q, 0.0, NEG), np.where(k <= q, 0.0, NEG)], axis=1)
    dist = (np.arange(U_D)[None] - 384.0) - np.arange(P)[:, None]
    pairs = HD // 4
    inv = np.float32(10000.0) ** (-np.arange(pairs, dtype=np.float32) / np.float32(pairs))
    d = np.arange(P) % HD
    t = np.arange(SEQ)
    pos = np.where((d // 32)[:, None] == 0, t[None] // HD, t[None] % HD).astype(np.float32)
    angle = (pos * inv[d % pairs][:, None]).astype(np.float32).astype(np.float64)
    sign = np.where((d % 32) < pairs, -1.0, 1.0)[:, None]
    rope = np.stack([np.cos(angle), sign * np.sin(angle)])
    return {n: np.ascontiguousarray(v.astype(np.float32)) for n, v in
            dict(dft=dft, small=small, window=window, dist=dist, rope=rope).items()}


def transformer(nc, x, c, ctx_in, c_ctx, norm_w, w_ada, b_ada, ffn_w_in, ffn_w_out, w_in, w_o,
                ret_decay, ret_gn_w, attn_sink, final_norm_w, dft, small, window, dist, rope, out):
    f32, f32r = mybir.dt.float32, mybir.dt.float32r
    ALU = mybir.AluOpType
    ACT = mybir.ActivationFunctionType
    AX = mybir.AxisListType
    ds = bass.ds

    ctx = ExitStack()
    with ctx:
        def sem(name):
            return ctx.enter_context(nc.semaphore(name))

        sizes = dict(h=KD * TOK * 4, xhi=KD * TOK * 4, xlo=KD * TOK * 4, ahi=HALF * TOK * 4,
                     alo=HALF * TOK * 4, raw=2 * HALF * P * 4, whi=2 * HALF * P * 4,
                     wlo=2 * HALF * P * 4, ada=2 * KD * P * 4, m=5 * TOK * 4)
        total = sum(sizes.values())
        slab = ctx.enter_context(nc.sbuf_tensor("slab", [P, total // 4], f32))
        start = {}
        at = nc.sbuf_base - total
        for name, size in sizes.items():
            start[name] = at
            at += size
        a0, x0, m0 = start["ahi"], start["xhi"], start["m"]

        def place(name, shape, dt, offset):
            return nc.alloc_sbuf_tensor_at(name, shape, dt, offset=offset)

        def sb(name, shape, dt=f32):
            return ctx.enter_context(nc.sbuf_tensor(name, shape, dt))

        h = place("h", [P, KD, TOK], f32, start["h"])
        xhi = place("xhi", [P, KD, TOK], f32r, start["xhi"])
        xlo = place("xlo", [P, KD, TOK], f32r, start["xlo"])
        ahi = place("ahi", [P, HALF, TOK], f32r, start["ahi"])
        alo = place("alo", [P, HALF, TOK], f32r, start["alo"])
        raw = place("raw", [P, 2, HALF, P], f32, start["raw"])
        whi = place("whi", [P, 2, HALF, P], f32r, start["whi"])
        wlo = place("wlo", [P, 2, HALF, P], f32r, start["wlo"])
        ada = place("ada", [P, 2, KD // 2, 2 * P], f32, start["ada"])
        rstd = place("rstd", [P, TOK], f32, m0)
        tnorm = place("tnorm", [P, 2, TOK], f32, m0 + TOK * 4)
        xfull = place("xfull", [P, 2, TOK], f32, m0 + 3 * TOK * 4)
        gate = place("gate", [P, TOK], f32, m0 + TOK * 4)
        xtok = place("xtok", [P, TOK // P, D], f32, start["alo"])
        chunk_bytes = KD * 4 * P * 4
        ada_first = [place(f"ada_first{q}", [P, KD, 4 * P], f32, at) for q, at in enumerate(
            (x0, x0 + chunk_bytes, a0, a0 + chunk_bytes))]
        part_first = place("part_first", [P, ADA_FIRST * P], f32, start["alo"] + TOK // P * D * 4)
        rows = place("rows", [P, 3, P], f32, m0)
        window_sb = place("window_sb", [P, 2 * P], f32, m0 + TOK * 4)
        t0 = a0 + WIN_TILES * TOK * 4
        z = place("z", [P, WIN_TILES, TOK], f32, a0)
        dft_sb = place("dft_sb", [P, 2, SEQ // P, SEQ], f32, t0)
        rope_sb = place("rope_sb", [P, 2, SEQ], f32, m0)
        swapped = place("swapped", [P, SEQ], f32, m0 + 2 * SEQ * 4)
        pq = place("pq", [P, TOK // P, 4 * P], f32, m0)
        strips = [place(f"strips{hd}", [P, U_D + 640], f32, at) for hd, at in enumerate(
            (x0 + 2 * TOK * 4, start["xlo"] + 2 * TOK * 4, t0, t0 + (U_D + 640) * 4))]
        strip_b = place("strip_b", [P, 640], f32, x0 + 5 * TOK * 4)
        vret = place("vret", [P, TOK // P, 2 * P], f32, m0)
        sdec = place("sdec", [P, 2, TOK], f32, m0 + 2 * TOK * 4)
        y4 = [start["xlo"] + k * TOK * 4 for k in range(4, 8)] + [x0 + k * TOK * 4 for k in (6, 7)]
        rk_st = [place(f"rk_st{b}", [P, TOK], f32r, y4[3 * b]) for b in range(2)]
        rq_hi = [place(f"rq_hi{b}", [P, TOK], f32r, y4[3 * b + 1]) for b in range(2)]
        rq_lo = [place(f"rq_lo{b}", [P, TOK], f32r, y4[3 * b + 2]) for b in range(2)]
        osq = place("osq", [P, 2, TOK], f32, x0 + 4 * TOK * 4)
        zt = [a0 + k * TOK * 4 for k in range(WIN_TILES)]
        ak_hi = [place(f"ak_hi{v}", [P, TOK], f32r, (zt[1], zt[6])[v]) for v in range(KV_HEADS)]
        ak_lo = [place(f"ak_lo{v}", [P, TOK], f32r, (zt[7], m0 + 4 * TOK * 4)[v]) for v in range(KV_HEADS)]
        aq_st = [[place(f"aq_st{b}{v}", [P, TOK], f32r, ((start["ada"], start["ada"] + TOK * 4), (zt[4], zt[5]))[b][v])
                  for v in range(KV_HEADS)] for b in range(2)]
        vatt = place("vatt", [P, TOK // P, P], f32, zt[0])
        prob = place("prob", [P, 2, 640], f32, t0 + 3072)
        probT = place("probT", [P, 2, 640], f32, t0 + 3072 + 5120)
        otok = place("otok", [P, 2, P], f32, t0 + 3072 + 10240)
        wfin = place("wfin", [P, D], f32, x0)
        osb = place("osb", [P, 2, D], f32, x0 + D * 4)
        junk = place("junk", [P, D], f32, x0 + 3 * D * 4)

        consts = sb("consts", [P, 5 * P + 2])
        fold = consts[:, 5 * P:5 * P + 2]
        ident_r = sb("ident_r", [P, P], f32r)
        window_r = sb("window_r", [P, 2, P], f32r)
        part = sb("part", [P, 2 * P])
        ident = consts[:, 0:P]
        block = consts[:, P:2 * P]
        center = consts[:, 2 * P:3 * P]
        cs64 = consts[:, 3 * P:5 * P]
        ones = sb("ones", [P, P])
        dist_sb = sb("dist_sb", [P, U_D])
        eps = sb("eps", [P, 1])
        bias = sb("bias", [P, DEPTH * MT])
        vecs = sb("vecs", [P, 76])
        cond = sb("cond", [P, KD, 32])
        mod = sb("mod", [P, DEPTH * MT, 2])
        acol = sb("acol", [P, KD, 2])
        gcol = sb("gcol", [P, KD, 2])
        sink = sb("sink", [P, DEPTH * AH])
        lg = sb("lg", [P, DEPTH * 2 * RH])
        lgt = sb("lgt", [P, 3, DEPTH * 2 * RH])
        nlg = sb("nlg", [P, DEPTH * 2 * RH])
        lgb = sb("lgb", [P, 2, DEPTH * 2 * RH])
        mx = sb("mx", [P, 4])
        negm = sb("negm", [P, 4])
        esink = sb("esink", [P, 4])
        den = sb("den", [P, 4])
        rden = sb("rden", [P, 4])
        fstat = sb("fstat", [P, SEQ // P])

        pg = [ctx.enter_context(nc.psum_tensor(f"pg{i}", [P, 1024], f32)) for i in range(2)]
        pn = ctx.enter_context(nc.psum_tensor("pn", [P, 1024], f32))
        p67 = ctx.enter_context(nc.psum_tensor("p67", [P, 1024], f32))
        pa = [p67[:, 0:512], p67[:, 512:1024]]
        pfin = [pg[0], pg[1], pn, p67]

        s_raw = [sem(f"raw_loaded{s}") for s in range(2)]
        s_whi = [sem(f"whi_ready{s}") for s in range(2)]
        s_w = [sem(f"weights_ready{s}") for s in range(2)]
        s_unit = [sem(f"unit_done{s}") for s in range(2)]
        s_free = [sem(f"psum_read{s}") for s in range(2)]
        s_ada = [sem(f"ada_loaded{s}") for s in range(2)]
        s_ada0 = [sem(f"ada_first_loaded{q}") for q in range(4)]
        s_ada_first = sem("ada_first_done")
        s_part0 = [sem(f"part_first_copied{b}") for b in range(2)]
        s_fold0 = sem("ada_first_folded")
        s_part = sem("ada_part_copied")
        s_fold = sem("ada_folded")
        s_ada_used = sem("ada_used")
        s_mod = sem("mod_ready")
        s_rows = sem("rows_loaded")
        s_const = sem("consts_loaded")
        s_vec = sem("vectors_loaded")
        s_x = [sem(f"x_loaded{b}") for b in range(3)]
        s_ones = sem("ones_ready")
        s_rowsT = sem("rows_transposed")
        s_cols = sem("columns_ready")
        s_cond = sem("cond_ready")
        s_xT = sem("x_transposed")
        s_xTr = [sem(f"x_transposed_read{b}") for b in range(2)]
        s_lg = sem("decay_exp")
        s_lgd = sem("decay_ready")
        NS = 3 * DEPTH
        s_sq = sem("squares")
        s_acc = sem("squares_summed")
        s_early = sem("early_part_done")
        s_h0 = sem("early_part_added")
        s_ss = sem("sum_squares")
        s_r = sem("rstd_ready")
        s_t = sem("t_ready")
        s_xf = sem("xfull_ready")
        s_xn = sem("xn_ready")
        s_coef = sem("coef_ready")
        s_ahi = {(m, hf): sem(f"a_hi{m}_{hf}") for m in (0, 2, 3, 5) for hf in range(2)}
        s_a = {(m, hf): sem(f"a_ready{m}_{hf}") for m in (0, 2, 3, 5) for hf in range(2)}
        s_zr = [sem(f"z_roped{l}") for l in range(DEPTH)]
        s_rope = [sem(f"rope_loaded{l}") for l in range(DEPTH)]
        s_dft = [sem(f"dft_loaded{l}") for l in range(DEPTH)]
        s_f1 = [sem(f"f1_done{l}") for l in range(DEPTH)]
        s_pq = [[sem(f"pq_ready{l}_{b}") for b in range(2)] for l in range(DEPTH)]
        s_f2 = [sem(f"f2_done{l}") for l in range(DEPTH)]
        s_yhi = [sem(f"y_hi{l}") for l in range(DEPTH)]
        s_y = [sem(f"y_ready{l}") for l in range(DEPTH)]
        s_vt = [sem(f"vret_done{l}") for l in range(DEPTH)]
        s_v = [sem(f"vret_ready{l}") for l in range(DEPTH)]
        s_st = [sem(f"strip_args{l}") for l in range(DEPTH)]
        s_se = [sem(f"strip_exp{l}") for l in range(DEPTH)]
        s_sr = [sem(f"strip_ready{l}") for l in range(DEPTH)]
        s_s = [sem(f"ret_scores{l}") for l in range(DEPTH)]
        s_sd = [sem(f"ret_decayed{l}") for l in range(DEPTH)]
        s_pv = [sem(f"ret_pv{l}") for l in range(DEPTH)]
        s_osq = [sem(f"ret_squares{l}") for l in range(DEPTH)]
        s_var = [sem(f"ret_var{l}") for l in range(DEPTH)]
        s_rr = [sem(f"ret_rstd{l}") for l in range(DEPTH)]
        s_rh = [sem(f"ret_stacks_hi{l}") for l in range(DEPTH)]
        s_rl = [sem(f"ret_stacks_lo{l}") for l in range(DEPTH)]
        s_kh = [sem(f"att_keys_hi{l}") for l in range(DEPTH)]
        s_kl = [sem(f"att_keys_lo{l}") for l in range(DEPTH)]
        s_qh = [sem(f"att_queries_hi{l}") for l in range(DEPTH)]
        s_ql = [sem(f"att_queries_lo{l}") for l in range(DEPTH)]
        s_as = [sem(f"att_scores{l}") for l in range(DEPTH)]
        s_nm = [sem(f"att_negmax{l}") for l in range(DEPTH)]
        s_den = [sem(f"att_den_read{l}") for l in range(DEPTH)]
        s_p = [sem(f"att_probs{l}") for l in range(DEPTH)]
        s_pt = [sem(f"att_probsT{l}") for l in range(DEPTH)]
        s_ptl = [sem(f"att_pt_local{l}") for l in range(DEPTH)]
        s_ptc = [sem(f"att_pt_ctx{l}") for l in range(DEPTH)]
        s_av = [sem(f"att_av{l}") for l in range(DEPTH)]
        s_o = [sem(f"att_out{l}") for l in range(DEPTH)]
        s_oT = [sem(f"att_outT{l}") for l in range(DEPTH)]
        s_dv = sem("dve_chain")
        s_ac = sem("act_chain")
        s_wf = sem("wfin_loaded")
        s_fT = sem("final_transposed")
        s_fs = sem("final_stat")
        s_fo = sem("final_rows")
        s_out = [sem(f"out_stored{i}") for i in range(2)]

        phases = []
        for l in range(DEPTH):
            for kind, m in (("ffn", 3 * l), ("mix", 3 * l + 1), ("ffn", 3 * l + 2)):
                if kind == "ffn":
                    for hf in range(2):
                        phases.append(("in", l, m, hf, 2 * HALF, KD))
                        phases.append(("out", l, m, hf, KD, HALF))
                else:
                    phases.append(("win", l, m, 0, WIN_TILES, KD))
                    phases.append(("wo", l, m, 0, KD, KD))

        def dmas(kind, j):
            return 3 if kind == "wo" else 2 if kind == "win" and AQ_T <= 2 * j < AK_T else 1

        first, pair, loads = [], 0, 0
        for ph in phases:
            first.append((pair, loads))
            pair += ph[4] // 2
            loads += sum(dmas(ph[0], j) for j in range(ph[4] // 2))

        def pair0(i):
            return first[i][0]

        def read_value(i, j):
            return j + (pair0(i) + 2)

        def raw_value(i, j):
            kind = phases[i][0]
            if kind == "win":
                return 16 * (first[i][1] + sum(dmas(kind, a) for a in range(j + 1)))
            return j * (16 * dmas(kind, 0)) + 16 * (first[i][1] + dmas(kind, 0))

        def tokens(i):
            kind, l, m = phases[i][:3]
            return SEQ if l == DEPTH - 1 and (kind == "wo" or m == NS - 1) else TOK

        def h_value(m, k):
            if m == 0:
                return 1
            i = max(i for i, ph in enumerate(phases) if ph[2] == m - 1)
            return read_value(i, k // 2)

        def next_norm(i):
            kind, l, m, hf = phases[i][:4]
            return m + 1 if (kind == "wo" or (kind == "out" and hf)) and m + 1 < NS else None

        def norm_tokens(m):
            return SEQ if m == NS - 1 else TOK

        def norm_parts(m):
            cut = SEQ if norm_tokens(m) == TOK else SEQ // 2
            return [(0, cut), (cut, norm_tokens(m))]

        def acc_count(m, part, n):
            base = 2 if m == 0 else (KD + 2) + (KD + 4) * (m - 1) + 2
            return base + n + 1 + (2 * part if m and n >= KD - 2 else 0)

        def sq_count(m, part, n):
            base = 0 if m == 0 else KD + (KD + 2) * (m - 1)
            return base + n + 1 + (2 * part if m and n >= KD - 2 else 0)

        def vector_high(part, k):
            return part == 1 or k % 2 == 1

        def coef_count(m, k):
            return k // 2 + 1 if m == 0 else KD // 2 + m

        def xn_count(m, part, k):
            return KD * (2 * m + part) + k + 1

        def win_tokens(l, n):
            return TOK if l < DEPTH - 1 or n in (4, 5, 6, 7, 14, 15) else SEQ

        def ada_runs(i, n):
            kind, l, m, hf = phases[i][:4]
            b, first_pairs, second_pairs = ADA_PAIRS.get((l, m % 3 // 2, hf), (0, 0, 0))
            count = {"in": first_pairs, "out": second_pairs}.get(kind, 0)
            if kind == "out":
                b += 2 * first_pairs
            runs, at = [], 0
            while at < min(count, n):
                layer = (b + 2 * at) // MT
                end = min(count, n, ((layer + 1) * MT - b) // 2)
                runs.append((at, end, b, layer))
                at = end
            if at < n:
                runs.append((at, n, None, l))
            return runs

        ret_blocks = TOK // P

        def att_units(l):
            blocks = range(TOK // P if l < DEPTH - 1 else SEQ // P)
            return [(n, t, s) for t in range(GROUP) for n in blocks for s in range(KV_HEADS)]

        def pair_units(l):
            return len(att_units(l)) // GROUP

        ret_steps = [(hd, jt) for hd in range(RH) for jt in range(TOK // P)]
        ret_turns = [("scores", r) for r in range(15)] + [("variance", 0)] + [
            ("scores", r) for r in range(15, len(ret_steps))] + [("variance", 1)]
        RET_POST = 20

        def local_keys(n):
            if n >= SEQ // P:
                return 0, 0
            lo, hi = max(n - 1, 0), min(n + 1, SEQ // P - 1)
            return lo, hi - lo + 1

        def y_count(l):
            return 4 + len(att_units(l)) // 2

        blk = ctx.enter_context(nc.Block())

        @blk.sync
        def _(sp):
            for l in range(DEPTH):
                sp.dma_start(rows[0:MT, l, :], b_ada[l].rearrange("(r q) -> r q", q=P)).then_inc(s_rows, 16)
            sp.dma_start(rows[0:48, 2, :], norm_w.rearrange("l i (k q) -> (l i k) q", q=P)).then_inc(s_rows, 16)
            sp.dma_start(rows[48:56, 2, :], c.rearrange("b (k q) -> (b k) q", q=P)).then_inc(s_rows, 16)
            sp.dma_start(rows[56:64, 2, :], c_ctx.rearrange("(k q) -> k q", q=P)).then_inc(s_rows, 16)
            sp.dma_start(rows[64:68, 2, :], ret_gn_w.rearrange("l (k q) -> (l k) q", q=P)).then_inc(s_rows, 16)
            sp.dma_start(consts[:, :], small).then_inc(s_const, 16)
            sp.dma_start(window_sb[:, :], window).then_inc(s_const, 16)
            for tt in range(TOK // P):
                src = x[0] if tt < SEQ // P else ctx_in[0]
                r = tt * P - (0 if tt < SEQ // P else SEQ)
                sp.dma_start(xtok[:, tt, :], src[r:r + P, :]).then_inc(s_x[tt // 2], 16)

            def load_ada(t, i, layer):
                for b in range(2):
                    if not (isinstance(i, int) and t + 2 * i == ADA_FIRST):
                        sp.wait_ge(s_ada_used, i * 2 + (t + b - ADA_FIRST - 1))
                    c0 = (t - layer * MT) * P
                    sp.dma_start(ada[:, b], w_ada[layer][D // 2 * b:D // 2 * (b + 1), ds(i * (2 * P) + c0, 2 * P)
                                                         ].rearrange("(k p) n -> p k n", p=P)).then_inc(s_ada[b], 16)

            def load_unit(i, s, j, src, wait):
                if wait is not None:
                    sp.wait_ge(s_w[s], wait)
                if phases[i][0] == "wo":
                    sp.dma_start(raw[:, s, 0:4], src[0]).then_inc(s_raw[s], 16)
                    for v in range(KV_HEADS):
                        sp.dma_start(raw[HD * v:HD * v + HD, s, 4:8], src[1 + v]).then_inc(s_raw[s], 16)
                else:
                    sp.dma_start(raw[:, s, 0:phases[i][5]], src).then_inc(s_raw[s], 16)

            def ffn_in_src(l, m, col):
                return ffn_w_in[l, m % 3 // 2][:, col].rearrange("(k p) n -> p k n", p=P)

            for i, (kind, l, m, hf, units, kt) in enumerate(phases):
                j0 = pair0(i)
                if kind == "in":
                    c0 = hf * HALF * P

                    def load_step(f, b, layer):
                        load_unit(i, 0, f, ffn_in_src(l, m, ds(f * P + c0, P)), f + j0)
                        load_unit(i, 1, f, ffn_in_src(l, m, ds(f * P + (DFF + c0), P)),
                                  f + j0)
                        if b is not None:
                            load_ada(b, f, layer)
                elif kind == "out":
                    r0 = hf * HALF * P

                    def load_step(j, b, layer):
                        for s in range(2):
                            src = ffn_w_out[l, m % 3 // 2][r0:r0 + HALF * P, ds(j * (2 * P) + s * P, P)]
                            load_unit(i, s, j, src.rearrange("(k p) n -> p k n", p=P), j + j0)
                        if b is not None:
                            load_ada(b, j, layer)
                if kind in ("in", "out"):
                    for a, e, b, layer in ada_runs(i, units // 2):
                        if i == 0 and a == 0:
                            load_unit(i, 0, 0, ffn_in_src(l, m, slice(0, P)), None)
                            load_unit(i, 1, 0, ffn_in_src(l, m, slice(DFF, DFF + P)), None)
                            for q in range(4):
                                for g in range(2):
                                    at = g * D + q * 2 * P
                                    sp.dma_start(ada_first[q][:, :, g * 2 * P:(g + 1) * 2 * P],
                                                 w_ada[0][:, at:at + 2 * P].rearrange("(k p) n -> p k n", p=P)
                                                 ).then_inc(s_ada0[q], 16)
                            sp.dma_start(dist_sb[:, :], dist).then_inc(s_vec, 16)
                            sp.dma_start(sink[:, :], attn_sink.rearrange("l n -> (l n)").partition_broadcast(P)
                                         ).then_inc(s_vec, 16)
                            sp.dma_start(lg[:, :], ret_decay.rearrange("l d n -> (l d n)").partition_broadcast(P)
                                         ).then_inc(s_vec, 16)
                            load_ada(b, 0, layer)
                            a = 1
                        with sp.Fori(a, e) as j:
                            load_step(j, b, layer)
                elif kind == "win":
                    for n in range(WIN_TILES):
                        if n == 4:
                            sp.wait_ge(s_xn, xn_count(m, 1, KD - 1))
                            sp.dma_start(rope_sb[:, :, :], rope.rearrange("a p t -> p a t")).then_inc(s_rope[l], 16)
                            sp.dma_start(dft_sb[:, :, :, :], dft.rearrange("a (t p) q -> p a t q", p=P)
                                         ).then_inc(s_dft[l], 16)
                        if AQ_T <= n < AK_T:
                            sp.wait_ge(s_w[n % 2], j0 + n // 2)
                            for v in range(KV_HEADS):
                                c0 = AQ_COL + (v * GROUP + n - AQ_T) * HD
                                src = w_in[l][:, c0:c0 + HD].rearrange("(k p) n -> p k n", p=P)
                                sp.dma_start(raw[:, n % 2, 0:KD, v * HD:(v + 1) * HD], src
                                             ).then_inc(s_raw[n % 2], 16)
                        else:
                            c0 = n * P
                            src = w_in[l][:, c0:c0 + P].rearrange("(k p) n -> p k n", p=P)
                            load_unit(i, n % 2, n // 2, src, j0 + n // 2)
                else:
                    with sp.Fori(0, units // 2) as j:
                        for s in range(2):
                            cols = ds(j * (2 * P) + s * P, P)
                            src = [w_o[l][0:512, cols].rearrange("(k p) n -> p k n", p=P)] + [
                                w_o[l][512 + 256 * v:768 + 256 * v, cols].rearrange("(t q) n -> q t n", q=HD)
                                for v in range(KV_HEADS)]
                            load_unit(i, s, j, src, j + j0)
            for s in range(2):
                sp.wait_ge(s_free[s], h_value(NS, KD - 2))
            sp.dma_start(wfin[:, :], final_norm_w.partition_broadcast(P)).then_inc(s_wf, 16)
            for tt in range(SEQ // P):
                sp.wait_ge(s_fo, tt + 1)
                sp.dma_start(out[0, tt * P:(tt + 1) * P, :], osb[:, tt % 2]).then_inc(s_out[tt % 2], 16)
            for b in range(2):
                sp.wait_ge(s_out[b], 16 * (SEQ // P // 2))

        @blk.gpsimd
        def _(pool):
            nc.gpsimd.memset(cond[:, :, :], 0.0).then_inc(s_ones, 1)
            nc.gpsimd.memset(eps[:, :], EPS).then_inc(s_ones, 1)
            nc.gpsimd.memset(ones[:, :], 1.0).then_inc(s_ones, 1)

            def low(out, src, high):
                return nc.gpsimd.tensor_tensor(out, src, high.bitcast(f32), ALU.subtract)

            def norm(m):
                for part_, (p0, p1) in enumerate(norm_parts(m)):
                    pool.wait_ge(s_r, 2 * m + part_ + 1)
                    for k in range(KD):
                        if k >= 2:
                            pool.wait_ge(s_xf, xn_count(m, part_, k - 2))
                        nc.gpsimd.tensor_tensor(tnorm[:, k % 2, p0:p1], h[:, k, p0:p1], rstd[:, p0:p1], ALU.mult
                                                ).then_inc(s_t, 1)

            for l in range(DEPTH):
                tq = TOK if l < DEPTH - 1 else SEQ
                norm(3 * l)
                norm(3 * l + 1)
                for hd in range(RH):
                    b = hd % 2
                    own, oth = slice(HD * b, HD * b + HD), slice(HD - HD * b, 2 * HD - HD * b)
                    k, q = z[own, RK_T + hd // 2, :], z[own, RQ_T + hd // 2, 0:tq]
                    pool.wait_ge(s_rh[l], hd + 1)
                    low(rk_st[b][oth, :], k, rk_st[b][own, :]).then_inc(s_rl[l], 1)
                    low(rq_lo[b][own, 0:tq], q, rq_hi[b][own, 0:tq]).then_inc(s_rl[l], 1)
                    low(rq_lo[b][oth, 0:tq], q, rq_hi[b][own, 0:tq]).then_inc(s_rl[l], 1)
                for v in range(KV_HEADS):
                    own = slice(HD * v, HD * v + HD)
                    pool.wait_ge(s_kh[l], 2 * v + 2)
                    for half in range(2):
                        low(ak_lo[v][HD * half:HD * half + HD, :], z[own, AK_T, :], ak_hi[v][own, :]
                            ).then_inc(s_kl[l], 1)
                for t in range(GROUP):
                    for v in range(KV_HEADS):
                        own, oth = slice(HD * v, HD * v + HD), slice(HD - HD * v, 2 * HD - HD * v)
                        st = aq_st[t % 2][v]
                        pool.wait_ge(s_qh[l], KV_HEADS * t + v + 1)
                        low(st[oth, 0:tq], z[own, AQ_T + t, 0:tq], st[own, 0:tq]).then_inc(s_ql[l], 1)
                norm(3 * l + 2)

        @blk.tensor
        def _(pe):
            def split_product(s, kt, i, hi, lo, t, before):
                parts = [(0, SEQ)] + ([(SEQ, TOK)] if t == TOK else [])
                last = None
                for k in range(kt):
                    if before is not None:
                        before(k)
                    for n, (w, v) in enumerate(((whi, hi), (whi, lo), (wlo, hi))):
                        for p0, p1 in parts:
                            last = nc.tensor.matmul(pg[s][:, p0:p1], w[:, s, k], v[:, k, p0:p1],
                                                    start=(k == 0 and n == 0), stop=(k == kt - 1 and n == 2))
                last.then_inc(s_unit[s], 1)

            def unit(i, s, j, hi, lo, t, before=None):
                pe.wait_ge(s_w[s], j + (pair0(i) + 1))
                pe.wait_ge(s_free[s], read_value(i, j - 1))
                split_product(s, phases[i][5], i, hi, lo, t, before)

            def ada_product(t, i):
                for b in range(2):
                    pe.wait_ge(s_ada[b], i * 16 + (8 * (t - ADA_FIRST) + 16))
                    for j in range(4):
                        last = nc.tensor.matmul(pa[0][32 * j:32 * j + 32, 0:2 * P], cond[:, 4 * b + j], ada[:, b, j],
                                                start=(b == 0), stop=(b == 1))
                    last.then_inc(s_ada_used, 1)

            def ada_fold(t, i):
                pe.wait_ge(s_part, i + ((t - ADA_FIRST) // 2 + 1))
                pe.wait_ge(s_mod, i + t // 2)
                for b in range(2):
                    last = nc.tensor.matmul(pa[1][:, 2 * b:2 * b + 2], part[:, b * P:(b + 1) * P], fold,
                                            start=True, stop=True)
                last.then_inc(s_fold, 1)

            pe.wait_ge(s_rows, 16 * 6)
            pe.wait_ge(s_const, 16 * 2)
            for r, n in enumerate((MT, MT, 68)):
                last = nc.tensor.transpose(pn[:, r * P:r * P + n], rows[0:n, r, :], ident[0:n, 0:n])
            last.then_inc(s_rowsT, 1)
            for tt in range(TOK // P):
                pe.wait_ge(s_x[tt // 2], 32)
                if tt >= 2:
                    pe.wait_ge(s_xTr[tt % 2], tt // 2)
                for k in range(KD):
                    last = nc.tensor.transpose(pg[tt % 2][:, k * P:(k + 1) * P], xtok[:, tt, k * P:(k + 1) * P],
                                               ident)
                last.then_inc(s_xT, 1)

            def first_modulation(q):
                pe.wait_ge(s_ada0[q], 32)
                if q >= 2:
                    pe.wait_ge(s_mod, 2 * (q - 1))
                for k in range(KD):
                    j = k % 4
                    last = nc.tensor.matmul(pa[q % 2][32 * j:32 * j + 32, :], cond[:, k], ada_first[q][:, k],
                                            start=(k < 4), stop=(k >= 4))
                last.then_inc(s_ada_first, 1)

            def first_fold(q):
                pe.wait_ge(s_part0[q % 2], q // 2 + 1)
                for t in range(4):
                    last = nc.tensor.matmul(pa[q % 2][:, 2 * t:2 * t + 2],
                                            part_first[:, (4 * q + t) * P:(4 * q + t + 1) * P], fold,
                                            start=True, stop=True)
                last.then_inc(s_fold0, 1)

            pe.wait_ge(s_cond, 1)
            pe.wait_ge(s_ones, 3)

            def square_sums(m, part_):
                p0, p1 = norm_parts(m)[part_]
                pe.wait_ge(s_acc, acc_count(m, part_, KD - 1))
                nc.tensor.matmul(pn[:, 512 * part_:512 * part_ + p1 - p0], ones[:, :], rstd[:, p0:p1],
                                 start=True, stop=True).then_inc(s_ss, 1)

            def part_product(s, k, kt, hi, lo, p0, p1, c0):
                for n, (w, v) in enumerate(((whi, hi), (whi, lo), (wlo, hi))):
                    last = nc.tensor.matmul(pg[s][:, c0:c0 + p1 - p0], w[:, s, k], v[:, k, p0:p1],
                                            start=(k == 0 and n == 0), stop=(k == kt - 1 and n == 2))
                return last

            def last_pair(i, hi, lo):
                m, kt, j = next_norm(i), phases[i][5], phases[i][4] // 2 - 1
                for part_, (p0, p1) in enumerate(norm_parts(m)):
                    for s in range(2):
                        if part_ == 0:
                            pe.wait_ge(s_w[s], j + pair0(i) + 1)
                            pe.wait_ge(s_free[s], read_value(i, j - 1))
                        for k in range(kt):
                            last = part_product(s, k, kt, hi, lo, p0, p1, 512 * part_)
                            if part_ == 1 and s == 0 and k == KD - 1:
                                square_sums(m, 0)
                        last.then_inc(s_unit[s] if part_ else s_early, 1)

            def first_pair(i, t):
                m = phases[i][2]
                parts = norm_parts(m) if t == norm_tokens(m) else norm_parts(m)[0:1]
                if m == 0:
                    first_modulation(0)
                    first_modulation(1)
                    square_sums(m, 0)
                    first_fold(0)
                    first_fold(1)
                    first_modulation(2)
                for part_, (p0, p1) in enumerate(parts):
                    half = KD // 2
                    if part_ < len(parts) - 1:
                        order = [(0, k) for k in range(half)] + [(1, k) for k in range(half)] + [
                            (s, k) for k in range(half, KD) for s in range(2)]
                    elif part_ == 0:
                        order = [(s, half * b + k) for b in range(2) for s in range(2) for k in range(half)]
                    else:
                        order = [(s, k) for s in range(2) for k in range(KD)]
                    for s, k in order:
                        if part_ == 0 and k == 0:
                            pe.wait_ge(s_w[s], pair0(i) + 1)
                            pe.wait_ge(s_free[s], read_value(i, -1))
                        if s == 0:
                            pe.wait_ge(s_xn, xn_count(m, part_, k))
                        last = part_product(s, k, KD, xhi, xlo, p0, p1, p0)
                        if k == KD - 1 and part_ == len(parts) - 1:
                            last.then_inc(s_unit[s], 1)
                        if part_ == 0 and (s, k) == (0, 1):
                            square_sums(m, 1)
                        if m == 0 and part_ == 0:
                            if (s, k) == (0, 1):
                                first_fold(2)
                            if (s, k) == (0, 3):
                                first_modulation(3)
                            if (s, k) == (1, 1):
                                first_fold(3)

            def mix(i, l):
                nt = TOK // P if l < DEPTH - 1 else SEQ // P
                tq = nt * P
                for s in range(2):
                    pe.wait_ge(s_free[s], read_value(i, WIN_TILES // 2 - 1))
                pe.wait_ge(s_zr[l], len(ROPE_TILES))
                for tt in range(nt):
                    if tt >= 2:
                        pe.wait_ge(s_pq[l][tt % 2], tt // 2)
                    for ft in range(2):
                        last = nc.tensor.matmul(pa[tt % 2][:, ft * 256:ft * 256 + 256],
                                                z[:, F_T + ft, tt * P:(tt + 1) * P], cs64, start=True, stop=True)
                    last.then_inc(s_f1[l], 1)
                for b in range(2):
                    pe.wait_ge(s_pq[l][b], nt // 2)
                pe.wait_ge(s_dft[l], 16)
                for ft in range(2):
                    dst = (pn, pg[0])[ft]
                    for tt in range(nt):
                        for cs in range(2):
                            w = pq[:, tt, ft * 256 + cs * P:ft * 256 + cs * P + P]
                            if tt < SEQ // P:
                                last = nc.tensor.matmul(dst[:, 0:SEQ], w, dft_sb[:, cs, tt],
                                                        start=(tt == 0 and cs == 0), stop=(tt == 3 and cs == 1))
                            else:
                                last = nc.tensor.matmul(dst[:, SEQ:TOK], w, dft_sb[:, cs, tt - 4, 0:SEQ:2],
                                                        start=(tt == 4 and cs == 0), stop=(tt == 5 and cs == 1))
                    last.then_inc(s_f2[l], 1)
                for tt in range(ret_blocks):
                    if tt >= 2:
                        pe.wait_ge(s_v[l], tt - 1)
                    for v in range(2):
                        nc.tensor.matmul(pa[tt % 2][:, v * P:(v + 1) * P], z[:, RV_T + v, tt * P:(tt + 1) * P],
                                         center, start=True, stop=True)
                    nc.tensor.transpose(pa[tt % 2][:, 2 * P:3 * P], z[:, AV_T, tt * P:(tt + 1) * P], ident
                                        ).then_inc(s_vt[l], 1)
                pe.wait_ge(s_v[l], ret_blocks)
                pe.wait_ge(s_y[l], 2)
                spare = [pg[1], pn]

                def free_slot(turn):
                    what, r = ret_turns[turn - 2]
                    pe.wait_ge(s_sd[l] if what == "scores" else s_rr[l], r + 1)

                def scores(turn, r):
                    hd, jt = ret_steps[r]
                    b = hd % 2
                    if turn >= 2:
                        free_slot(turn)
                    if jt == 0:
                        pe.wait_ge(s_rl[l], 3 * (hd + 1))
                    kT = rk_st[b][:, jt * P:(jt + 1) * P]
                    for p0, p1 in [(0, SEQ)] + ([(SEQ, TOK)] if jt >= SEQ // P and tq == TOK else []):
                        nc.tensor.matmul(spare[turn % 2][:, p0:p1], kT, rq_hi[b][:, p0:p1], start=True, stop=False)
                        last = nc.tensor.matmul(spare[turn % 2][:, p0:p1], kT, rq_lo[b][:, p0:p1],
                                                start=False, stop=True)
                    last.then_inc(s_s[l], 1)

                def variance(turn, p):
                    free_slot(turn)
                    pe.wait_ge(s_osq[l], p + 1)
                    for p0, p1 in [(0, SEQ)] + ([(SEQ, TOK)] if tq == TOK else []):
                        last = nc.tensor.matmul(spare[turn % 2][:, p0:p1], block, osq[:, p, p0:p1],
                                                start=True, stop=True)
                    last.then_inc(s_var[l], 1)

                def values(r):
                    hd, jt = ret_steps[r]
                    p0 = HD * (hd % 2)
                    pe.wait_ge(s_sd[l], r + 1)
                    o = (pg[0], p67)[hd // 2]
                    w = vret[:, jt, hd * HD:(hd + 1) * HD]
                    last = nc.tensor.matmul(o[p0:p0 + HD, 0:SEQ], w, sdec[:, r % 2, 0:SEQ],
                                            start=(jt == 0), stop=(jt == ret_blocks - 1))
                    if jt >= SEQ // P and tq == TOK:
                        last = nc.tensor.matmul(o[p0:p0 + HD, SEQ:TOK], w, sdec[:, r % 2, SEQ:TOK],
                                                start=(jt == SEQ // P), stop=(jt == ret_blocks - 1))
                    last.then_inc(s_pv[l], 1)

                units = att_units(l)

                def att_scores(q):
                    n, t, s = units[q]
                    lo, nk = local_keys(n)
                    if q >= 2:
                        pe.wait_ge(s_p[l], q - 1)
                    if q % pair_units(l) == 0:
                        pe.wait_ge(s_ql[l], KV_HEADS * (t + 1))
                    w = aq_st[t % 2][s][:, n * P:(n + 1) * P]
                    if nk:
                        c0 = SEQ - nk * P
                        sides = ([(c0, 0)] if n > 0 else []) + ([(SEQ - P, 1)] if n < SEQ // P - 1 else [])
                        for part_, (k, first_) in enumerate(((ak_hi, True), (ak_lo, False))):
                            nc.tensor.matmul(pg[q % 2][:, c0:SEQ], w, k[s][:, lo * P:(lo + nk) * P], start=first_,
                                             stop=False, skip_group_check=True)
                        for c, side in sides:
                            nc.tensor.matmul(pg[q % 2][:, c:c + P], ident_r[:, :], window_r[:, side], start=False,
                                             stop=(c, side) == sides[-1], skip_group_check=True)
                    nc.tensor.matmul(pg[q % 2][:, SEQ:TOK], w, ak_hi[s][:, SEQ:TOK], start=True, stop=False)
                    nc.tensor.matmul(pg[q % 2][:, SEQ:TOK], w, ak_lo[s][:, SEQ:TOK], start=False, stop=True
                                     ).then_inc(s_as[l], 1)

                for turn, (what, r) in enumerate(ret_turns):
                    if what == "variance":
                        if r == 1:
                            values(len(ret_steps) - 1)
                            pe.wait_ge(s_y[l], 3)
                            pe.wait_ge(s_kl[l], 2 * KV_HEADS)
                            att_scores(0)
                        variance(turn, r)
                    else:
                        scores(turn, r)
                        if r:
                            values(r - 1)
                def att_transpose(q):
                    n, t, s = units[q]
                    nk, nb = local_keys(n)[1], max(local_keys(n)[1], 1)
                    pe.wait_ge(s_p[l], q + 1)
                    if q >= 1:
                        pe.wait_ge(s_ptc[l], q)
                        pe.wait_ge(s_ptl[l], q)
                    for j in range(nk + 2):
                        dst = j * P if j < nb else 512 + (j - nb) * P
                        last = nc.tensor.transpose(pn[:, dst:dst + P], prob[:, q % 2, j * P:(j + 1) * P], ident)
                    last.then_inc(s_pt[l], 1)

                def att_values(q):
                    n, t, s = units[q]
                    lo, nk = local_keys(n)
                    if q == 0:
                        pe.wait_ge(s_y[l], 4)
                    pe.wait_ge(s_ptc[l], q + 1)
                    pe.wait_ge(s_ptl[l], q + 1)
                    if s == 0 and q >= 4:
                        pe.wait_ge(s_y[l], 3 + q // 2)
                    tiles = [lo + j for j in range(nk)] + [4, 5]
                    for j, kt in enumerate(tiles):
                        last = nc.tensor.matmul(pa[q // 2 % 2][:, s * HD:(s + 1) * HD], probT[:, q % 2, j * P:(j + 1) * P],
                                                vatt[:, kt, s * HD:(s + 1) * HD],
                                                start=(j == 0), stop=(j == len(tiles) - 1))
                    last.then_inc(s_av[l], 1)

                def att_out(pr):
                    pe.wait_ge(s_o[l], pr + 1)
                    nc.tensor.transpose(pa[pr % 2][:, P:2 * P], otok[:, pr % 2], ident).then_inc(s_oT[l], 1)

                att_scores(1)
                for q in range(len(units) + 3):
                    if q >= 4 and q % 2 == 0:
                        att_out((q - 4) // 2)
                    if q + 2 < len(units):
                        att_scores(q + 2)
                    if q < len(units):
                        att_transpose(q)
                    if 1 <= q <= len(units):
                        att_values(q - 1)

            for i, (kind, l, m, hf, units, kt) in enumerate(phases):
                t = tokens(i)
                if kind == "in":
                    for a, e, b, _ in ada_runs(i, units // 2):
                        if hf == 0 and a == 0:
                            first_pair(i, t)
                            if b is not None:
                                ada_product(b, 0)
                                ada_fold(b, 0)
                            a = 1
                        with pe.Fori(a, e) as f:
                            unit(i, 0, f, xhi, xlo, t)
                            if b is not None:
                                ada_product(b, f)
                            unit(i, 1, f, xhi, xlo, t)
                            if b is not None:
                                ada_fold(b, f)
                elif kind == "out":
                    n = units // 2 - (next_norm(i) is not None)
                    for a, e, b, _ in ada_runs(i, n):
                        with pe.Fori(a, e) as j:
                            unit(i, 0, j, ahi, alo, t, lambda k: pe.wait_ge(s_a[m, hf], k + 1))
                            if b is not None:
                                ada_product(b, j)
                            unit(i, 1, j, ahi, alo, t)
                            if b is not None:
                                ada_fold(b, j)
                    if next_norm(i) is not None:
                        last_pair(i, ahi, alo)
                elif kind == "win":
                    first_pair(i, win_tokens(l, 0))
                    runs, n = [], 2
                    while n < WIN_TILES:
                        e = n
                        while e < WIN_TILES and win_tokens(l, e) == win_tokens(l, n):
                            e += 2
                        runs.append((n // 2, e // 2, win_tokens(l, n)))
                        n = e
                    for b, e, tw in runs:
                        if tw == TOK:
                            pe.wait_ge(s_xn, xn_count(m, 1, KD - 1))
                        with pe.Fori(b, e) as j:
                            unit(i, 0, j, xhi, xlo, tw)
                            unit(i, 1, j, xhi, xlo, tw)
                    mix(i, l)
                else:
                    pe.wait_ge(s_y[l], y_count(l))
                    with pe.Fori(0, units // 2 - 1) as j:
                        unit(i, 0, j, xhi, xlo, t)
                        unit(i, 1, j, xhi, xlo, t)
                    last_pair(i, xhi, xlo)
            for s in range(2):
                pe.wait_ge(s_free[s], h_value(NS, KD - 2))
            for tt in range(SEQ // P):
                for k in range(KD):
                    last = nc.tensor.transpose(pfin[tt][:, k * P:(k + 1) * P], h[:, k, tt * P:(tt + 1) * P], ident)
                last.then_inc(s_fT, 1)

        @blk.scalar
        def _(act):
            chain = [0]

            def link(ins):
                chain[0] += 1
                ins.then_inc(s_ac, 1)
                act.wait_ge(s_ac, chain[0])

            def split_hi(i, s, j, after=None):
                act.wait_ge(s_raw[s], raw_value(i, j))
                if i or not isinstance(j, int) or j:
                    act.wait_ge(s_unit[s], j + pair0(i))
                nk = phases[i][5]
                nc.scalar.copy(whi[:, s, 0:nk], raw[:, s, 0:nk]).then_inc(s_whi[s], 1)

            def square(m, k, s, value):
                t = norm_tokens(m)
                col = slice(k, k + 1) if isinstance(k, int) else ds(k, 1)
                act.wait_ge(s_free[s], value)
                act.wait_ge(s_acc, k + (acc_count(m, 0, 0) - 2))
                nc.scalar.activation(xfull[:, s, 0:t], h[:, col, 0:t].rearrange("p o t -> p (o t)"), ACT.Square
                                     ).then_inc(s_sq, 1)

            def square_part(i, part_, s):
                m = next_norm(i)
                p0, p1 = norm_parts(m)[part_]
                if part_ == 0:
                    act.wait_ge(s_h0, 2 * (m - 1) + s + 1)
                    act.wait_ge(s_acc, acc_count(m, 0, KD - 4 + s))
                else:
                    act.wait_ge(s_free[s], read_value(i, phases[i][4] // 2 - 1))
                nc.scalar.activation(xfull[:, s, p0:p1], h[:, KD - 2 + s, p0:p1], ACT.Square).then_inc(s_sq, 1)

            def copy_part(t, i):
                act.wait_ge(s_ada_used, i * 2 + (t - ADA_FIRST + 2))
                nc.scalar.copy(part[:, :], pa[0][:, 0:2 * P]).then_inc(s_part, 1)

            act.wait_ge(s_cols, 1)
            act.wait_ge(s_ones, 3)
            nc.scalar.activation(cond[:, :, 0:2], vecs[:, 48:64].rearrange("p (v k) -> p k v", v=2), ACT.Silu
                                 ).then_inc(s_cond, 1)
            for tt in range(0, TOK // P, 2):
                act.wait_ge(s_xT, tt + 1)
                nc.scalar.copy(h[:, :, tt * P:(tt + 1) * P], pg[0][:, :].rearrange("p (k t) -> p k t", k=KD)
                               ).then_inc(s_xTr[0] if tt < 4 else s_free[0], 1)
            split_hi(0, 0, 0)
            split_hi(0, 1, 0)
            act.wait_ge(s_free[1], 1)
            for k in range(KD):
                square(0, k, k % 2, 1)

            def copy_first(q):
                act.wait_ge(s_ada_first, q + 1)
                nc.scalar.copy(part_first[:, q * 512:(q + 1) * 512], pa[0]).then_inc(s_part0[0], 1)

            copy_first(0)

            def decays():
                act.wait_ge(s_lgd, 1)
                link(nc.scalar.activation(lgt[:, 1], lgt[:, 0], ACT.Exp, scale=-1.0))
                nc.scalar.activation(lgt[:, 2], lgt[:, 1], ACT.Ln, bias=1.0).then_inc(s_lg, 1)

            def norm(i, m):
                def root(part_):
                    p0, p1 = norm_parts(m)[part_]
                    act.wait_ge(s_ss, 2 * m + part_ + 1)
                    link(nc.scalar.activation(rstd[:, p0:p1], pn[:, 512 * part_:512 * part_ + p1 - p0], ACT.Ln,
                                              bias=eps[:, :], scale=1.0 / D))
                    nc.scalar.activation(rstd[:, p0:p1], rstd[:, p0:p1], ACT.Exp, scale=-0.5).then_inc(s_r, 1)

                def modulate(part_, k):
                    p0, p1 = norm_parts(m)[part_]
                    act.wait_ge(s_t, xn_count(m, part_, k))
                    if part_ == 0:
                        act.wait_ge(s_coef, coef_count(m, k))
                    if k >= 2:
                        act.wait_ge(s_xn, xn_count(m, part_, k - 2))
                    v = 1 if p0 >= SEQ else 0
                    for dst in (xfull[:, k % 2, p0:p1], xhi[:, k, p0:p1])[:1 if vector_high(part_, k) else 2]:
                        last = nc.scalar.activation(dst, tnorm[:, k % 2, p0:p1], ACT.Identity,
                                                    bias=mod[:, shift + k, v:v + 1], scale=acol[:, k, v:v + 1])
                    last.then_inc(s_xf, 1)

                shift = m // 3 * MT + m % 3 * 3 * KD
                nc.scalar.preload_act_table_set("natural_log_exp_and_others")
                root(0)
                if m:
                    split_hi(i + 1, 0, 0)
                    square_part(i, 1, 0)
                modulate(0, 0)
                modulate(0, 1)
                if m:
                    split_hi(i + 1, 1, 0)
                    square_part(i, 1, 1)
                for k in range(2, KD):
                    if m == 0 and k == 2:
                        copy_first(2)
                    modulate(0, k)
                    if k == 5:
                        root(1)
                for k in range(KD):
                    modulate(1, k)
                if m == 0:
                    decays()

            def mix(i, l):
                nt = TOK // P if l < DEPTH - 1 else SEQ // P
                tq = nt * P
                def ret_hi(hd):
                    b = hd % 2
                    own, oth = slice(HD * b, HD * b + HD), slice(HD - HD * b, 2 * HD - HD * b)
                    k, q = z[own, RK_T + hd // 2, :], z[own, RQ_T + hd // 2, 0:tq]
                    if hd >= 2:
                        act.wait_ge(s_s[l], ret_blocks * (hd - 1))
                    nc.scalar.copy(rk_st[b][own, :], k)
                    nc.scalar.copy(rq_hi[b][own, 0:tq], q)
                    nc.scalar.copy(rq_hi[b][oth, 0:tq], q).then_inc(s_rh[l], 1)

                def att_keys_hi():
                    act.wait_ge(s_vt[l], ret_blocks)
                    for v in range(KV_HEADS):
                        for half in range(2):
                            nc.scalar.copy(ak_hi[v][HD * half:HD * half + HD, :], z[HD * v:HD * v + HD, AK_T, :]
                                           ).then_inc(s_kh[l], 1)

                def att_queries_hi(t, v):
                    own = slice(HD * v, HD * v + HD)
                    nc.scalar.copy(aq_st[t % 2][v][own, 0:tq], z[own, AQ_T + t, 0:tq]).then_inc(s_qh[l], 1)

                def squares(p):
                    act.wait_ge(s_pv[l], 2 * ret_blocks * (p + 1))
                    nc.scalar.activation(osq[:, p, 0:tq], (pg[0], p67)[p][:, 0:tq], ACT.Square).then_inc(s_osq[l], 1)

                def ret_rstd(p):
                    act.wait_ge(s_var[l], p + 1)
                    src = (pg[1], pn)[ret_turns.index(("variance", p)) % 2]
                    link(nc.scalar.activation(osq[:, p, 0:tq], src[:, 0:tq], ACT.Ln, bias=eps[:, :]))
                    nc.scalar.activation(osq[:, p, 0:tq], osq[:, p, 0:tq], ACT.Exp, scale=-0.5).then_inc(s_rr[l], 1)

                act.wait_ge(s_zr[l], len(ROPE_TILES))
                act.wait_ge(s_unit[1], pair0(i) + WIN_TILES // 2)
                nc.scalar.preload_act_table_set("natural_log_exp_and_others")
                for tt in range(0, nt, 2):
                    act.wait_ge(s_f1[l], tt + 1)
                    length = SEQ if tt < SEQ // P else CTX
                    nc.scalar.mul(pq[:, tt], pa[0], float((length * HD) ** -0.5)).then_inc(s_pq[l][0], 1)
                ret_hi(0)
                ret_hi(1)

                def strip(hd):
                    b = l * 2 * RH + hd
                    act.wait_ge(s_st[l], hd + 1)
                    if hd:
                        act.wait_ge(s_sr[l], hd)
                    nc.scalar.activation(strips[hd][:, 0:U_D], strips[hd][:, 0:U_D], ACT.Exp)
                    nc.scalar.activation(strips[hd][:, U_D:], dist_sb[:, 256:U_D], ACT.Exp,
                                         bias=lgb[:, 0, b:b + 1], scale=lg[:, b:b + 1])
                    nc.scalar.activation(strip_b[:, :], dist_sb[:, 256:U_D], ACT.Exp,
                                         bias=lgb[:, 1, b + RH:b + RH + 1], scale=nlg[:, b + RH:b + RH + 1]
                                         ).then_inc(s_se[l], 1)

                strip(0)
                for ft in range(2):
                    act.wait_ge(s_f2[l], ft + 1)
                    nc.scalar.copy(xhi[:, ft, 0:tq], (pn, pg[0])[ft][:, 0:tq]).then_inc(s_yhi[l], 1)
                    if ft == 0:
                        strip(1)
                att_keys_hi()
                strip(2)
                ret_hi(2)
                strip(3)
                ret_hi(3)
                squares(0)
                ret_rstd(0)
                att_queries_hi(0, 0)
                att_queries_hi(0, 1)
                squares(1)
                ret_rstd(1)
                units = att_units(l)
                for q in range(len(units) + 4):
                    if q < len(units):
                        n, t, s = units[q]
                        hd = l * AH + t + GROUP * s
                        w = (local_keys(n)[1] + 2) * P
                        act.wait_ge(s_nm[l], q + 1)
                        if q >= 2:
                            act.wait_ge(s_pt[l], q - 1)
                        if q >= 4:
                            act.wait_ge(s_den[l], q // 2 - 1)
                        b = slice(q % 4, q % 4 + 1)
                        nc.scalar.activation(esink[:, b], sink[:, hd:hd + 1], ACT.Exp, bias=negm[:, b])
                        nc.scalar.activation(prob[:, q % 2, 0:w], pg[q % 2][:, TOK - w:TOK], ACT.Exp,
                                             bias=negm[:, b], accum_out=den[:, b]).then_inc(s_p[l], 1)
                    if 1 <= q <= len(units):
                        nk = local_keys(units[q - 1][0])[1]
                        nb = max(nk, 1)
                        act.wait_ge(s_pt[l], q)
                        if q >= 3:
                            act.wait_ge(s_av[l], q - 2)
                        nc.scalar.copy(probT[:, (q - 1) % 2, nb * P:(nk + 2) * P], pn[:, 512:512 + (nk + 2 - nb) * P]
                                       ).then_inc(s_ptc[l], 1)
                    if q >= 4 and q % 2 == 0:
                        pr = (q - 4) // 2
                        n, t, _ = units[2 * pr]
                        act.wait_ge(s_oT[l], pr + 1)
                        nc.scalar.copy(xhi[:, 4 + t, n * P:(n + 1) * P], pa[pr % 2][:, P:2 * P]).then_inc(s_yhi[l], 1)
                    at = q % pair_units(l) - 2
                    if q // pair_units(l) + 1 < GROUP and 0 <= at < KV_HEADS:
                        if q == 2:
                            act.wait_ge(s_rl[l], 3 * RH)
                        act.wait_ge(s_as[l], q)
                        att_queries_hi(q // pair_units(l) + 1, at)

            for i, (kind, l, m, hf, units, kt) in enumerate(phases):
                t = tokens(i)
                j0 = pair0(i)
                more = i + 1 < len(phases)
                if kind in ("in", "win") and hf == 0:
                    norm(i - 1, m)
                if kind == "in":
                    def step(f, nxt, jn, b):
                        act.wait_ge(s_unit[0], f + (j0 + 1))
                        if hf or not isinstance(f, int) or f:
                            if isinstance(f, int) and f == 0:
                                act.wait_ge(s_a[m, 0], HALF)
                            else:
                                act.wait_ge(s_a[m, hf], f)
                        nc.scalar.activation(gate[:, 0:t], pg[0][:, 0:t], ACT.Silu).then_inc(s_free[0], 1)
                        split_hi(nxt, 0, jn)
                        if b is not None:
                            copy_part(b, f)
                        split_hi(nxt, 1, jn)

                    for a, e, b, _ in ada_runs(i, HALF):
                        if a == 0:
                            step(0, i, 1, b)
                            a = 1
                        with act.Fori(a, e if e < HALF else HALF - 1) as f:
                            step(f, i, f + 1, b)
                    step(HALF - 1, i + 1, 0, b)
                elif kind in ("out", "wo"):
                    def step(j, nxt, jn, b):
                        for s in range(2):
                            if nxt < len(phases):
                                split_hi(nxt, s, jn)
                            if b is not None and s == 0:
                                copy_part(b, j)
                            if next_norm(i) is not None:
                                square(next_norm(i), j * 2 + s, s, read_value(i, j))

                    for a, e, b, _ in ada_runs(i, units // 2 - 1):
                        with act.Fori(a, e) as j:
                            step(j, i, j + 1, b)
                    if next_norm(i) is None:
                        step(units // 2 - 1, i + 1, 0, None)
                    else:
                        square_part(i, 0, 0)
                        square_part(i, 0, 1)
                else:
                    for n in range(WIN_TILES):
                        s, tw = n % 2, win_tokens(l, n)
                        act.wait_ge(s_unit[s], j0 + n // 2 + 1)
                        if RG_T <= n < AQ_T:
                            nc.scalar.activation(z[:, n, 0:tw], pg[s][:, 0:tw], ACT.Silu).then_inc(s_free[s], 1)
                        else:
                            scaled = RK_T <= n < RV_T or AQ_T <= n < AK_T
                            nc.scalar.mul(z[:, n, 0:tw], pg[s][:, 0:tw], HD ** -0.5 if scaled else 1.0
                                          ).then_inc(s_free[s], 1)
                        nxt, jn = (i, n // 2 + 1) if n + 2 < WIN_TILES else (i + 1, 0)
                        split_hi(nxt, s, jn)
                    mix(i, l)
            nc.scalar.preload_act_table_set("natural_log_exp_and_others")
            for tt in range(SEQ // P):
                act.wait_ge(s_fT, tt + 1)
                b = slice(tt, tt + 1)
                link(nc.scalar.activation(junk[:, :], pfin[tt][:, :], ACT.Square, accum_out=fstat[:, b]))
                link(nc.scalar.activation(fstat[:, b], fstat[:, b], ACT.Ln, bias=eps[:, :], scale=1.0 / D))
                nc.scalar.activation(fstat[:, b], fstat[:, b], ACT.Exp, scale=-0.5).then_inc(s_fs, 1)

        @blk.vector
        def _(dve):
            chain = [0]

            def mark(ins):
                chain[0] += 1
                ins.then_inc(s_dv, 1)
                return chain[0]

            def link(ins):
                dve.wait_ge(s_dv, mark(ins))

            def split_lo(i, s, j):
                dve.wait_ge(s_whi[s], j + (pair0(i) + 1))
                nk = phases[i][5]
                nc.vector.tensor_sub(wlo[:, s, 0:nk], raw[:, s, 0:nk], whi[:, s, 0:nk].bitcast(f32)
                                     ).then_inc(s_w[s], 1)

            def clear_squares(m):
                nc.vector.memset(rstd[:, 0:norm_tokens(m)], 0.0).then_inc(s_acc, 2)

            def sum_squares(m, k, s):
                t = norm_tokens(m)
                dve.wait_ge(s_sq, k + sq_count(m, 0, 0))
                dve.wait_ge(s_acc, k + (acc_count(m, 0, 0) - 1))
                nc.vector.tensor_tensor(rstd[:, 0:t], rstd[:, 0:t], xfull[:, s, 0:t], ALU.add).then_inc(s_acc, 1)

            dve.wait_ge(s_rowsT, 1)
            nc.vector.tensor_copy(bias[:, 0:MT], pn[:, 0:MT])
            nc.vector.tensor_copy(bias[:, MT:2 * MT], pn[:, P:P + MT])
            nc.vector.tensor_copy(vecs[:, 0:68], pn[:, 2 * P:2 * P + 68]).then_inc(s_cols, 1)
            dve.wait_ge(s_cols, 1)
            nc.vector.tensor_copy(ident_r[:, :], ident)
            nc.vector.tensor_copy(window_r[:, :, :], window_sb[:, :].rearrange("p (a k) -> p a k", a=2))
            clear_squares(0)
            for tt in range(1, TOK // P, 2):
                dve.wait_ge(s_xT, tt + 1)
                nc.vector.tensor_copy(h[:, :, tt * P:(tt + 1) * P], pg[1][:, :].rearrange("p (k t) -> p k t", k=KD)
                                      ).then_inc(s_xTr[1] if tt < 4 else s_free[1], 1)
            for k in range(KD):
                sum_squares(0, k, k % 2)
            split_lo(0, 0, 0)
            split_lo(0, 1, 0)

            def copy_first(q):
                dve.wait_ge(s_ada_first, q + 1)
                nc.vector.tensor_copy(part_first[:, q * 512:(q + 1) * 512], pa[1]).then_inc(s_part0[1], 1)

            def read_first(q):
                dve.wait_ge(s_fold0, q + 1)
                for g in range(2):
                    c = slice(g * KD + 2 * q, g * KD + 2 * q + 2)
                    nc.vector.tensor_tensor(mod[:, c], pa[q % 2][:, 4 * g:4 * g + 4].rearrange("p (t v) -> p t v", v=2),
                                            bias[:, c].unsqueeze(2).broadcast_to([P, 2, 2]), ALU.add
                                            ).then_inc(s_mod, 1)
                dve.wait_ge(s_mod, 2 * q + 2)
                k = slice(2 * q, 2 * q + 2)
                nc.vector.scalar_tensor_tensor(acol[:, k], mod[:, KD + 2 * q:KD + 2 * q + 2], 1.0,
                                               vecs[:, k].unsqueeze(2).broadcast_to([P, 2, 2]),
                                               ALU.add, ALU.mult).then_inc(s_coef, 1)

            def decays():
                dve.wait_ge(s_vec, 16 * 3)
                link(nc.vector.tensor_scalar(lgt[:, 1], lg[:, :], -1.0, None, ALU.mult))
                nc.vector.tensor_tensor(lgt[:, 0], lg[:, :], lgt[:, 1], ALU.max).then_inc(s_lgd, 1)
                dve.wait_ge(s_lg, 1)
                dve.wait_ge(s_lgd, 1)
                link(nc.vector.tensor_scalar(lgt[:, 0], lgt[:, 1], 1.0, -1.0, ALU.add, ALU.add))
                link(nc.vector.tensor_scalar(nlg[:, :], lgt[:, 0], 0.0, None, ALU.is_equal))
                link(nc.vector.tensor_tensor(lgt[:, 0], lgt[:, 0], nlg[:, :], ALU.add))
                link(nc.vector.tensor_tensor(lgt[:, 2], lgt[:, 2], nlg[:, :], ALU.add))
                link(nc.vector.reciprocal(lgt[:, 0], lgt[:, 0]))
                link(nc.vector.tensor_tensor(lgt[:, 2], lgt[:, 2], lgt[:, 0], ALU.mult))
                link(nc.vector.tensor_tensor(lgt[:, 2], lgt[:, 2], lgt[:, 1], ALU.mult))
                link(nc.vector.scalar_tensor_tensor(lg[:, :], lg[:, :], 0.0, lgt[:, 2], ALU.min, ALU.subtract))
                link(nc.vector.tensor_scalar(nlg[:, :], lg[:, :], -1.0, None, ALU.mult))
                link(nc.vector.tensor_scalar(lgb[:, 0], lg[:, :], float(CTX), None, ALU.mult))
                link(nc.vector.tensor_scalar(lgb[:, 1], lg[:, :], float(SEQ), None, ALU.mult))

            def read_mod(t, i):
                dve.wait_ge(s_fold, i + ((t - ADA_FIRST) // 2 + 1))
                nc.vector.tensor_tensor(mod[:, ds(i * 2 + t, 2)], pa[1][:, 0:4].rearrange("p (t v) -> p t v", v=2),
                                        bias[:, ds(i * 2 + t, 2)].unsqueeze(2).broadcast_to([P, 2, 2]), ALU.add
                                        ).then_inc(s_mod, 1)

            def coefficients(m):
                b = m // 3 * MT + (m % 3 * 3 + 1) * KD
                dve.wait_ge(s_mod, (b + KD) // 2)
                nc.vector.scalar_tensor_tensor(acol[:, :, :], mod[:, b:b + KD], 1.0,
                                               vecs[:, m * KD:(m + 1) * KD].unsqueeze(2).broadcast_to([P, KD, 2]),
                                               ALU.add, ALU.mult).then_inc(s_coef, 1)

            def gates(m):
                b = m // 3 * MT + (m % 3 * 3 + 2) * KD
                dve.wait_ge(s_mod, (b + KD) // 2)
                link(nc.vector.tensor_scalar(gcol[:, :, :], mod[:, b:b + KD], 1.0 if m % 3 == 1 else 0.5, None,
                                             ALU.mult))

            def add_part(i, part_, s):
                m = next_norm(i)
                p0, p1 = norm_parts(m)[part_]
                n, v = KD - 2 + s, 1 if p0 >= SEQ else 0
                if part_:
                    dve.wait_ge(s_unit[s], pair0(i) + phases[i][4] // 2)
                else:
                    dve.wait_ge(s_early, 2 * (m - 1) + s + 1)
                nc.vector.scalar_tensor_tensor(h[:, n, p0:p1], pg[s][:, 512 * part_:512 * part_ + p1 - p0],
                                               gcol[:, n, v:v + 1], h[:, n, p0:p1], ALU.mult, ALU.add
                                               ).then_inc(s_free[s] if part_ else s_h0, 1)

            def sum_part(m, part_, s):
                p0, p1 = norm_parts(m)[part_]
                dve.wait_ge(s_sq, sq_count(m, part_, KD - 2 + s))
                dve.wait_ge(s_acc, acc_count(m, part_, KD - 2 + s) - 1)
                nc.vector.tensor_tensor(rstd[:, p0:p1], rstd[:, p0:p1], xfull[:, s, p0:p1], ALU.add
                                        ).then_inc(s_acc, 1)

            def norm(i, m):
                def low(part_, k):
                    p0, p1 = norm_parts(m)[part_]
                    dve.wait_ge(s_xf, xn_count(m, part_, k))
                    if vector_high(part_, k):
                        link(nc.vector.tensor_copy(xhi[:, k, p0:p1], xfull[:, k % 2, p0:p1]))
                    nc.vector.tensor_sub(xlo[:, k, p0:p1], xfull[:, k % 2, p0:p1], xhi[:, k, p0:p1].bitcast(f32)
                                         ).then_inc(s_xn, 1)

                if m:
                    add_part(i, 1, 1)
                low(0, 0)
                if m:
                    sum_part(m, 1, 1)
                low(0, 1)
                if m:
                    split_lo(i + 1, 1, 0)
                for k in range(2, KD):
                    if m == 0 and k == 3:
                        read_first(2)
                    if m == 0 and k == 4:
                        copy_first(3)
                    if m == 0 and k == 5:
                        read_first(3)
                    low(0, k)
                for k in range(KD):
                    low(1, k)
                if m == 0:
                    decays()

            def add_branch(i, s, j, n):
                dve.wait_ge(s_unit[s], j + (pair0(i) + 1))
                t = tokens(i)
                col = slice(n, n + 1) if isinstance(n, int) else ds(n, 1)
                for v, (p0, p1) in enumerate([(0, SEQ)] + ([(SEQ, TOK)] if t == TOK else [])):
                    hv = h[:, col, p0:p1].rearrange("p o t -> p (o t)")
                    last = nc.vector.scalar_tensor_tensor(hv, pg[s][:, p0:p1], gcol[:, col, v:v + 1].rearrange(
                        "p o v -> p (o v)"), hv, ALU.mult, ALU.add)
                last.then_inc(s_free[s], 1)

            def y_low(l, k, src, p0, p1, hi_count):
                dve.wait_ge(s_yhi[l], hi_count)
                nc.vector.tensor_sub(xlo[:, k, p0:p1], src, xhi[:, k, p0:p1].bitcast(f32)).then_inc(s_y[l], 1)

            def mix(i, l):
                nt = TOK // P if l < DEPTH - 1 else SEQ // P
                tq = nt * P

                def strip_slopes(hd):
                    b = l * 2 * RH + hd
                    link(nc.vector.tensor_scalar(strips[hd][:, 0:U_D], dist_sb[:, :], nlg[:, b + RH:b + RH + 1],
                                                 None, ALU.mult))

                def strip_args(hd):
                    b = l * 2 * RH + hd
                    nc.vector.scalar_tensor_tensor(strips[hd][:, 0:U_D], dist_sb[:, :], lg[:, b:b + 1],
                                                   strips[hd][:, 0:U_D], ALU.mult, ALU.min).then_inc(s_st[l], 1)

                def strip_sum(hd):
                    dve.wait_ge(s_se[l], hd + 1)
                    nc.vector.tensor_tensor(strips[hd][:, 384:512], strips[hd][:, 384:512], ident, ALU.add)
                    nc.vector.tensor_tensor(strips[hd][:, U_D:], strips[hd][:, U_D:], strip_b[:, :], ALU.add
                                            ).then_inc(s_sr[l], 1)

                for tt in range(1, nt, 2):
                    dve.wait_ge(s_f1[l], tt + 1)
                    length = SEQ if tt < SEQ // P else CTX
                    nc.vector.tensor_scalar(pq[:, tt], pa[1], float((length * HD) ** -0.5), None, ALU.mult
                                            ).then_inc(s_pq[l][1], 1)
                strip_slopes(0)
                strip_args(0)
                strip_slopes(1)
                strip_args(1)
                strip_sum(0)
                for ft in range(2):
                    y_low(l, ft, (pn, pg[0])[ft][:, 0:tq], 0, tq, ft + 1)
                    if ft == 0:
                        strip_sum(1)
                for tt in range(ret_blocks):
                    dve.wait_ge(s_vt[l], tt + 1)
                    nc.vector.tensor_copy(vret[:, tt], pa[tt % 2][:, 0:256])
                    nc.vector.tensor_copy(vatt[:, tt], pa[tt % 2][:, 256:384]).then_inc(s_v[l], 1)

                def ret_post(p, stage):
                    o = osq[:, p, 0:tq]
                    if stage == 0:
                        dve.wait_ge(s_rr[l], p + 1)
                        link(nc.vector.tensor_tensor(o, (pg[0], p67)[p][:, 0:tq], o, ALU.mult))
                    elif stage == 1:
                        link(nc.vector.scalar_tensor_tensor(o, o, vecs[:, 64 + 2 * l + p:65 + 2 * l + p],
                                                            z[:, RG_T + p, 0:tq], ALU.mult, ALU.mult))
                    elif stage == 2:
                        link(nc.vector.tensor_copy(xhi[:, 2 + p, 0:tq], o))
                    else:
                        nc.vector.tensor_sub(xlo[:, 2 + p, 0:tq], o, xhi[:, 2 + p, 0:tq].bitcast(f32)
                                             ).then_inc(s_y[l], 1)

                for hd in range(RH):
                    dve.wait_ge(s_sr[l], hd + 1)
                    for jt in range(ret_blocks):
                        r = hd * ret_blocks + jt
                        src = (pg[1], pn)[ret_turns.index(("scores", r)) % 2]
                        dve.wait_ge(s_s[l], r + 1)
                        if r >= 2:
                            dve.wait_ge(s_pv[l], r - 1)
                        if jt < SEQ // P:
                            g = strips[hd][:, 384 - jt * P:384 - jt * P + SEQ]
                        else:
                            c0 = U_D + P * (1 - (jt - 4))
                            g = strips[hd][:, c0:c0 + SEQ]
                            if tq == TOK:
                                g0 = 384 - (jt - 4) * P
                                nc.vector.tensor_tensor(sdec[:, r % 2, SEQ:TOK], src[:, SEQ:TOK],
                                                        strips[hd][:, g0:g0 + CTX], ALU.mult)
                        nc.vector.tensor_tensor(sdec[:, r % 2, 0:SEQ], src[:, 0:SEQ], g, ALU.mult
                                                ).then_inc(s_sd[l], 1)
                        if hd == 0 and jt < 4:
                            (strip_slopes, strip_args)[jt % 2](2 + jt // 2)
                        if hd == 1 and jt in (0, 4):
                            strip_sum(2 + jt // 4)
                        if RET_POST <= r < RET_POST + 4:
                            ret_post(0, r - RET_POST)
                units = att_units(l)
                for q in range(-1, len(units) + 3):
                    if q == 1:
                        for stage in range(4):
                            ret_post(1, stage)
                    pr = (q - 3) // 2 if q >= 3 and q % 2 and q < len(units) + 2 else None
                    if q + 1 < len(units):
                        n, t, s = units[q + 1]
                        hd = l * AH + t + GROUP * s
                        w = (local_keys(n)[1] + 2) * P
                        b = slice((q + 1) % 4, (q + 1) % 4 + 1)
                        dve.wait_ge(s_as[l], q + 2)
                        max_done = mark(nc.vector.reduce_max(mx[:, b], pg[(q + 1) % 2][:, TOK - w:TOK], AX.X))
                    if pr is not None:
                        dve.wait_ge(s_p[l], 2 * pr + 2)
                        p = slice(pr % 2 * 2, pr % 2 * 2 + 2)
                        nc.vector.tensor_tensor(rden[:, p], den[:, p], esink[:, p], ALU.add).then_inc(s_den[l], 1)
                    if q + 1 < len(units):
                        dve.wait_ge(s_dv, max_done)
                        nc.vector.tensor_scalar(negm[:, b], mx[:, b], sink[:, hd:hd + 1], -1.0, ALU.max, ALU.mult
                                                ).then_inc(s_nm[l], 1)
                    if pr is not None:
                        dve.wait_ge(s_den[l], pr + 1)
                        rden_done = mark(nc.vector.reciprocal(rden[:, p], rden[:, p]))
                    if 1 <= q <= len(units):
                        nb = max(local_keys(units[q - 1][0])[1], 1)
                        dve.wait_ge(s_pt[l], q)
                        if q >= 3:
                            dve.wait_ge(s_av[l], q - 2)
                        nc.vector.tensor_copy(probT[:, (q - 1) % 2, 0:nb * P], pn[:, 0:nb * P]).then_inc(s_ptl[l], 1)
                    if pr is not None:
                        dve.wait_ge(s_av[l], 2 * pr + 2)
                        dve.wait_ge(s_dv, rden_done)
                        nc.vector.tensor_tensor(otok[:, pr % 2].rearrange("p (s f) -> p s f", s=2),
                                                pa[pr % 2][:, 0:P].rearrange("p (s f) -> p s f", s=2),
                                                rden[:, p].unsqueeze(2).broadcast_to([P, 2, HD]), ALU.mult
                                                ).then_inc(s_o[l], 1)
                    if q >= 4 and q % 2 == 0:
                        out = (q - 4) // 2
                        n, t, _ = units[2 * out]
                        y_low(l, 4 + t, pa[out % 2][:, P:2 * P], n * P, (n + 1) * P, 3 + out)

            copy_first(1)
            read_first(0)
            read_first(1)
            for i, (kind, l, m, hf, units, kt) in enumerate(phases):
                t = tokens(i)
                j0 = pair0(i)
                more = i + 1 < len(phases)
                if kind in ("in", "win") and hf == 0:
                    norm(i - 1, m)
                if kind == "in":
                    def step(f, nxt, jn):
                        split_lo(nxt, 0, jn)
                        dve.wait_ge(s_unit[1], f + (j0 + 1))
                        dve.wait_ge(s_free[0], read_value(i, f))
                        col = slice(f, f + 1) if isinstance(f, int) else ds(f, 1)
                        hi = ahi[:, col, 0:t].rearrange("p o t -> p (o t)")
                        lo = alo[:, col, 0:t].rearrange("p o t -> p (o t)")
                        nc.vector.tensor_tensor(gate[:, 0:t], gate[:, 0:t], pg[1][:, 0:t], ALU.mult
                                                ).then_inc(s_free[1], 1)
                        dve.wait_ge(s_free[1], read_value(i, f))
                        nc.vector.tensor_copy(hi, gate[:, 0:t]).then_inc(s_ahi[m, hf], 1)
                        dve.wait_ge(s_ahi[m, hf], f + 1)
                        nc.vector.tensor_sub(lo, gate[:, 0:t], hi.bitcast(f32)).then_inc(s_a[m, hf], 1)
                        split_lo(nxt, 1, jn)

                    runs = ada_runs(i, HALF)
                    for a, e, b, _ in runs:
                        with dve.Fori(a, e if e < HALF else HALF - 1) as f:
                            step(f, i, f + 1)
                            if b is not None:
                                read_mod(b, f)
                    step(HALF - 1, i + 1, 0)
                    if runs[-1][2] is not None:
                        read_mod(runs[-1][2], HALF - 1)
                    if hf == 0:
                        gates(m)
                elif kind in ("out", "wo"):
                    nn = next_norm(i)
                    if nn is not None:
                        clear_squares(nn)
                    if kind == "wo":
                        gates(m)
                    for a, e, b, _ in ada_runs(i, units // 2 - 1):
                        with dve.Fori(a, e) as j:
                            for s in range(2):
                                add_branch(i, s, j, j * 2 + s)
                                split_lo(i, s, j + 1)
                                if nn is not None:
                                    sum_squares(nn, j * 2 + s, s)
                            if b is not None:
                                read_mod(b, j)
                    if nn is None:
                        for s in range(2):
                            add_branch(i, s, units // 2 - 1, units - 2 + s)
                            if more:
                                split_lo(i + 1, s, 0)
                    else:
                        coefficients(nn)
                        for s in range(2):
                            add_part(i, 0, s)
                            sum_part(nn, 0, s)
                        add_part(i, 1, 0)
                        sum_part(nn, 1, 0)
                        split_lo(i + 1, 0, 0)
                else:
                    for n in range(WIN_TILES):
                        s = n % 2
                        if n in ROPE_TILES:
                            dve.wait_ge(s_free[s], read_value(i, n // 2))
                            if n == ROPE_TILES[0]:
                                dve.wait_ge(s_rope[l], 16)
                            else:
                                dve.wait_ge(s_zr[l], ROPE_TILES.index(n))
                            zn = z[:, n, 0:SEQ]
                            link(nc.vector.stream_shuffle(swapped[:, :], zn, [(a + 16) % 32 for a in range(32)]))
                            link(nc.vector.tensor_tensor(zn, zn, rope_sb[:, 0], ALU.mult))
                            link(nc.vector.tensor_tensor(swapped[:, :], swapped[:, :], rope_sb[:, 1], ALU.mult))
                            nc.vector.tensor_tensor(zn, zn, swapped[:, :], ALU.add).then_inc(s_zr[l], 1)
                        nxt, jn = (i, n // 2 + 1) if n + 2 < WIN_TILES else (i + 1, 0)
                        split_lo(nxt, s, jn)
                    mix(i, l)
            dve.wait_ge(s_wf, 16)
            for tt in range(SEQ // P):
                dve.wait_ge(s_fs, tt + 1)
                if tt >= 2:
                    dve.wait_ge(s_out[tt % 2], 16)
                nc.vector.scalar_tensor_tensor(osb[:, tt % 2], pfin[tt][:, :], fstat[:, tt:tt + 1],
                                               wfin[:, :], ALU.mult, ALU.mult).then_inc(s_fo, 1)


INPUTS = ['x', 'c', 'ctx', 'c_ctx', 'norm_w', 'w_ada', 'b_ada', 'ffn_w_in', 'ffn_w_out', 'w_in', 'w_o',
          'ret_decay', 'ret_gn_w', 'attn_sink', 'final_norm_w']


def kernel(**inputs):
    import concourse.bacc as bacc
    from concourse.bass_utils import run_bass_kernel_spmd

    nc = bacc.Bacc("TRN2", target_bir_lowering=False, num_devices=1)
    arrays, args = {}, []
    tables = constants()
    for name in INPUTS + list(tables):
        a = np.ascontiguousarray(inputs[name] if name in inputs else tables[name])
        arrays[f"in_{name}"] = a
        args.append(nc.dram_tensor(f"in_{name}", a.shape, mybir.dt.from_np(a.dtype), kind="ExternalInput").ap())
    shape = (1, SEQ, D)
    args.append(nc.dram_tensor("out_h", shape, mybir.dt.float32, kind="ExternalOutput").ap())
    transformer(nc, *args)
    return run_bass_kernel_spmd(nc, [arrays], core_ids=[0]).results[0]["out_h"]
```
